# Optimizing a Trainium2 kernel written in Bass

```python
import jax, jax.numpy as jnp
from jax import lax
import numpy as np

D_MODEL = 1024
BATCH = 1
SEQ = 1024
DEPTH = 1

CTX_LEN = 256
GRID_W = 64
D_MIX = D_MODEL
HEAD_DIM = 64
D_ATTN = D_MIX // 2
N_Q_HEADS = D_ATTN // HEAD_DIM
N_KV_HEADS = 2
Q_PER_KV = N_Q_HEADS // N_KV_HEADS
D_KV = N_KV_HEADS * HEAD_DIM
D_LRU = D_MIX - D_ATTN
LRU_BLOCKS = 8
LRU_BLOCK = D_LRU // LRU_BLOCKS
CONV_W = 4
CONV_PAD_LEFT = 2
RG_C = 8.0
ROPE_THETA = 10000.0
ROPE_FREQS = HEAD_DIM // 4
Q_BLOCK = 128
D_IN = D_ATTN + 2 * D_KV + 2 * D_LRU
PEER_HEADS = 8
PEER_NKEYS = 128
PEER_N = PEER_NKEYS * PEER_NKEYS
PEER_DKEY = 256
PEER_TOPK = 16
PEER_CHUNK = 128
N_MOD = 6
EPS = 1e-6

kernel_name = "hybrid_rglru_gqa_peer_prefix_dit"

def rmsnorm(x, g):
    x32 = x.astype(jnp.float32)
    y = x32 * lax.rsqrt(jnp.mean(x32 * x32, axis=-1, keepdims=True) + EPS)
    return (y * g.astype(jnp.float32)).astype(x.dtype)

def modulate(h, shift, scale):
    return h * (1.0 + scale) + shift

def split_heads(t, n):
    return t.reshape(t.shape[:-1] + (n, HEAD_DIM))

def group_q(q):
    return q.reshape(q.shape[:2] + (N_KV_HEADS, Q_PER_KV, HEAD_DIM))

def axial_rope(x, row, col):
    inv = ROPE_THETA ** (-jnp.arange(ROPE_FREQS, dtype=jnp.float32) / ROPE_FREQS)
    ang = jnp.stack([row.astype(jnp.float32)[:, None] * inv,
                     col.astype(jnp.float32)[:, None] * inv], axis=1)
    cos = jnp.cos(ang)[None, :, None].astype(x.dtype)
    sin = jnp.sin(ang)[None, :, None].astype(x.dtype)
    xp = x.reshape(x.shape[:-1] + (2, 2, ROPE_FREQS))
    x1, x2 = xp[..., 0, :], xp[..., 1, :]
    out = jnp.stack([x1 * cos - x2 * sin, x1 * sin + x2 * cos], axis=-2)
    return out.reshape(x.shape)

def attend(q, k, v):
    s = jnp.einsum('bqkgd,bskd->bkgqs', q, k).astype(jnp.float32) * (HEAD_DIM ** -0.5)
    p = jax.nn.softmax(s, axis=-1).astype(v.dtype)
    return jnp.einsum('bkgqs,bskd->bqkgd', p, v)

def latent_attention(q, k_all, v_all):
    B, T = q.shape[:2]
    nb = T // Q_BLOCK
    qb = jnp.moveaxis(q.reshape(B, nb, Q_BLOCK, N_KV_HEADS, Q_PER_KV, HEAD_DIM), 1, 0)
    ob = lax.map(lambda qq: attend(qq, k_all, v_all), qb)
    return jnp.moveaxis(ob, 0, 1).reshape(B, T, D_ATTN)

def dwconv(x, w, b):
    T = x.shape[1]
    xp = jnp.pad(x, ((0, 0), (CONV_PAD_LEFT, CONV_W - 1 - CONV_PAD_LEFT), (0, 0)))
    return sum(xp[:, j:j + T] * w[j] for j in range(CONV_W)) + b

def rglru_coeffs(x, wa, ba, wi, bi, lam):
    xb = x.reshape(x.shape[:2] + (LRU_BLOCKS, LRU_BLOCK))
    r = jax.nn.sigmoid(jnp.einsum('btni,nij->btnj', xb, wa).reshape(x.shape) + ba)
    i = jax.nn.sigmoid(jnp.einsum('btni,nij->btnj', xb, wi).reshape(x.shape) + bi)
    log_a = -RG_C * r.astype(jnp.float32) * jax.nn.softplus(-lam.astype(jnp.float32))
    a = jnp.exp(log_a)
    b = jnp.sqrt(jnp.maximum(-jnp.expm1(2.0 * log_a), 0.0)) * (i * x).astype(jnp.float32)
    return a, b

def linear_scan(a, b, reverse):
    def combine(l, r):
        return l[0] * r[0], r[0] * l[1] + r[1]
    return lax.associative_scan(combine, (a, b), axis=1, reverse=reverse)[1]

def rglru_bidir(xc, xl, wa, ba, wi, bi, lam):
    yc, yl = 0.0, 0.0
    for d, reverse in ((0, False), (1, True)):
        ac, bc = rglru_coeffs(xc, wa[d], ba[d], wi[d], bi[d], lam[d])
        hc = linear_scan(ac, bc, reverse)
        h0 = hc[:, 0] if reverse else hc[:, -1]
        al, bl = rglru_coeffs(xl, wa[d], ba[d], wi[d], bi[d], lam[d])
        edge = -1 if reverse else 0
        bl = bl.at[:, edge].add(al[:, edge] * h0)
        hl = linear_scan(al, bl, reverse)
        yc = yc + hc
        yl = yl + hl
    return yc.astype(xc.dtype), yl.astype(xl.dtype)

def peer(h, wq, subkeys, u, v):
    shp = h.shape
    chunks = h.reshape(-1, PEER_CHUNK, D_MODEL)

    def one(xc):
        q = (xc @ wq).reshape(PEER_CHUNK, PEER_HEADS, 2, PEER_DKEY // 2)
        s = jnp.einsum('nhpd,hpkd->nhpk', q, subkeys).astype(jnp.float32)
        s1, i1 = lax.top_k(s[:, :, 0], PEER_TOPK)
        s2, i2 = lax.top_k(s[:, :, 1], PEER_TOPK)
        cand_s = (s1[..., :, None] + s2[..., None, :]).reshape(PEER_CHUNK, PEER_HEADS, PEER_TOPK * PEER_TOPK)
        cand_i = (i1[..., :, None] * PEER_NKEYS + i2[..., None, :]).reshape(PEER_CHUNK, PEER_HEADS, PEER_TOPK * PEER_TOPK)
        top_s, pos = lax.top_k(cand_s, PEER_TOPK)
        idx = jnp.take_along_axis(cand_i, pos, axis=-1)
        g = jax.nn.softmax(top_s, axis=-1).astype(xc.dtype)
        act = jax.nn.gelu(jnp.einsum('nhkd,nd->nhk', u[idx], xc))
        return jnp.einsum('nhk,nhkd->nd', g * act, v[idx])

    return lax.map(one, chunks).reshape(shp)

def setup_inputs(seed: int = 0) -> dict:
    key = jax.random.key(seed)
    ks = jax.random.split(key, 26)
    f32 = jnp.float32

    def nrm(k, shape, scale):
        return jax.random.normal(k, shape, f32) * scale

    def gain(k, n):
        return 1.0 + 0.02 * jax.random.normal(k, (DEPTH, n), f32)

    a0 = jax.random.uniform(ks[25], (DEPTH, 2, D_LRU), f32, 0.9, 0.999)
    rg_lambda = jnp.log(a0) - jnp.log1p(-a0)
    return {
        "x": nrm(ks[0], (BATCH, SEQ, D_MODEL), 1.0),
        "c": nrm(ks[1], (BATCH, D_MODEL), 1.0),
        "ctx": nrm(ks[2], (BATCH, CTX_LEN, D_MODEL), 1.0),
        "c_ctx": nrm(ks[3], (D_MODEL,), 1.0),
        "w_mod": nrm(ks[4], (DEPTH, D_MODEL, N_MOD * D_MODEL), 0.5 * D_MODEL ** -0.5),
        "b_mod": nrm(ks[5], (DEPTH, N_MOD * D_MODEL), 0.01),
        "g_pre_mix": gain(ks[6], D_MODEL),
        "g_post_mix": gain(ks[7], D_MODEL),
        "g_pre_ffn": gain(ks[8], D_MODEL),
        "g_post_ffn": gain(ks[9], D_MODEL),
        "w_in": nrm(ks[10], (DEPTH, D_MODEL, D_IN), D_MODEL ** -0.5),
        "q_norm_g": gain(ks[11], HEAD_DIM),
        "k_norm_g": gain(ks[12], HEAD_DIM),
        "conv_w": nrm(ks[13], (DEPTH, CONV_W, D_LRU), CONV_W ** -0.5),
        "conv_b": nrm(ks[14], (DEPTH, D_LRU), 0.01),
        "rg_wa": nrm(ks[15], (DEPTH, 2, LRU_BLOCKS, LRU_BLOCK, LRU_BLOCK), LRU_BLOCK ** -0.5),
        "rg_ba": nrm(ks[16], (DEPTH, 2, D_LRU), 0.01),
        "rg_wi": nrm(ks[17], (DEPTH, 2, LRU_BLOCKS, LRU_BLOCK, LRU_BLOCK), LRU_BLOCK ** -0.5),
        "rg_bi": nrm(ks[18], (DEPTH, 2, D_LRU), 0.01),
        "rg_lambda": rg_lambda,
        "w_out": nrm(ks[19], (DEPTH, D_MIX, D_MODEL), D_MIX ** -0.5),
        "peer_wq": nrm(ks[20], (DEPTH, D_MODEL, PEER_HEADS * PEER_DKEY), D_MODEL ** -0.5),
        "peer_subkeys": nrm(ks[21], (DEPTH, PEER_HEADS, 2, PEER_NKEYS, PEER_DKEY // 2), (PEER_DKEY // 2) ** -0.5),
        "peer_u": nrm(ks[22], (DEPTH, PEER_N, D_MODEL), D_MODEL ** -0.5),
        "peer_v": nrm(ks[23], (DEPTH, PEER_N, D_MODEL), D_MODEL ** -0.5),
    }

def reference(x, c, ctx, c_ctx, w_mod, b_mod, g_pre_mix, g_post_mix, g_pre_ffn, g_post_ffn,
              w_in, q_norm_g, k_norm_g, conv_w, conv_b, rg_wa, rg_ba, rg_wi, rg_bi, rg_lambda,
              w_out, peer_wq, peer_subkeys, peer_u, peer_v):
    B, T, _ = x.shape
    C = ctx.shape[1]
    ROWS = T // GRID_W
    row = jnp.repeat(jnp.arange(ROWS, dtype=jnp.int32), GRID_W)
    col = jnp.tile(jnp.arange(GRID_W, dtype=jnp.int32), ROWS)
    silu_c = jax.nn.silu(c)
    silu_cc = jax.nn.silu(c_ctx)
    cuts = [D_ATTN, D_ATTN + D_KV, D_ATTN + 2 * D_KV, D_ATTN + 2 * D_KV + D_LRU]

    for l in range(DEPTH):
        last = l == DEPTH - 1
        mod_x = (silu_c @ w_mod[l] + b_mod[l]).reshape(B, N_MOD, 1, D_MODEL)
        mod_c = (silu_cc @ w_mod[l] + b_mod[l]).reshape(N_MOD, 1, D_MODEL)
        sh1, sc1, g1, sh2, sc2, g2 = (mod_x[:, i] for i in range(N_MOD))
        csh1, csc1, cg1, csh2, csc2, cg2 = (mod_c[i] for i in range(N_MOD))

        px = modulate(rmsnorm(x, g_pre_mix[l]), sh1, sc1) @ w_in[l]
        pc = modulate(rmsnorm(ctx, g_pre_mix[l]), csh1, csc1) @ w_in[l]
        qx, kx, vx, lx, zx = jnp.split(px, cuts, axis=-1)
        qc, kc, vc, lc, zc = jnp.split(pc, cuts, axis=-1)

        qx = axial_rope(rmsnorm(split_heads(qx, N_Q_HEADS), q_norm_g[l]), row, col)
        kx = axial_rope(rmsnorm(split_heads(kx, N_KV_HEADS), k_norm_g[l]), row, col)
        kc = rmsnorm(split_heads(kc, N_KV_HEADS), k_norm_g[l])
        vc = split_heads(vc, N_KV_HEADS)
        k_all = jnp.concatenate([kc, kx], axis=1)
        v_all = jnp.concatenate([vc, split_heads(vx, N_KV_HEADS)], axis=1)
        attn_x = latent_attention(group_q(qx), k_all, v_all)

        yc, yl = rglru_bidir(dwconv(lc, conv_w[l], conv_b[l]), dwconv(lx, conv_w[l], conv_b[l]),
                             rg_wa[l], rg_ba[l], rg_wi[l], rg_bi[l], rg_lambda[l])
        lru_x = yl * jax.nn.gelu(zx)

        mix_x = jnp.concatenate([attn_x, lru_x], axis=-1) @ w_out[l]
        x_mid = x + g1 * rmsnorm(mix_x, g_post_mix[l])

        if not last:
            qc = rmsnorm(split_heads(qc, N_Q_HEADS), q_norm_g[l])
            attn_c = attend(group_q(qc), kc, vc).reshape(B, C, D_ATTN)
            lru_c = yc * jax.nn.gelu(zc)
            mix_c = jnp.concatenate([attn_c, lru_c], axis=-1) @ w_out[l]
            ctx = ctx + cg1 * rmsnorm(mix_c, g_post_mix[l])
            hc2 = modulate(rmsnorm(ctx, g_pre_ffn[l]), csh2, csc2)
            ctx = ctx + cg2 * rmsnorm(peer(hc2, peer_wq[l], peer_subkeys[l], peer_u[l], peer_v[l]), g_post_ffn[l])

        hx2 = modulate(rmsnorm(x_mid, g_pre_ffn[l]), sh2, sc2)
        ffn_x = peer(hx2, peer_wq[l], peer_subkeys[l], peer_u[l], peer_v[l])
        x = x_mid + g2 * rmsnorm(ffn_x, g_post_ffn[l])

    return x


_drawn_inputs = setup_inputs


def setup_inputs(seed=0):
    import zlib

    import numpy as np

    out = dict(_drawn_inputs(seed))
    spreads = {}
    factors = {'g_post_ffn': 8.0, 'q_norm_g': 8.0, 'k_norm_g': 8.0, 'rg_ba': 8.0, 'rg_bi': 6.926}
    for name, (base, spread) in spreads.items():
        noise = np.random.default_rng([zlib.crc32(name.encode()), seed]).standard_normal(out[name].shape)
        drawn = base * np.exp(spread * noise) if base else spread * noise
        out[name] = __import__('jax').numpy.asarray(drawn.astype(out[name].dtype))
    for name, factor in factors.items():
        out[name] = (out[name] * factor).astype(out[name].dtype)
    return out
```

```python
from contextlib import ExitStack

import numpy as np

import concourse.bass as bass
from concourse import mybir

ALU = mybir.AluOpType
ACT = mybir.ActivationFunctionType
AX = mybir.AxisListType.X
F32 = mybir.dt.float32
U32 = mybir.dt.uint32

P = 128
D = 1024
KT = D // P
SEQ, CTX = 1024, 256
GRID_W = 64
NX, NC_ = SEQ // P, CTX // P
NTOK = NX + NC_
HD = 64
NQ, NKV = 8, 2
D_ATTN = NQ * HD
D_KV = NKV * HD
D_LRU = 512
LF = D_LRU // P
D_IN = D_ATTN + 2 * D_KV + 2 * D_LRU
QKV = D_ATTN + 2 * D_KV
CONV_W, PADL = 4, 2
GAP = 3
XLW = PADL + CTX + GAP + SEQ + 1
LW = CTX + GAP + SEQ
RG_C = 8.0
KEYS = CTX + SEQ
PH, NK, DK = 8, 128, 128
TOPK = 16
SLOTS = PH * TOPK
RING = 8
DIAGS = 4
EPS = 1e-6
NEG = -3.0e38
GELU_C, GELU_K = 0.044715, 0.7978845608028654
ATT_T = 3 * NQ
STAGES = 9
SLICE = 14
PAIR_STEPS = 31
CHUNK_STEPS = 196


class Chain:

    def __init__(self, eng, sem):
        self.eng, self.sem, self.base, self.k = eng, sem, 0, 0

    def step(self, ins):
        self.k += 1
        return ins.then_inc(self.sem, 1)

    def sync(self):
        self.eng.wait_ge(self.sem, self.base + self.k)

    def link(self, ins):
        self.step(ins)
        self.sync()

    def link_alone(self, ins, passed):
        self.link(ins)
        self.eng.sem_inc(passed, 1)

    def enter(self, i, per):
        self.start = self.base + self.k
        self.per = per
        self.base, self.k = self.start + i * per, 0

    def leave(self, count):
        assert self.k == self.per, (self.k, self.per)
        self.base, self.k = self.start + count * self.per, 0


def layer(nc, t):
    with ExitStack() as ctx:
        def sb(name, shape, dt=F32):
            return ctx.enter_context(nc.sbuf_tensor(name, shape, dt))

        def sem(name):
            return ctx.enter_context(nc.semaphore(name))

        ident = sb("ident", [P, P])
        wbig = sb("wbig", [P, KT * 2048])
        w_in = wbig[:, 0:KT * D_IN].rearrange("p (t n) -> p t n", t=KT)
        wq = wbig[:, :].rearrange("p (t n) -> p t n", t=KT)
        skT = sb("skT", [P, 2 * PH, NK])
        kT = sb("kT", [P, NKV, KEYS])
        v = sb("v", [P, NTOK, D_KV])
        rows = sb("rows", [P, 4, D])
        G1, A2, B2, G2 = (rows[:, i, :] for i in range(4))
        modc = sb("modc", [P, 4, KT])
        gcol = sb("gcol", [P, KT])
        iota16 = sb("iota16", [P, TOPK])
        small = sb("small", [P, 64])
        convw = sb("convw", [P, LF, CONV_W])
        convb = sb("convb", [P, LF])
        lrub = sb("lrub", [P, 2, 2, LF])
        lam = sb("lam", [P, 2, LF])
        lt = sb("lt", [P, 5, 2 * LF])
        lruk = sb("lruk", [P, 2 * LF])
        ARENA = 25680
        arena = sb("arena", [P, ARENA])

        at = [0]

        def view(n, *dims):
            assert at[0] + n <= ARENA, at[0] + n
            a = arena[:, at[0]:at[0] + n]
            at[0] += n
            
            if dims:
                names = "abcd"[:len(dims)]
                a = a.rearrange("p (%s) -> p %s" % (" ".join(names), " ".join(names)),
                                **dict(zip(names, dims)))
            return a

        wm = view(2 * 4096, 2, KT, 512)
        bmod = view(6 * D)
        rowm = view(2 * D)
        silb = view(KT * P, KT, P)
        ccol = view(2 * KT, 2, KT)
        csil = view(2 * KT, 2, KT)
        sil2 = view(2 * KT, KT, 2)
        ones = view(P)
        at[0] = 0
        XL = view(LF * XLW, LF, XLW)
        Z = view(LF * SEQ, LF, SEQ)
        lru_at = at[0]
        xp = view(2 * D, 2, D)
        hT = view(KT * 2 * P, KT, 2 * P)
        cosr = view(NTOK * HD, NTOK, HD)
        sinr = view(NTOK * HD, NTOK, HD)
        tabs = view(4 * NTOK * HD, 4, NTOK, HD)
        gq = view(2 * HD, 2, HD)
        qk = view(640)
        rot = view(768)
        swp = view(640)
        qst = view(4 * P)
        junk = view(D)
        bd = view(16 * P, 16, P)
        at[0] = lru_at
        cu = view(LW)
        tr = view(LW)
        ti = view(LW)
        av = view(LW)
        bv = view(LW)
        hf = view(LW)
        hb = view(LW)
        assert at[0] < 21000
        at[0] = 0
        ring = view(RING * D, RING, D)
        wo = view(KT * 512, KT, 512)
        pr = view(KEYS)
        pT = view(KEYS, NTOK, P)
        qc = view(4 * P, 4, P)
        lc = view(4 * P, 4, P)
        att = view(4 * P, 4, P)
        xm_new, xm_cur, hx_new, hx_cur = (view(D) for _ in range(4))
        mix = view(D)
        hxT = view(KT * P, KT, P)
        sc = view(8 * NK, 8, NK)
        diag = view(DIAGS * P, DIAGS, P)
        ff = hxT.rearrange("p t n -> p (t n)")
        act_, gx, wt, gate, top = (view(SLOTS) for _ in range(5))
        idxf = gx
        cand = view(TOPK * TOPK)
        cnd2 = view(TOPK * TOPK)
        tk = cnd2[:, 0:NK]
        tv = view(2 * TOPK, 2, TOPK)
        pabu = cand[:, 0:P].bitcast(U32).rearrange("p (a h k) -> p a h k", a=2, h=4)
        selv = cand[:, P:2 * P].rearrange("p (a h k) -> p a h k", a=2, h=4)
        q_tok = pr[:, 0:D]
        q_T = pT[:, 0:8, :]
        oneh = mix.rearrange("p (h k a) -> p h k a", h=4, k=TOPK)
        ixu = sb("ixu", [P, PH, 2, TOPK], U32)
        posu = sb("posu", [P, PH, TOPK], U32)
        idx_new = sb("idx_new", [P, SLOTS], U32)
        idx_u = sb("idx_u", [P, SLOTS], U32)
        idx_v = sb("idx_v", [P, SLOTS], U32)

        psum = ctx.enter_context(nc.psum_tensor("psum", [P, 8 * 512], F32))

        def bank(b, n=1):
            return psum[:, 512 * b:512 * (b + n)]

        q_scr = nc.dram_tensor("q_scr", (NX, P, 4 * P), F32, kind="Internal").ap()
        l_scr = nc.dram_tensor("l_scr", (LF, P, SEQ), F32, kind="Internal").ap()

        S = {n: sem(n) for n in (
            "consts_made", "vec_chain", "act_chain", "pool_chain",
            "c_loaded", "bmod_loaded", "gains_loaded", "wm_loaded0", "wm_loaded1", "wm_used", "sub_loaded",
            "silu_ready", "tanh_c", "mod_mm", "mod_out", "modT_ready", "modc_ready", 
            "w_in_loaded", "x_loaded", "x_sq", "x_var", "x_sd", "xn_ready", "xT_ready", "hT_vec", "hT_act",
            "qkv_ready", "lru_ready", "z_ready", "lz_out", "qk_sq", "qk_var", "qk_sd", "qkv_read", "rot_ready", "qkT_ready",
            "q_staged", "q_free", "q_opened", "ff_free", "sc_used", "k_staged", "q_stored", "tab_loaded", "lruw_loaded", "bd_zeroed", "bd_loaded",
            "conv_done", "gates_ready", "gates_out", "lru_a", "lru_m", "lru_s", "lru_used", "lru_out", "lru_stored",
            "z_tanh", "z_in", "lam_abs", "lam_exp", "lruk_ready",
            "wq_loaded", "wo_loaded", "q_loaded", "l_loaded", "xc_loaded",
            "scores_ready", "negmax_ready", "probs_ready", "probs_normed", "pt_ready", "pt_even", "pt_odd",
            "pv_ready", "att_ready", "out_half", "mix_sq", "mix_var", "mix_sd", "xm_ready", "xm_sq",
            "xm_var", "xm_sd", "hx_ready", "hxT_ready", "hxT_even", "hxT_odd", "q_ready", "q_out",
            "qT_ready", "qT_even", "qT_odd", "s_ready", "s_even", "s_odd", "gate_in", "gate_exp", "top_passed", "idx_ready",
            "xm_moved", "idx_taken", "u_opened", "v_opened", "u_used", "v_used", "gelu_in", "gelu_tanh", "w_ready", "diag_ready",
            "ffn_ready", "ffn_sq", "ffn_var", "ffn_sd", "ffn_read", "out_ready", "out_stored")}
        got = [sem(f"got{r}") for r in range(RING)]

        block = ctx.enter_context(nc.Block())

        @block.sync
        def _(sp):
            for i, name in enumerate(("c", "c_ctx")):
                sp.dma_start(ccol[:, i, :], t[name].rearrange("(p t) -> p t", p=P)).then_inc(S["c_loaded"], 16)
            sp.dma_start(bmod[0:1, :], t["b_mod"]).then_inc(S["bmod_loaded"], 16)
            wmv = t["w_mod"].rearrange("(p t) n -> p t n", p=P)

            def mod_block(n):
                if n >= 2:
                    sp.wait_ge(S["wm_used"], n - 1)
                sp.dma_start(wm[:, n % 2, :, :], wmv[:, :, 512 * n:512 * n + 512])\
                    .then_inc(S["wm_loaded%d" % (n % 2)], 16)

            mod_block(0)
            mod_block(1)
            sp.dma_start(skT[:], t["subkeys"]).then_inc(S["sub_loaded"], 16)
            for g, name in ((G1, "g_post_mix"), (A2, "g_pre_ffn"), (G2, "g_post_ffn")):
                sp.dma_start(g, t[name].broadcast_to([P, D])).then_inc(S["gains_loaded"], 16)
            sp.dma_start(gcol[:, :], t["g_pre_mix"]).then_inc(S["gains_loaded"], 16)
            for n in range(2, 12):
                mod_block(n)
                if n == 5:
                    sp.dma_start(w_in, t["w_in"].rearrange("(t p) n -> p t n", p=P)).then_inc(S["w_in_loaded"], 16)
                    for dst, name in ((lrub, "lru_bias"), (lam, "rg_lambda"), (convw, "conv_w"), (convb, "conv_b")):
                        sp.dma_start(dst[:], t[name]).then_inc(S["lruw_loaded"], 16)
            sp.wait_ge(S["modc_ready"], 1)
            sp.wait_ge(S["wm_used"], 12)
            sp.dma_start(xp, t["xin"][0:2].rearrange("t p d -> p t d")).then_inc(S["x_loaded"], 16)
            sp.dma_start(cosr, t["cos"]).then_inc(S["tab_loaded"], 16)
            sp.dma_start(sinr, t["sin"]).then_inc(S["tab_loaded"], 16)
            sp.dma_start(gq[:, 0, :], t["q_norm_g"].broadcast_to([P, HD])).then_inc(S["tab_loaded"], 16)
            sp.dma_start(gq[:, 1, :], t["k_norm_g"].broadcast_to([P, HD])).then_inc(S["tab_loaded"], 16)
            sp.wait_ge(S["bd_zeroed"], 2)
            for d in range(2):
                for g, w in enumerate(("rg_wa", "rg_wi")):
                    for b in range(2):
                        j = (2 * d + g) * LF
                        sp.dma_start(bd[64 * b:64 * b + 64, j:j + LF, 64 * b:64 * b + 64],
                                     t[w][d, b::2].rearrange("f i j -> i f j")).then_inc(S["bd_loaded"], 16)
            with sp.Fori(1, NTOK // 2) as m:
                sp.wait_ge(S["xT_ready"], m)
                sp.dma_start(xp, t["xin"][bass.ds(m * 2, 2)].rearrange("t p d -> p t d"))\
                    .then_inc(S["x_loaded"], 16)
            sp.wait_ge(S["qkv_ready"], NTOK)
            sp.wait_ge(S["lru_ready"], LF * NTOK // 2)
            sp.wait_ge(S["z_ready"], LF * NX // 2)
            sp.dma_start(wq, t["wq"].rearrange("(t p) n -> p t n", p=P)).then_inc(S["wq_loaded"], 16)
            for f in range(LF):
                sp.wait_ge(S["lru_out"], f + 1)
                sp.dma_start(l_scr[f], hf[:, CTX + GAP:LW]).then_inc(S["lru_stored"], 16)

            wov = t["w_out"].rearrange("(t p) n -> p t n", p=P)

            def chunk_loads(n, first):
                if not first:
                    sp.wait_ge(S["scores_ready"], NQ * n)
                sp.dma_start(qc, q_scr[bass.ds(n, 1)].rearrange("o p (j c) -> (o p) j c", j=4))\
                    .then_inc(S["q_loaded"], 16)
                if not first:
                    sp.wait_ge(S["out_half"], 2 * n)
                sp.dma_start(wo, wov[:, :, 0:512]).then_inc(S["wo_loaded"], 16)
                sp.dma_start(lc, l_scr[:, :, bass.ds(n * P, P)].rearrange("f p c -> p f c"))\
                    .then_inc(S["l_loaded"], 16)
                if not first:
                    sp.wait_ge(S["xm_moved"], n)
                sp.dma_start(xm_new, t["xin"][bass.ds(n + NC_, 1)].rearrange("o p d -> (o p) d"))\
                    .then_inc(S["xc_loaded"], 16)
                sp.wait_ge(S["out_half"], 2 * n + 1)
                sp.dma_start(wo, wov[:, :, 512:D]).then_inc(S["wo_loaded"], 16)

            def store(c):
                sp.wait_ge(S["out_ready"], c + 1)
                sp.dma_start(t["out"][bass.ds(c, 1)].rearrange("o p d -> (o p) d"), ff)\
                    .then_inc(S["out_stored"], 16)
                sp.wait_ge(S["out_stored"], 16 * c + 16)
                sp.sem_inc(S["ff_free"], 1)

            sp.sem_inc(S["ff_free"], 1)
            sp.wait_ge(S["q_stored"], 16 * NX)
            sp.wait_ge(S["lru_stored"], 16 * LF)
            chunk_loads(0, True)
            with sp.Fori(1, NX) as n:
                chunk_loads(n, False)
                store(n - 1)
            store(NX - 1)
            sp.wait_ge(S["out_stored"], 16 * NX)
            sp.wait_ge(S["q_stored"], 16 * NX)
            sp.wait_ge(S["lru_stored"], 16 * LF)

        @block.gpsimd
        def _(pool):
            ch = Chain(pool, S["pool_chain"])
            ch.link(nc.gpsimd.memset(ident[:, :], 0.0))
            ch.link(nc.gpsimd.affine_select(out=ident[:, :], in_=ident[:, :], compare_op=ALU.not_equal, fill=1.0,
                                            base=0, pattern=[[-1, P]], channel_multiplier=1))
            nc.gpsimd.memset(ones, 1.0).then_inc(S["consts_made"], 1)
            nc.gpsimd.iota(iota16[:, :], pattern=[[1, TOPK]], base=0, channel_multiplier=0,
                           allow_small_or_imprecise_dtypes=True).then_inc(S["consts_made"], 1)
            pool.wait_ge(S["modc_ready"], 1)
            pool.wait_ge(S["wm_used"], 12)
            nc.gpsimd.memset(XL, 0.0).then_inc(S["bd_zeroed"], 1)
            nc.gpsimd.memset(bd, 0.0).then_inc(S["bd_zeroed"], 1)

            pool.sem_inc(S["q_free"], 1)
            with pool.Fori(0, NX) as x:
                pool.wait_ge(S["q_staged"], x + 1)
                pool.sem_inc(S["q_opened"], 1)
                pool.dma_start(q_scr[bass.ds(x, 1)].rearrange("o p n -> (o p) n"), qst)\
                    .then_inc(S["q_stored"], 16)
                pool.wait_ge(S["q_stored"], 16 * x + 16)
                pool.sem_inc(S["q_free"], 1)

            pool.sem_inc(S["v_used"], RING)
            pool.wait_ge(S["lru_stored"], 16 * LF)
            pool.wait_ge(S["q_stored"], 16 * NX)

            def gather(table, idx, j, r):
                pool.indirect_dma_start(ring[:, r, :], None, t[table],
                                        bass.IndirectOffsetOnAxis(idx[:, j:j + 1], 0)).then_inc(got[r], 16)

            with pool.Fori(0, NX) as c:
                pool.wait_ge(S["idx_ready"], c + 1)
                pool.sem_inc(S["u_opened"], 1)
                ch.enter(c, 2)
                ch.link(nc.gpsimd.tensor_copy(idx_u[:, :], idx_new[:, :]))
                pool.sem_inc(S["idx_taken"], 1)
                for j in range(SLOTS):
                    if j < RING:
                        pool.wait_ge(S["v_used"], c * SLOTS + j + 1)
                    else:
                        pool.wait_ge(S["u_used"], c * SLOTS + j - RING + 1)
                    pool.sem_inc(S["u_opened"], 1)
                    gather("u", idx_u, j, j % RING)
                pool.wait_ge(S["v_used"], c * SLOTS + RING)
                pool.sem_inc(S["v_opened"], 1)
                ch.link(nc.gpsimd.tensor_copy(idx_v[:, :], idx_u[:, :]))
                for j in range(SLOTS):
                    if j < RING:
                        pool.wait_ge(S["u_used"], c * SLOTS + SLOTS - RING + j + 1)
                    else:
                        pool.wait_ge(S["v_used"], c * SLOTS + j + 1)
                    pool.sem_inc(S["v_opened"], 1)
                    gather("v", idx_v, j, j % RING)
            ch.leave(NX)

        def wait(eng, name, val):
            if isinstance(val, int) and val <= 0:
                return
            eng.wait_ge(S[name], val)

        @block.scalar
        def _(act):
            ch = Chain(act, S["act_chain"])
            A = nc.scalar.activation
            act.wait_ge(S["c_loaded"], 32)
            A(csil, ccol, ACT.Tanh, scale=0.5).then_inc(S["tanh_c"], 1)

            def pair(m, latent, m_is_static):
                act.wait_ge(S["x_loaded"], 16 * m + 16)
                ch.link(A(junk, xp[:, 0, :], ACT.Square, accum_out=small[:, 0:1]))
                A(junk, xp[:, 1, :], ACT.Square, accum_out=small[:, 1:2]).then_inc(S["x_sq"], 1)
                act.wait_ge(S["x_var"], m + 1)
                A(small[:, 2:4], small[:, 2:4], ACT.Sqrt).then_inc(S["x_sd"], 1)
                sc_, sh_ = (0, 1) if latent else (2, 3)
                act.wait_ge(S["xT_ready"], m + 1)
                for kt in range(KT):
                    ins = A(hT[:, kt, P:2 * P], psum[:, D + kt * P:D + (kt + 1) * P], ACT.Identity,
                            scale=modc[:, sc_, kt:kt + 1], bias=modc[:, sh_, kt:kt + 1])
                ins.then_inc(S["hT_act"], 1)
                lo = 0 if latent else D_ATTN
                for tt in range(2):
                    n = 2 * m + tt
                    act.wait_ge(S["qkv_ready"], n + 1)
                    wait(act, "rot_ready", n)
                    A(swp[:, lo:640], psum[:, 2048 + lo:2048 + 640], ACT.Square).then_inc(S["qk_sq"], 1)
                    act.wait_ge(S["qk_var"], n + 1)
                    A(small[:, 16 + lo // HD:26], small[:, 16 + lo // HD:26], ACT.Sqrt).then_inc(S["qk_sd"], 1)
                    if tt == 0 or latent:
                        for f in range(LF):
                            if tt == 0:
                                act.wait_ge(S["lru_ready"], LF * m + f + 1)
                                dst = XL[:, f, bass.ds(m * 256 + (PADL + GAP), 256)] if latent \
                                    else XL[:, f, PADL:PADL + CTX]
                            else:
                                act.wait_ge(S["z_ready"], LF * m - LF + f + 1)
                                dst = Z[:, f, bass.ds(m * 256 - 256, 256)]
                            A(dst, bank(6 + f % 2)[:, 0:256], ACT.Copy).then_inc(S["lz_out"], 1)
                    if latent:
                        act.wait_ge(S["qkT_ready"], n + 1)
                        act.wait_ge(S["q_free"], n - 1)
                        A(qst, bank(4), ACT.Copy).then_inc(S["q_staged"], 1)

            act.wait_ge(S["modc_ready"], 1)
            act.wait_ge(S["wm_used"], 12)
            act.wait_ge(S["bd_zeroed"], 2)
            pair(0, False, True)
            with act.Fori(1, NTOK // 2) as m:
                ch.enter(m - 1, 1)
                pair(m, True, False)
            ch.leave(NTOK // 2 - 1)

            act.wait_ge(S["lam_abs"], 1)
            A(lt[:, 1, :], lt[:, 0, :], ACT.Exp, scale=-1.0).then_inc(S["lam_exp"], 1)
            act.wait_ge(S["lruk_ready"], 1)
            for f in range(LF):
                for d in range(2):
                    k = 2 * f + d
                    act.wait_ge(S["gates_ready"], k + 1)
                    wait(act, "lru_used", k)
                    kcol = lruk[:, LF * d + f:LF * d + f + 1]
                    A(tr, psum[:, 0:LW], ACT.Tanh, scale=0.5, bias=lrub[:, d, 0, f:f + 1]).then_inc(S["gates_out"], 1)
                    A(ti, psum[:, 1536:1536 + LW], ACT.Tanh, scale=0.5, bias=lrub[:, d, 1, f:f + 1])\
                        .then_inc(S["gates_out"], 1)
                    act.wait_ge(S["gates_out"], 2 * k + 2)
                    ch.link(A(av, tr, ACT.Exp, scale=kcol, bias=kcol))
                    A(tr, tr, ACT.Tanh, scale=kcol, bias=kcol).then_inc(S["lru_a"], 1)
                    act.wait_ge(S["lru_m"], k + 1)
                    A(bv, bv, ACT.Sqrt, scale=0.25).then_inc(S["lru_s"], 1)
                act.wait_ge(S["z_in"], f + 1)
                A(tr[:, 0:SEQ], tr[:, 0:SEQ], ACT.Tanh, scale=GELU_K).then_inc(S["z_tanh"], 1)

            def probs(n, h):
                a, b = 44 + h % 2, 46 + h % 2
                act.wait_ge(S["negmax_ready"], n * NQ + h + 1)
                wait(act, "pt_ready", n * ATT_T + 3 * h)
                A(pr, psum[:, 0:KEYS], ACT.Exp, scale=HD ** -0.5, bias=small[:, a:a + 1],
                  accum_out=small[:, b:b + 1]).then_inc(S["probs_ready"], 1)

            def att(n, h):
                for g in range(3):
                    if (3 * h + g) % 2:
                        k = 4 if g < 2 else 2
                        act.wait_ge(S["pt_ready"], n * ATT_T + 3 * h + g + 1)
                        A(pT[:, 4 * g:4 * g + k, :], bank(4)[:, 0:k * P], ACT.Copy).then_inc(S["pt_odd"], 1)
                if h + 1 < NQ:
                    probs(n, h + 1)

            def post(n, k):
                if k == 1:
                    act.wait_ge(S["out_half"], 2 * n + 2)
                    wait(act, "idx_ready", n)
                    A(mix, psum[:, 0:D], ACT.Square, accum_out=small[:, 48:49]).then_inc(S["mix_sq"], 1)
                    act.wait_ge(S["mix_var"], n + 1)
                    A(small[:, 49:50], small[:, 49:50], ACT.Sqrt).then_inc(S["mix_sd"], 1)
                    act.wait_ge(S["xm_ready"], n + 1)
                    A(mix, xm_new, ACT.Square, accum_out=small[:, 48:49]).then_inc(S["xm_sq"], 1)
                    act.wait_ge(S["xm_var"], n + 1)
                    A(small[:, 49:50], small[:, 49:50], ACT.Sqrt).then_inc(S["xm_sd"], 1)
                elif k == 2:
                    act.wait_ge(S["hxT_ready"], n + 1)
                    wait(act, "ff_free", n)
                    A(hxT[:, 4:8, :], bank(4), ACT.Copy).then_inc(S["hxT_odd"], 1)
                elif k in (3, 6):
                    act.wait_ge(S["q_ready"], 2 * n + k // 3)
                    A(q_tok, psum[:, 0:D], ACT.Copy).then_inc(S["q_out"], 1)
                elif k in (4, 7):
                    act.wait_ge(S["qT_ready"], 2 * n + k // 3)
                    A(q_T[:, 4:8, :], bank(4), ACT.Copy).then_inc(S["qT_odd"], 1)
                elif k in (5, 8):
                    act.wait_ge(S["s_ready"], 2 * n + k // 3)
                    wait(act, "sc_used", 2 * n + k // 3 - 1)
                    A(sc[:, 4:8, :], bank(5), ACT.Copy).then_inc(S["s_odd"], 1)
                    if k == 8:
                        act.wait_ge(S["gate_in"], n + 1)
                        A(gate, gate, ACT.Exp).then_inc(S["gate_exp"], 1)

            def diags(c, lo, hi):
                if lo == 0:
                    act.wait_ge(S["w_ready"], c + 1)
                for j in range(lo, min(hi, SLOTS)):
                    act.wait_ge(S["v_used"], c * SLOTS + j + 1 + RING - DIAGS)
                    A(diag[:, j % DIAGS, :], ident[:, :], ACT.Copy, scale=wt[:, j:j + 1]).then_inc(S["diag_ready"], 1)

            def finish(c):
                act.wait_ge(S["ffn_ready"], c + 1)
                act.wait_ge(S["ff_free"], c + 1)
                A(ff, bank(6, 2), ACT.Square, accum_out=small[:, 52:53]).then_inc(S["ffn_sq"], 1)
                act.wait_ge(S["ffn_var"], c + 1)
                A(small[:, 53:54], small[:, 53:54], ACT.Sqrt).then_inc(S["ffn_sd"], 1)

            def gelu(c):
                act.wait_ge(S["gelu_in"], c + 1)
                A(gx, gx, ACT.Tanh, scale=GELU_K).then_inc(S["gelu_tanh"], 1)

            probs(0, 0)
            for h in range(NQ):
                att(0, h)
            for k in range(STAGES):
                post(0, k)
            with act.Fori(0, NX - 1) as c:
                probs(c + 1, 0)
                for h in range(NQ):
                    att(c + 1, h)
                gelu(c)
                done = 0
                for k in range(STAGES):
                    diags(c, done, SLICE * (k + 1) + DIAGS)
                    done = SLICE * (k + 1) + DIAGS
                    post(c + 1, k)
                diags(c, done, SLOTS)
                finish(c)
            gelu(NX - 1)
            diags(NX - 1, 0, SLOTS)
            finish(NX - 1)

        @block.vector
        def _(dve):
            ch = Chain(dve, S["vec_chain"])
            V = nc.vector

            dve.wait_ge(S["tanh_c"], 1)
            dve.wait_ge(S["consts_made"], 2)
            ch.link(V.scalar_tensor_tensor(csil, csil, 1.0, ccol, ALU.add, ALU.mult))
            ch.link(V.tensor_scalar(csil, csil, 0.5, None, ALU.mult))
            ch.step(V.tensor_copy(sil2, csil.rearrange("p i t -> p t i")))
            ch.link(V.tensor_copy(silb, csil[:, 0, :].unsqueeze(2).broadcast_to([P, KT, P])))
            dve.sem_inc(S["silu_ready"], 1)

            def mod_row(n):
                dve.wait_ge(S["wm_used"], n + 1)
                src, at_ = bank(n % 2), slice(512 * (n % 2), 512 * (n % 2) + 512)
                if n < 4:
                    ins = V.tensor_copy(rowm[0:2, 512 * n:512 * n + 512], src[0:2, :])
                elif n < 6:
                    ins = V.tensor_tensor(G1[:, at_], src, G1[:, at_], ALU.mult)
                elif n < 8:
                    ins = V.tensor_copy(B2[:, at_], src)
                elif n < 10:
                    ins = V.scalar_tensor_tensor(A2[:, at_], src, 1.0, A2[:, at_], ALU.add, ALU.mult)
                else:
                    ins = V.tensor_tensor(G2[:, at_], src, G2[:, at_], ALU.mult)
                ins.then_inc(S["mod_out"], 1)

            for n in range(4):
                mod_row(n)
            dve.wait_ge(S["modT_ready"], 1)
            dve.wait_ge(S["gains_loaded"], 64)
            cols = bank(2)[:, 0:4 * KT].rearrange("p (j i) -> p i j", i=2)
            for i in range(2):
                ch.step(V.scalar_tensor_tensor(modc[:, 2 * i, :], cols[:, i, KT:2 * KT], 1.0, gcol[:, :],
                                               ALU.add, ALU.mult))
                ch.link(V.tensor_copy(modc[:, 2 * i + 1, :], cols[:, i, 0:KT]))
            dve.sem_inc(S["modc_ready"], 1)
            for n in range(4, 12):
                mod_row(n)

            dve.wait_ge(S["tab_loaded"], 64)
            half = "p n (x h f) -> p n x h f"
            for i in range(2):
                g = gq[:, i, :]
                ch.step(V.tensor_tensor(tabs[:, 2 * i], cosr, g.unsqueeze(1).broadcast_to([P, NTOK, HD]), ALU.mult))
                g4 = g.rearrange("p (x h f) -> p x h f", x=2, h=2)
                for hf_ in range(2):
                    for x_ in range(2):
                        o = 32 * x_ + 16 * hf_
                        ch.step(V.tensor_tensor(tabs[:, 2 * i + 1, :, o:o + 16], sinr[:, :, o:o + 16],
                                                g4[:, x_, 1 - hf_, :].unsqueeze(1).broadcast_to([P, NTOK, 16]),
                                                ALU.mult))
            ch.sync()

            def pair(m, latent):
                dve.wait_ge(S["x_sq"], m + 1)
                ch.step(V.tensor_scalar(small[:, 2:4], small[:, 0:2], 1.0 / D, EPS, ALU.mult, ALU.add))
                ch.sync()
                dve.sem_inc(S["x_var"], 1)
                dve.wait_ge(S["x_sd"], m + 1)
                ch.link(V.reciprocal(small[:, 4:6], small[:, 2:4]))
                ch.step(V.tensor_scalar(xp[:, 0, :], xp[:, 0, :], small[:, 4:5], None, ALU.mult))
                V.tensor_scalar(xp[:, 1, :], xp[:, 1, :], small[:, 5:6], None, ALU.mult)\
                    .then_inc(S["xn_ready"], 1)
                sc_, sh_ = (0, 1) if latent else (2, 3)
                dve.wait_ge(S["xT_ready"], m + 1)
                for kt in range(KT):
                    ins = V.tensor_scalar(hT[:, kt, 0:P], psum[:, kt * P:(kt + 1) * P],
                                          modc[:, sc_, kt:kt + 1], modc[:, sh_, kt:kt + 1], ALU.mult, ALU.add)
                ins.then_inc(S["hT_vec"], 1)
                h0 = 0 if latent else NQ
                lo = h0 * HD
                for tt in range(2):
                    n = 2 * m + tt
                    dve.wait_ge(S["qk_sq"], n + 1)
                    ch.step(V.tensor_copy(v[:, bass.ds(n, 1), :].rearrange("p o d -> p (o d)"),
                                          psum[:, 2048 + 640:2048 + 768]))
                    ch.link(V.tensor_reduce(small[:, 16 + h0:26],
                                            swp[:, lo:640].rearrange("p (h d) -> p h d", d=HD), AX, ALU.add))
                    ch.link(V.tensor_scalar(small[:, 16 + h0:26], small[:, 16 + h0:26], 1.0 / HD, EPS,
                                            ALU.mult, ALU.add))
                    dve.sem_inc(S["qk_var"], 1)
                    dve.wait_ge(S["qk_sd"], n + 1)
                    ch.link(V.reciprocal(small[:, 32 + h0:42], small[:, 16 + h0:26]))
                    nh = 10 - h0
                    ch.link(V.tensor_tensor(
                        qk[:, lo:640].rearrange("p (h d) -> p h d", d=HD),
                        psum[:, 2048 + lo:2048 + 640].rearrange("p (h d) -> p h d", d=HD),
                        small[:, 32 + h0:42].unsqueeze(2).broadcast_to([P, nh, HD]), ALU.mult))
                    wait(dve, "qkT_ready", n)
                    parts = [(1, NQ, 10)] + ([(0, 0, NQ)] if latent else [])
                    for i, a, b in parts:
                        k_ = b - a
                        tab = tabs[:, 2 * i + 1, bass.ds(n, 1), :].rearrange("p o d -> p (o d)")
                        for hf_ in range(2):
                            def half_of(ap, which, heads=k_):
                                ap = ap.rearrange("p (h x s f) -> p h x s f", x=2, s=2, f=16)
                                return ap[:, :, :, which, :]
                            tb = tab.rearrange("p (x s f) -> p x s f", x=2, s=2)[:, :, hf_, :]
                            ch.step(V.tensor_tensor(half_of(swp[:, a * HD:b * HD], hf_),
                                                    half_of(qk[:, a * HD:b * HD], 1 - hf_),
                                                    tb.unsqueeze(1).broadcast_to([P, k_, 2, 16]), ALU.mult))
                    ch.sync()
                    for i, a, b in parts:
                        k_ = b - a
                        q3 = qk[:, a * HD:b * HD].rearrange("p (h d) -> p h d", d=HD)
                        cs = tabs[:, 2 * i, bass.ds(n, 1), :].rearrange("p o d -> p (o d)")
                        ch.step(V.tensor_tensor(q3, q3, cs.unsqueeze(1).broadcast_to([P, k_, HD]), ALU.mult))
                    ch.sync()
                    if latent:
                        ch.step(V.tensor_tensor(rot[:, 0:D_ATTN], qk[:, 0:D_ATTN], swp[:, 0:D_ATTN], ALU.add))
                    for dup in range(2):
                        ch.step(V.tensor_tensor(
                            rot[:, 512:768].rearrange("p (k u d) -> p k u d", k=2, u=2)[:, :, dup, :],
                            qk[:, 512:640].rearrange("p (k d) -> p k d", k=2),
                            swp[:, 512:640].rearrange("p (k d) -> p k d", k=2), ALU.add))
                    ch.sync()
                    dve.sem_inc(S["rot_ready"], 1)
                    dve.wait_ge(S["qkT_ready"], n + 1)
                    V.tensor_copy(kT[:, :, bass.ds(n * P, P)],
                                  bank(5)[:, 0:2 * P].rearrange("p (k n) -> p k n", k=2)).then_inc(S["k_staged"], 1)

            pair(0, False)
            with dve.Fori(1, NTOK // 2) as m:
                ch.enter(m - 1, PAIR_STEPS)
                pair(m, True)
            ch.leave(NTOK // 2 - 1)

            dve.wait_ge(S["lruw_loaded"], 16 * 4)
            lamf = lam[:, :, :].rearrange("p d f -> p (d f)")
            V.scalar_tensor_tensor(lt[:, 0, :], lamf, -1.0, lamf, ALU.mult, ALU.max).then_inc(S["lam_abs"], 1)
            lb = lrub[:, :, :, :].rearrange("p d g f -> p (d g f)")
            ch.step(V.tensor_scalar(lb, lb, 0.5, None, ALU.mult))
            dve.wait_ge(S["lam_exp"], 1)
            ch.link(V.tensor_scalar(lt[:, 2, :], lt[:, 1, :], 2.0, None, ALU.add))
            ch.link(V.reciprocal(lt[:, 2, :], lt[:, 2, :]))
            ch.link(V.tensor_tensor(lt[:, 1, :], lt[:, 1, :], lt[:, 2, :], ALU.mult))
            ch.link(V.tensor_tensor(lt[:, 2, :], lt[:, 1, :], lt[:, 1, :], ALU.mult))
            ch.link(V.tensor_scalar(lt[:, 3, :], lt[:, 2, :], 1.0 / 17, None, ALU.mult))
            for k in range(15, 1, -2):
                ch.link(V.scalar_tensor_tensor(lt[:, 3, :], lt[:, 3, :], 1.0 / k, lt[:, 2, :], ALU.add, ALU.mult))
            ch.link(V.scalar_tensor_tensor(lt[:, 3, :], lt[:, 3, :], 1.0, lt[:, 1, :], ALU.add, ALU.mult))
            ch.link(V.tensor_scalar(lt[:, 4, :], lamf, -1.0, 0.0, ALU.mult, ALU.max))
            ch.link(V.scalar_tensor_tensor(lt[:, 4, :], lt[:, 3, :], 2.0, lt[:, 4, :], ALU.mult, ALU.add))
            ch.link(V.tensor_scalar(lruk[:, :], lt[:, 4, :], -RG_C / 2, None, ALU.mult))
            dve.sem_inc(S["lruk_ready"], 1)

            lx = slice(CTX + GAP, LW)
            dve.wait_ge(S["lz_out"], LF + 2 * LF * (NTOK // 2 - 1))
            for f in range(LF):
                wait(dve, "gates_ready", 2 * f)
                ch.link(V.tensor_scalar(cu, XL[:, f, 0:LW], convw[:, f, 0:1], convb[:, f:f + 1],
                                        ALU.mult, ALU.add))
                for j in range(1, CONV_W):
                    ins = V.scalar_tensor_tensor(cu, XL[:, f, j:j + LW], convw[:, f, j:j + 1], cu,
                                                 ALU.mult, ALU.add)
                    if j < CONV_W - 1:
                        ch.link(ins)
                ch.link(ins)
                dve.sem_inc(S["conv_done"], 1)
                for d in range(2):
                    k = 2 * f + d
                    dve.wait_ge(S["lru_a"], k + 1)
                    ch.link(V.tensor_tensor(bv, av, av, ALU.mult))
                    ch.link(V.scalar_tensor_tensor(bv, bv, 1.0, tr, ALU.add, ALU.mult))
                    V.tensor_scalar(bv, bv, -1.0, 0.0, ALU.mult, ALU.max).then_inc(S["lru_m"], 1)
                    ch.link(V.scalar_tensor_tensor(ti, ti, 1.0, cu, ALU.add, ALU.mult))
                    dve.wait_ge(S["lru_s"], k + 1)
                    ch.link(V.tensor_tensor(bv, bv, ti, ALU.mult))
                    if d == 0:
                        ch.step(V.memset(av[:, CTX:CTX + GAP], 1.0))
                        ch.link(V.memset(bv[:, CTX:CTX + GAP], 0.0))
                        wait(dve, "lru_stored", 16 * f)
                        ins = V.tensor_tensor_scan(hf, av, bv, 0.0, ALU.mult, ALU.add)
                    else:
                        ch.link(V.tensor_tensor_scan(hb[:, 0:CTX][:, ::-1], av[:, 0:CTX][:, ::-1],
                                                     bv[:, 0:CTX][:, ::-1], 0.0, ALU.mult, ALU.add))
                        ins = V.tensor_tensor_scan(hb[:, lx][:, ::-1], av[:, lx][:, ::-1], bv[:, lx][:, ::-1],
                                                   hb[:, 0:1], ALU.mult, ALU.add)
                    ch.link(ins)
                    if d == 0:
                        dve.sem_inc(S["lru_used"], 1)
                zf = Z[:, f, :]
                ch.link(V.tensor_tensor(hf[:, lx], hf[:, lx], hb[:, lx], ALU.add))
                ch.link(V.tensor_tensor(tr[:, 0:SEQ], zf, zf, ALU.mult))
                ch.link(V.tensor_scalar(tr[:, 0:SEQ], tr[:, 0:SEQ], GELU_C, 1.0, ALU.mult, ALU.add))
                V.tensor_tensor(tr[:, 0:SEQ], tr[:, 0:SEQ], zf, ALU.mult).then_inc(S["z_in"], 1)
                ch.link(V.scalar_tensor_tensor(hf[:, lx], hf[:, lx], 0.5, zf, ALU.mult, ALU.mult))
                dve.wait_ge(S["z_tanh"], f + 1)
                ch.link(V.scalar_tensor_tensor(hf[:, lx], tr[:, 0:SEQ], 1.0, hf[:, lx], ALU.add, ALU.mult))
                dve.sem_inc(S["lru_out"], 1)
                dve.sem_inc(S["lru_used"], 1)

            def negmax(n, h):
                a = 44 + h % 2
                dve.wait_ge(S["scores_ready"], n * NQ + h + 1)
                ch.link(V.tensor_reduce(small[:, a:a + 1], psum[:, 0:KEYS], AX, ALU.max))
                V.tensor_scalar(small[:, a:a + 1], small[:, a:a + 1], -HD ** -0.5, None, ALU.mult)\
                    .then_inc(S["negmax_ready"], 1)

            def att_step(n, h):
                b = 46 + h % 2
                dve.wait_ge(S["probs_ready"], n * NQ + h + 1)
                ch.link(V.reciprocal(small[:, b:b + 1], small[:, b:b + 1]))
                V.tensor_scalar(pr, pr, small[:, b:b + 1], None, ALU.mult).then_inc(S["probs_normed"], 1)
                for g in range(3):
                    if (3 * h + g) % 2 == 0:
                        k = 4 if g < 2 else 2
                        dve.wait_ge(S["pt_ready"], n * ATT_T + 3 * h + g + 1)
                        V.tensor_copy(pT[:, 4 * g:4 * g + k, :], bank(3)[:, 0:k * P]).then_inc(S["pt_even"], 1)
                if h + 1 < NQ:
                    negmax(n, h + 1)
                dve.wait_ge(S["pv_ready"], n * NQ + h + 1)
                o = 64 * (h % 2)
                V.tensor_copy(att[o:o + 64, h // 2, :], bank(5)[0:64, 128 * (h % 2):128 * (h % 2) + 128])\
                    .then_inc(S["att_ready"], 1)

            def root(count, at_, sq, var, sd):
                dve.wait_ge(S[sq], count)
                V.tensor_scalar(small[:, at_ + 1:at_ + 2], small[:, at_:at_ + 1], 1.0 / D, EPS,
                                ALU.mult, ALU.add).then_inc(S[var], 1)
                dve.wait_ge(S[sd], count)
                ch.link(V.reciprocal(small[:, at_ + 2:at_ + 3], small[:, at_ + 1:at_ + 2]))

            def top16(vals, idx, src, scratch):
                passed = S["top_passed"]
                ch.link_alone(V.max(vals[:, 0:8], src), passed)
                ch.step(V.max_index(idx[:, 0:8], vals[:, 0:8], src))
                ch.link_alone(V.match_replace(scratch, vals[:, 0:8], src, NEG), passed)
                ch.link_alone(V.max(vals[:, 8:16], scratch), passed)
                ch.link_alone(V.max_index(idx[:, 8:16], vals[:, 8:16], scratch), passed)

            def retrieve(n, u):
                for j in range(4):
                    h = 4 * u + j
                    for p_ in range(2):
                        top16(tv[:, p_, :], ixu[:, h, p_, :], sc[:, 2 * j + p_, :], tk)
                    ch.link(V.tensor_tensor(cand.rearrange("p (a b) -> p a b", a=TOPK),
                                            tv[:, 0, :].unsqueeze(2).broadcast_to([P, TOPK, TOPK]),
                                            tv[:, 1, :].unsqueeze(1).broadcast_to([P, TOPK, TOPK]), ALU.add))
                    dve.sem_inc(S["top_passed"], 1)
                    top16(top[:, TOPK * h:TOPK * h + TOPK], posu[:, h, :], cand, cnd2)
                dve.sem_inc(S["sc_used"], 1)
                hs = slice(4 * u, 4 * u + 4)
                ch.step(V.tensor_scalar(pabu[:, 0], posu[:, hs, :], 4, None, ALU.logical_shift_right))
                ch.link(V.tensor_scalar(pabu[:, 1], posu[:, hs, :], 15, None, ALU.bitwise_and))
                for p_ in range(2):
                    for j in range(4):
                        ch.step(V.tensor_tensor(oneh[:, j], pabu[:, p_, j, :].unsqueeze(2).broadcast_to([P, TOPK, TOPK]),
                                                iota16[:, :].unsqueeze(1).broadcast_to([P, TOPK, TOPK]), ALU.is_equal))
                    ch.sync()
                    ch.link(V.tensor_tensor(oneh, oneh, ixu[:, hs, p_, :].unsqueeze(2)
                                            .broadcast_to([P, 4, TOPK, TOPK]), ALU.mult))
                    ch.link(V.tensor_reduce(selv[:, p_], oneh, AX, ALU.add))
                if u == 0:
                    wait(dve, "idx_taken", n)
                ch.link(V.scalar_tensor_tensor(idxf[:, 64 * u:64 * u + 64],
                                               selv[:, 0].rearrange("p h k -> p (h k)"), float(NK),
                                               selv[:, 1].rearrange("p h k -> p (h k)"), ALU.mult, ALU.add))
                ch.link(V.tensor_copy(idx_new[:, 64 * u:64 * u + 64], idxf[:, 64 * u:64 * u + 64]))

            def post(n):
                root(n + 1, 48, "mix_sq", "mix_var", "mix_sd")
                ch.link(V.scalar_tensor_tensor(mix, psum[:, 0:D], small[:, 50:51], G1, ALU.mult, ALU.mult))
                dve.wait_ge(S["xc_loaded"], 16 * n + 16)
                ch.link(V.tensor_tensor(xm_new, xm_new, mix, ALU.add))
                dve.sem_inc(S["xm_ready"], 1)
                root(n + 1, 48, "xm_sq", "xm_var", "xm_sd")
                ch.link(V.scalar_tensor_tensor(hx_new, xm_new, small[:, 50:51], A2, ALU.mult, ALU.mult))
                ch.link(V.tensor_tensor(hx_new, hx_new, B2, ALU.add))
                dve.sem_inc(S["hx_ready"], 1)
                dve.wait_ge(S["hxT_ready"], n + 1)
                wait(dve, "ff_free", n)
                V.tensor_copy(hxT[:, 0:4, :], bank(3)).then_inc(S["hxT_even"], 1)
                for u in range(2):
                    dve.wait_ge(S["qT_ready"], 2 * n + u + 1)
                    V.tensor_copy(q_T[:, 0:4, :], bank(3)).then_inc(S["qT_even"], 1)
                    dve.wait_ge(S["s_ready"], 2 * n + u + 1)
                    ch.link(V.tensor_copy(sc[:, 0:4, :], bank(2)))
                    dve.sem_inc(S["s_even"], 1)
                    dve.wait_ge(S["s_odd"], 2 * n + u + 1)
                    dve.sem_inc(S["top_passed"], 1)
                    retrieve(n, u)
                t3 = top.rearrange("p (h k) -> p h k", k=TOPK)
                g3 = gate.rearrange("p (h k) -> p h k", k=TOPK)
                V.tensor_tensor(g3, t3, t3[:, :, 0:1].broadcast_to([P, PH, TOPK]), ALU.subtract)\
                    .then_inc(S["gate_in"], 1)
                dve.wait_ge(S["gate_exp"], n + 1)
                ch.link(V.tensor_reduce(small[:, 56:64], g3, AX, ALU.add))
                ch.link(V.reciprocal(small[:, 56:64], small[:, 56:64]))
                ch.link(V.tensor_tensor(g3, g3, small[:, 56:64].unsqueeze(2).broadcast_to([P, PH, TOPK]), ALU.mult))
                dve.sem_inc(S["idx_ready"], 1)

            def move():
                ch.step(V.tensor_copy(xm_cur, xm_new))
                ch.link(V.tensor_copy(hx_cur, hx_new))
                dve.sem_inc(S["xm_moved"], 1)

            def u_slots(c, lo, hi):
                for j in range(lo, hi):
                    r = j % RING
                    dve.wait_ge(got[r], c * (16 * 2 * SLOTS // RING) + 16 * (j // RING + 1))
                    V.tensor_tensor_reduce(ring[:, r, :], ring[:, r, :], hx_cur, 1.0, 0.0, ALU.mult, ALU.add,
                                           act_[:, j:j + 1]).then_inc(S["u_used"], 1)

            def weights(c):
                dve.wait_ge(S["u_used"], c * SLOTS + SLOTS)
                ch.link(V.tensor_tensor(gx, act_, act_, ALU.mult))
                ch.link(V.tensor_scalar(gx, gx, GELU_C, 1.0, ALU.mult, ALU.add))
                V.tensor_tensor(gx, gx, act_, ALU.mult).then_inc(S["gelu_in"], 1)
                dve.wait_ge(S["v_used"], c * SLOTS + RING)
                ch.link(V.scalar_tensor_tensor(wt, act_, 0.5, gate, ALU.mult, ALU.mult))
                dve.wait_ge(S["gelu_tanh"], c + 1)
                ch.link(V.scalar_tensor_tensor(wt, gx, 1.0, wt, ALU.add, ALU.mult))
                dve.sem_inc(S["w_ready"], 1)

            def finish(c):
                root(c + 1, 52, "ffn_sq", "ffn_var", "ffn_sd")
                ch.link(V.scalar_tensor_tensor(ff, bank(6, 2), small[:, 54:55], G2, ALU.mult, ALU.mult))
                dve.sem_inc(S["ffn_read"], 1)
                ch.link(V.tensor_tensor(ff, ff, xm_cur, ALU.add))
                dve.sem_inc(S["out_ready"], 1)

            negmax(0, 0)
            for h in range(NQ):
                att_step(0, h)
            post(0)
            move()
            with dve.Fori(0, NX - 1) as c:
                ch.enter(c, CHUNK_STEPS)
                negmax(c + 1, 0)
                for h in range(NQ):
                    u_slots(c, TOPK * h, TOPK * h + TOPK)
                    att_step(c + 1, h)
                weights(c)
                post(c + 1)
                finish(c)
                move()
            ch.leave(NX - 1)
            u_slots(NX - 1, 0, SLOTS)
            weights(NX - 1)
            finish(NX - 1)

        @block.tensor
        def _(pe):
            M = nc.tensor.matmul
            T = nc.tensor.transpose
            pe.wait_ge(S["consts_made"], 2)

            def mod_block(n):
                w = 2 if n < 4 else P
                wait(pe, "mod_out", n - 1)
                pe.wait_ge(S["wm_loaded%d" % (n % 2)], 16 * (n // 2 + 1))
                out = bank(n % 2)[0:w, :]
                M(out, lhsT=ones[0:1, 0:w], rhs=bmod[0:1, 512 * n:512 * n + 512], start=True, stop=False)
                for kt in range(KT):
                    lhs = sil2[:, kt, :] if n < 4 else silb[:, kt, :]
                    ins = M(out, lhsT=lhs, rhs=wm[:, n % 2, kt, :], start=False, stop=(kt == KT - 1))
                ins.then_inc(S["wm_used"], 1)

            pe.wait_ge(S["silu_ready"], 1)
            pe.wait_ge(S["bmod_loaded"], 16)
            for n in range(4):
                mod_block(n)
            pe.wait_ge(S["mod_out"], 4)
            for j in range(2 * KT):
                ins = T(bank(2)[:, 2 * j:2 * j + 2], rowm[0:2, j * P:(j + 1) * P], ident[0:2, 0:2])
            ins.then_inc(S["modT_ready"], 1)
            for n in range(4, 12):
                mod_block(n)
            pe.wait_ge(S["mod_out"], 12)
            pe.wait_ge(S["w_in_loaded"], 16)

            def pair(m, latent):
                pe.wait_ge(S["xn_ready"], m + 1)
                for tt in range(2):
                    for kt in range(KT):
                        ins = T(psum[:, tt * D + kt * P:tt * D + (kt + 1) * P], xp[:, tt, kt * P:(kt + 1) * P],
                                ident[:, :])
                ins.then_inc(S["xT_ready"], 1)
                pe.wait_ge(S["hT_vec"], m + 1)
                pe.wait_ge(S["hT_act"], m + 1)
                out_before = LF + 2 * LF * (m - 1)
                for tt in range(2):
                    n = 2 * m + tt
                    toks = slice(tt * P, tt * P + P)
                    wait(pe, "k_staged", n)
                    if latent:
                        if tt:
                            pe.wait_ge(S["q_staged"], n - 2)
                        for kt in range(KT):
                            M(bank(4), lhsT=hT[:, kt, toks], rhs=w_in[:, kt, 0:512], start=(kt == 0), stop=(kt == KT - 1))
                    for kt in range(KT):
                        ins = M(bank(5)[:, 0:256], lhsT=hT[:, kt, toks], rhs=w_in[:, kt, 512:768],
                                start=(kt == 0), stop=(kt == KT - 1))
                    ins.then_inc(S["qkv_ready"], 1)
                    if tt == 0 or latent:
                        for f in range(LF):
                            l = LF * tt + f
                            if latent:
                                pe.wait_ge(S["lz_out"], out_before + l - 1)
                            else:
                                wait(pe, "lz_out", l - 1)
                            o = QKV + D_LRU * tt + f * P
                            for kt in range(KT):
                                ins = M(bank(6 + f % 2)[:, 0:256], lhsT=w_in[:, kt, o:o + P], rhs=hT[:, kt, :],
                                        start=(kt == 0), stop=(kt == KT - 1))
                            ins.then_inc(S["z_ready" if tt else "lru_ready"], 1)
                    pe.wait_ge(S["rot_ready"], n + 1)
                    if latent:
                        for j in range(4):
                            T(bank(4)[:, j * P:(j + 1) * P], rot[:, j * P:(j + 1) * P], ident[:, :])
                    for j in range(2):
                        ins = T(bank(5)[:, j * P:(j + 1) * P], rot[:, 512 + j * P:512 + (j + 1) * P], ident[:, :])
                    ins.then_inc(S["qkT_ready"], 1)

            pair(0, False)
            with pe.Fori(1, NTOK // 2) as m:
                pair(m, True)

            pe.wait_ge(S["bd_loaded"], 16 * 8)
            pe.wait_ge(S["lz_out"], LF + 2 * LF * (NTOK // 2 - 1))
            for f in range(LF):
                pe.wait_ge(S["conv_done"], f + 1)
                for d in range(2):
                    k = 2 * f + d
                    wait(pe, "gates_out", 2 * k)
                    for g in range(2):
                        for o in range(0, LW, 512):
                            w = min(512, LW - o)
                            ins = M(psum[:, 1536 * g + o:1536 * g + o + w], lhsT=bd[:, (2 * d + g) * LF + f, :],
                                    rhs=cu[:, o:o + w], start=True, stop=True)
                    ins.then_inc(S["gates_ready"], 1)

            def scores(n, h):
                if h == 0:
                    pe.wait_ge(S["q_loaded"], 16 * n + 16)
                    wait(pe, "s_even", 2 * n)
                    wait(pe, "s_odd", 2 * n)
                wait(pe, "probs_ready", n * NQ + h)
                o = 64 * (h % 2)
                for b in range(0, KEYS, 512):
                    w = min(512, KEYS - b)
                    ins = M(psum[:, b:b + w], lhsT=qc[o:o + 64, h // 2, :], rhs=kT[o:o + 64, h // 4, b:b + w],
                            start=True, stop=True)
                ins.then_inc(S["scores_ready"], 1)

            def att_step(n, h):
                if h + 1 < NQ:
                    scores(n, h + 1)
                pe.wait_ge(S["probs_normed"], n * NQ + h + 1)
                for g in range(3):
                    l = 3 * h + g
                    wait(pe, "pt_odd" if l % 2 else "pt_even", n * (ATT_T // 2) + l // 2)
                    for j in range(4 if g < 2 else 2):
                        kt = 4 * g + j
                        ins = T(bank(3 + l % 2)[:, j * P:(j + 1) * P], pr[:, kt * P:(kt + 1) * P], ident[:, :])
                    ins.then_inc(S["pt_ready"], 1)
                wait(pe, "att_ready", n * NQ + h - 1)
                for g in range(3):
                    l = 3 * h + g
                    pe.wait_ge(S["pt_odd" if l % 2 else "pt_even"], n * (ATT_T // 2) + l // 2 + 1)
                    for kt in range(4 * g, 4 * g + (4 if g < 2 else 2)):
                        ins = M(bank(5)[0:64, 128 * (h % 2):128 * (h % 2) + 128],
                                lhsT=v[:, kt, 64 * (h // 4):64 * (h // 4) + 64], rhs=pT[:, kt, :],
                                start=(kt == 0), stop=(kt == NTOK - 1))
                ins.then_inc(S["pv_ready"], 1)

            def post(n, k):
                if k < 2:
                    if k == 0:
                        pe.wait_ge(S["att_ready"], n * NQ + NQ)
                        pe.wait_ge(S["l_loaded"], 16 * n + 16)
                    pe.wait_ge(S["wo_loaded"], 32 * n + 16 + 16 * k)
                    for kt in range(KT):
                        ins = M(bank(k), lhsT=att[:, kt, :] if kt < 4 else lc[:, kt - 4, :], rhs=wo[:, kt, :],
                                start=(kt == 0), stop=(kt == KT - 1))
                    ins.then_inc(S["out_half"], 1)
                elif k == 2:
                    pe.wait_ge(S["hx_ready"], n + 1)
                    for kt in range(KT):
                        ins = T(psum[:, 1536 + kt * P:1536 + (kt + 1) * P], hx_new[:, kt * P:(kt + 1) * P], ident[:, :])
                    ins.then_inc(S["hxT_ready"], 1)
                elif k in (3, 6):
                    u = k // 3 - 1
                    pe.wait_ge(S["hxT_even"], n + 1)
                    pe.wait_ge(S["hxT_odd"], n + 1)
                    if k == 3:
                        pe.wait_ge(S["wq_loaded"], 16)
                        pe.wait_ge(S["sub_loaded"], 16)
                    for b in range(2):
                        for kt in range(KT):
                            ins = M(bank(b), lhsT=hxT[:, kt, :], rhs=wq[:, kt, D * u + 512 * b:D * u + 512 * b + 512],
                                    start=(kt == 0), stop=(kt == KT - 1))
                    ins.then_inc(S["q_ready"], 1)
                elif k in (4, 7):
                    pe.wait_ge(S["q_out"], 2 * n + k // 3)
                    for j in range(8):
                        ins = T(psum[:, 1536 + j * P:1536 + (j + 1) * P], q_tok[:, j * P:(j + 1) * P], ident[:, :])
                    ins.then_inc(S["qT_ready"], 1)
                elif k in (5, 8):
                    u = k // 3 - 1
                    pe.wait_ge(S["qT_even"], 2 * n + u + 1)
                    pe.wait_ge(S["qT_odd"], 2 * n + u + 1)
                    if u:
                        pe.wait_ge(S["s_even"], 2 * n + u)
                        pe.wait_ge(S["s_odd"], 2 * n + u)
                    for j in range(8):
                        ins = M(bank(2 if j < 4 else 5)[:, (j % 4) * P:(j % 4 + 1) * P], lhsT=q_T[:, j, :],
                                rhs=skT[:, 8 * u + j, :], start=True, stop=True)
                    ins.then_inc(S["s_ready"], 1)

            def v_slots(c, lo, hi):
                for j in range(lo, hi):
                    r = j % RING
                    pe.wait_ge(S["diag_ready"], c * SLOTS + j + 1)
                    pe.wait_ge(got[r], c * (16 * 2 * SLOTS // RING) + 16 * (SLOTS // RING + j // RING + 1))
                    for b in range(2):
                        ins = M(bank(6 + b), lhsT=diag[:, j % DIAGS, :], rhs=ring[:, r, 512 * b:512 * b + 512],
                                start=(j == 0), stop=(j == SLOTS - 1))
                    ins.then_inc(S["v_used"], 1)
                if hi == SLOTS:
                    pe.wait_ge(S["v_used"], c * SLOTS + SLOTS + RING)
                    pe.sem_inc(S["ffn_ready"], 1)

            scores(0, 0)
            for h in range(NQ):
                att_step(0, h)
            for k in range(STAGES):
                post(0, k)
            with pe.Fori(0, NX - 1) as c:
                scores(c + 1, 0)
                for h in range(NQ):
                    att_step(c + 1, h)
                for k in range(STAGES):
                    v_slots(c, SLICE * k, SLICE * (k + 1))
                    post(c + 1, k)
                v_slots(c, SLICE * STAGES, SLOTS)
                pe.wait_ge(S["ffn_read"], c + 1)
            v_slots(NX - 1, 0, SLOTS)


def _rope_tables():
    f = np.float32
    nf = HD // 4
    inv = f(10000.0) ** (-np.arange(nf, dtype=f) / f(nf))
    pos = np.arange(SEQ)
    ang = np.stack([(pos // GRID_W).astype(f)[:, None] * inv, (pos % GRID_W).astype(f)[:, None] * inv], 1)
    cos, sin = np.cos(ang), np.sin(ang)
    cos = np.stack([cos, cos], 2).reshape(SEQ, HD)
    sin = np.stack([-sin, sin], 2).reshape(SEQ, HD)
    cos = np.concatenate([np.ones((CTX, HD), f), cos])
    sin = np.concatenate([np.zeros((CTX, HD), f), sin])
    return [np.ascontiguousarray(a.reshape(NTOK, P, HD).transpose(1, 0, 2).astype(f)) for a in (cos, sin)]


def kernel(**inputs):
    import concourse.bacc as bacc
    from concourse.bass_utils import run_bass_kernel_spmd as run

    one = {n: np.ascontiguousarray(np.asarray(a)) for n, a in inputs.items()}
    cos, sin = _rope_tables()

    def cols(a):
        return np.moveaxis(a.reshape(a.shape[:-1] + (-1, P)), -1, 0)

    arrays = {
        "xin": np.concatenate([one["ctx"][0], one["x"][0]]).reshape(NTOK, P, D),
        "c": one["c"].reshape(D), "c_ctx": one["c_ctx"], "w_mod": one["w_mod"][0], "b_mod": one["b_mod"],
        "g_pre_mix": cols(one["g_pre_mix"][0]), "g_post_mix": one["g_post_mix"], "g_pre_ffn": one["g_pre_ffn"],
        "g_post_ffn": one["g_post_ffn"], "w_in": one["w_in"][0], "q_norm_g": one["q_norm_g"],
        "k_norm_g": one["k_norm_g"], 
        "conv_w": cols(one["conv_w"][0]).transpose(0, 2, 1), "conv_b": cols(one["conv_b"][0]),
        "lru_bias": np.stack([cols(one["rg_ba"][0]), cols(one["rg_bi"][0])], 2),
        "rg_lambda": cols(one["rg_lambda"][0]), "rg_wa": one["rg_wa"][0], "rg_wi": one["rg_wi"][0], "w_out": one["w_out"][0], "wq": one["peer_wq"][0],
        "subkeys": one["peer_subkeys"].reshape(2 * PH, NK, DK).transpose(2, 0, 1), "u": one["peer_u"][0], "v": one["peer_v"][0],
        "cos": cos, "sin": sin,
    }
    arrays = {n: np.ascontiguousarray(a) for n, a in arrays.items()}
    nc = bacc.Bacc("TRN2", target_bir_lowering=False, num_devices=1)
    t = {n: nc.dram_tensor("in_" + n, a.shape, F32, kind="ExternalInput").ap() for n, a in arrays.items()}
    t["out"] = nc.dram_tensor("out", (NX, P, D), F32, kind="ExternalOutput").ap()
    nc.disable_value_cache = True
    layer(nc, t)
    r = run(nc, [{"in_" + n: a for n, a in arrays.items()}], core_ids=[0])
    return r.results[0]["out"].reshape(1, SEQ, D)
```

```python
from contextlib import ExitStack

import numpy as np

import concourse.bass as bass
from concourse import mybir

ALU = mybir.AluOpType
ACT = mybir.ActivationFunctionType
AX = mybir.AxisListType.X
F32 = mybir.dt.float32
U32 = mybir.dt.uint32

P = 128
D = 1024
KT = D // P
SEQ, CTX = 1024, 256
GRID_W = 64
NX, NC_ = SEQ // P, CTX // P
NTOK = NX + NC_
HD = 64
NQ, NKV = 8, 2
D_ATTN = NQ * HD
D_KV = NKV * HD
D_LRU = 512
LF = D_LRU // P
D_IN = D_ATTN + 2 * D_KV + 2 * D_LRU
QKV = D_ATTN + 2 * D_KV
CONV_W, PADL = 4, 2
GAP = 3
XLW = PADL + CTX + GAP + SEQ + 1
LW = CTX + GAP + SEQ
RG_C = 8.0
KEYS = CTX + SEQ
PH, NK, DK = 8, 128, 128
TOPK = 16
SLOTS = PH * TOPK
RING = 8
DIAGS = 4
EPS = 1e-6
NEG = -3.0e38
GELU_C, GELU_K = 0.044715, 0.7978845608028654
ATT_T = 3 * NQ
AFTER = (("out", 0), ("out", 1), ("hxT", 0), ("q", 0), ("q", 1), ("qT", 0), ("s", 0), ("q", 2), ("q", 3), ("qT", 1),
         ("s", 1))
HEADS_AT, PER_HEAD = 11, 7
MIX_AT, XM_AT, HXT_AT, QT_AT, SIM_AT = 85, 88, 94, (109, 127), (112, SLOTS + 46)
TOP_AT = (SLOTS + 4, SLOTS + 49)
TOP_EVERY = 8
LAST_SIM = 44
HEAD_START = (5, 7)
V_VEC = [j for j in range(SLOTS) if j % 2 == 1]
V_PE = [j for j in range(SLOTS) if j not in V_VEC]
RANK = {j: i for part in (V_VEC, V_PE) for i, j in enumerate(part)}
assert len(V_PE) % DIAGS == 0
PAIR_STEPS = 31
CHUNK_STEPS = 185


class Chain:

    def __init__(self, eng, sem):
        self.eng, self.sem, self.base, self.k = eng, sem, 0, 0

    def step(self, ins):
        self.k += 1
        return ins.then_inc(self.sem, 1)

    def sync(self):
        self.eng.wait_ge(self.sem, self.base + self.k)

    def link(self, ins):
        self.step(ins)
        self.sync()

    def link_alone(self, ins, passed):
        self.link(ins)
        self.eng.sem_inc(passed, 1)

    def enter(self, i, per):
        self.start = self.base + self.k
        self.per = per
        self.base, self.k = self.start + i * per, 0

    def leave(self, count):
        assert self.k == self.per, (self.k, self.per)
        self.base, self.k = self.start + count * self.per, 0


def layer(nc, t):
    with ExitStack() as ctx:
        def sb(name, shape, dt=F32):
            return ctx.enter_context(nc.sbuf_tensor(name, shape, dt))

        def sem(name):
            return ctx.enter_context(nc.semaphore(name))

        ident = sb("ident", [P, P])
        wbig = sb("wbig", [P, KT * 2048])
        w_in = wbig[:, 0:KT * D_IN].rearrange("p (t n) -> p t n", t=KT)
        wq = wbig[:, :].rearrange("p (t n) -> p t n", t=KT)
        skT = sb("skT", [P, 2 * PH, NK])
        kT = sb("kT", [P, NKV, KEYS])
        v = sb("v", [P, NTOK, D_KV])
        rows = sb("rows", [P, 4, D])
        G1, A2, B2, G2 = (rows[:, i, :] for i in range(4))
        modc = sb("modc", [P, 4, KT])
        gcol = sb("gcol", [P, KT])
        iota16 = sb("iota16", [P, TOPK])
        small = sb("small", [P, 64])
        convw = sb("convw", [P, LF, CONV_W])
        convb = sb("convb", [P, LF])
        lrub = sb("lrub", [P, 2, 2, LF])
        lam = sb("lam", [P, 2, LF])
        lt = sb("lt", [P, 5, 2 * LF])
        lruk = sb("lruk", [P, 2 * LF])
        ARENA = 25680
        arena = sb("arena", [P, ARENA])

        at = [0]

        def view(n, *dims):
            assert at[0] + n <= ARENA, at[0] + n
            a = arena[:, at[0]:at[0] + n]
            at[0] += n
            
            if dims:
                names = "abcd"[:len(dims)]
                a = a.rearrange("p (%s) -> p %s" % (" ".join(names), " ".join(names)),
                                **dict(zip(names, dims)))
            return a

        wm = view(2 * 4096, 2, KT, 512)
        bmod = view(6 * D)
        rowm = view(2 * D)
        silb = view(KT * P, KT, P)
        ccol = view(2 * KT, 2, KT)
        csil = view(2 * KT, 2, KT)
        sil2 = view(2 * KT, KT, 2)
        ones = view(P)
        at[0] = 0
        XL = view(LF * XLW, LF, XLW)
        Z = view(LF * SEQ, LF, SEQ)
        lru_at = at[0]
        xp = view(2 * D, 2, D)
        hT = view(KT * 2 * P, KT, 2 * P)
        cosr = view(NTOK * HD, NTOK, HD)
        sinr = view(NTOK * HD, NTOK, HD)
        tabs = view(4 * NTOK * HD, 4, NTOK, HD)
        gq = view(2 * HD, 2, HD)
        qk = view(640)
        rot = view(768)
        swp = view(640)
        qst = view(4 * P)
        junk = view(D)
        bd = view(16 * P, 16, P)
        at[0] = lru_at
        cu = view(LW)
        tr = view(LW)
        ti = view(LW)
        av = view(LW)
        bv = view(LW)
        hf = view(LW)
        hb = view(LW)
        assert at[0] < 21000
        at[0] = 0
        ring = view(RING * D, RING, D)
        wo = view(KT * 512, KT, 512)
        pr = view(KEYS)
        pT = view(KEYS, NTOK, P)
        qc = view(4 * P, 4, P)
        lc = view(4 * P, 4, P)
        att = view(4 * P, 4, P)
        xm_new, xm_cur, hx_new, hx_cur = (view(D) for _ in range(4))
        mix = view(D)
        hxT = view(KT * P, KT, P)
        sc = view(8 * NK, 8, NK)
        diag = view(DIAGS * P, DIAGS, P)
        ff = hxT.rearrange("p t n -> p (t n)")
        act_, gx, wt, gate, top = (view(SLOTS) for _ in range(5))
        idxf = gx
        vacc = hx_cur
        cand = view(TOPK * TOPK)
        cnd2 = view(TOPK * TOPK)
        tk = cnd2[:, 0:NK]
        tv = view(2 * TOPK, 2, TOPK)
        pabu = cand[:, 0:P].bitcast(U32).rearrange("p (a h k) -> p a h k", a=2, h=4)
        selv = cand[:, P:2 * P].rearrange("p (a h k) -> p a h k", a=2, h=4)
        q_tok = pr[:, 0:D]
        q_T = pT[:, 0:8, :]
        oneh = mix.rearrange("p (h k a) -> p h k a", h=4, k=TOPK)
        ixu = sb("ixu", [P, PH, 2, TOPK], U32)
        posu = sb("posu", [P, PH, TOPK], U32)
        idx_new = sb("idx_new", [P, SLOTS], U32)
        idx_u = sb("idx_u", [P, SLOTS], U32)
        idx_v = sb("idx_v", [P, SLOTS], U32)

        psum = ctx.enter_context(nc.psum_tensor("psum", [P, 8 * 512], F32))

        def bank(b, n=1):
            return psum[:, 512 * b:512 * (b + n)]

        q_scr = nc.dram_tensor("q_scr", (NX, P, 4 * P), F32, kind="Internal").ap()
        l_scr = nc.dram_tensor("l_scr", (LF, P, SEQ), F32, kind="Internal").ap()

        S = {n: sem(n) for n in (
            "consts_made", "vec_chain", "act_chain", "pool_chain",
            "c_loaded", "bmod_loaded", "gains_loaded", "wm_loaded0", "wm_loaded1", "wm_used", "sub_loaded",
            "silu_ready", "tanh_c", "mod_mm", "mod_out", "modT_ready", "modc_ready", 
            "w_in_loaded", "x_loaded", "x_sq", "x_var", "x_sd", "xn_ready", "xT_ready", "hT_vec", "hT_act",
            "qkv_ready", "lru_ready", "z_ready", "lz_out", "qk_sq", "qk_var", "qk_sd", "qkv_read", "rot_ready", "qkT_ready",
            "q_staged", "q_free", "q_opened", "ff_free", "sc_used", "k_staged", "q_stored", "tab_loaded", "lruw_loaded", "bd_zeroed", "bd_loaded",
            "conv_done", "gates_ready", "gates_out", "lru_a", "lru_m", "lru_s", "lru_used", "lru_out", "lru_stored",
            "z_tanh", "z_in", "lam_abs", "lam_exp", "lruk_ready",
            "wq_loaded", "wo_loaded", "q_loaded", "l_loaded", "xc_loaded",
            "scores_ready", "negmax_ready", "probs_ready", "probs_normed", "pt_ready", "pt_out",
            "pv_ready", "att_ready", "out_half", "mix_sq", "mix_var", "mix_sd", "xm_ready", "xm_sq",
            "xm_var", "xm_sd", "hx_ready", "hxT_ready", "hxT_even", "hxT_odd", "q_ready", "q_out",
            "qT_ready", "qT_even", "qT_odd", "s_ready", "s_even", "s_odd", "gate_in", "gate_exp", "top_passed", "idx_ready",
            "xm_moved", "idx_taken", "u_opened", "v_opened", "u_used", "v_used", "vv_used", "gelu_in", "gelu_tanh", "w_ready", "diag_ready",
            "ffn_ready", "ffn_sq", "ffn_var", "ffn_sd", "ffn_read", "out_ready", "out_stored")}
        got = [sem(f"got{r}") for r in range(RING)]

        block = ctx.enter_context(nc.Block())

        @block.sync
        def _(sp):
            for i, name in enumerate(("c", "c_ctx")):
                sp.dma_start(ccol[:, i, :], t[name].rearrange("(p t) -> p t", p=P)).then_inc(S["c_loaded"], 16)
            sp.dma_start(bmod[0:1, :], t["b_mod"]).then_inc(S["bmod_loaded"], 16)
            wmv = t["w_mod"].rearrange("(p t) n -> p t n", p=P)

            def mod_block(n):
                if n >= 2:
                    sp.wait_ge(S["wm_used"], n - 1)
                sp.dma_start(wm[:, n % 2, :, :], wmv[:, :, 512 * n:512 * n + 512])\
                    .then_inc(S["wm_loaded%d" % (n % 2)], 16)

            mod_block(0)
            mod_block(1)
            sp.dma_start(skT[:], t["subkeys"]).then_inc(S["sub_loaded"], 16)
            for g, name in ((G1, "g_post_mix"), (A2, "g_pre_ffn"), (G2, "g_post_ffn")):
                sp.dma_start(g, t[name].broadcast_to([P, D])).then_inc(S["gains_loaded"], 16)
            sp.dma_start(gcol[:, :], t["g_pre_mix"]).then_inc(S["gains_loaded"], 16)
            for n in range(2, 12):
                mod_block(n)
                if n == 5:
                    sp.dma_start(w_in, t["w_in"].rearrange("(t p) n -> p t n", p=P)).then_inc(S["w_in_loaded"], 16)
                    for dst, name in ((lrub, "lru_bias"), (lam, "rg_lambda"), (convw, "conv_w"), (convb, "conv_b")):
                        sp.dma_start(dst[:], t[name]).then_inc(S["lruw_loaded"], 16)
            sp.wait_ge(S["modc_ready"], 1)
            sp.wait_ge(S["wm_used"], 12)
            sp.dma_start(xp, t["xin"][0:2].rearrange("t p d -> p t d")).then_inc(S["x_loaded"], 16)
            sp.dma_start(cosr, t["cos"]).then_inc(S["tab_loaded"], 16)
            sp.dma_start(sinr, t["sin"]).then_inc(S["tab_loaded"], 16)
            sp.dma_start(gq[:, 0, :], t["q_norm_g"].broadcast_to([P, HD])).then_inc(S["tab_loaded"], 16)
            sp.dma_start(gq[:, 1, :], t["k_norm_g"].broadcast_to([P, HD])).then_inc(S["tab_loaded"], 16)
            sp.wait_ge(S["bd_zeroed"], 2)
            for d in range(2):
                for g, w in enumerate(("rg_wa", "rg_wi")):
                    for b in range(2):
                        j = (2 * d + g) * LF
                        sp.dma_start(bd[64 * b:64 * b + 64, j:j + LF, 64 * b:64 * b + 64],
                                     t[w][d, b::2].rearrange("f i j -> i f j")).then_inc(S["bd_loaded"], 16)
            with sp.Fori(1, NTOK // 2) as m:
                sp.wait_ge(S["xT_ready"], m)
                sp.dma_start(xp, t["xin"][bass.ds(m * 2, 2)].rearrange("t p d -> p t d"))\
                    .then_inc(S["x_loaded"], 16)
            sp.wait_ge(S["qkv_ready"], NTOK)
            sp.wait_ge(S["lru_ready"], LF * NTOK // 2)
            sp.wait_ge(S["z_ready"], LF * NX // 2)
            sp.dma_start(wq, t["wq"].rearrange("(t p) n -> p t n", p=P)).then_inc(S["wq_loaded"], 16)
            for f in range(LF):
                sp.wait_ge(S["lru_out"], f + 1)
                sp.dma_start(l_scr[f], hf[:, CTX + GAP:LW]).then_inc(S["lru_stored"], 16)

            wov = t["w_out"].rearrange("(t p) n -> p t n", p=P)

            def load_front(n, first):
                if not first:
                    sp.wait_ge(S["scores_ready"], NQ * n)
                sp.dma_start(qc, q_scr[bass.ds(n, 1)].rearrange("o p (j c) -> (o p) j c", j=4))\
                    .then_inc(S["q_loaded"], 16)
                if not first:
                    sp.wait_ge(S["out_half"], 2 * n)
                sp.dma_start(wo, wov[:, :, 0:512]).then_inc(S["wo_loaded"], 16)
                sp.dma_start(lc, l_scr[:, :, bass.ds(n * P, P)].rearrange("f p c -> p f c"))\
                    .then_inc(S["l_loaded"], 16)

            def load_rest(n, first):
                if not first:
                    sp.wait_ge(S["xm_moved"], n)
                sp.dma_start(xm_new, t["xin"][bass.ds(n + NC_, 1)].rearrange("o p d -> (o p) d"))\
                    .then_inc(S["xc_loaded"], 16)
                sp.wait_ge(S["out_half"], 2 * n + 1)
                sp.dma_start(wo, wov[:, :, 512:D]).then_inc(S["wo_loaded"], 16)

            def store(c):
                sp.wait_ge(S["out_ready"], c + 1)
                sp.dma_start(t["out"][bass.ds(c, 1)].rearrange("o p d -> (o p) d"), ff)\
                    .then_inc(S["out_stored"], 16)
                sp.wait_ge(S["out_stored"], 16 * c + 16)
                sp.sem_inc(S["ff_free"], 1)

            sp.sem_inc(S["ff_free"], 1)
            sp.wait_ge(S["q_stored"], 16 * NX)
            sp.wait_ge(S["lru_stored"], 16 * LF)
            load_front(0, True)
            load_rest(0, True)
            load_front(1, False)
            with sp.Fori(1, NX - 1) as n:
                load_rest(n, False)
                load_front(n + 1, False)
                store(n - 1)
            load_rest(NX - 1, False)
            store(NX - 2)
            store(NX - 1)
            sp.wait_ge(S["out_stored"], 16 * NX)
            sp.wait_ge(S["q_stored"], 16 * NX)
            sp.wait_ge(S["lru_stored"], 16 * LF)

        @block.gpsimd
        def _(pool):
            ch = Chain(pool, S["pool_chain"])
            ch.link(nc.gpsimd.memset(ident[:, :], 0.0))
            ch.link(nc.gpsimd.affine_select(out=ident[:, :], in_=ident[:, :], compare_op=ALU.not_equal, fill=1.0,
                                            base=0, pattern=[[-1, P]], channel_multiplier=1))
            nc.gpsimd.memset(ones, 1.0).then_inc(S["consts_made"], 1)
            nc.gpsimd.iota(iota16[:, :], pattern=[[1, TOPK]], base=0, channel_multiplier=0,
                           allow_small_or_imprecise_dtypes=True).then_inc(S["consts_made"], 1)
            pool.wait_ge(S["modc_ready"], 1)
            pool.wait_ge(S["wm_used"], 12)
            nc.gpsimd.memset(XL, 0.0).then_inc(S["bd_zeroed"], 1)
            nc.gpsimd.memset(bd, 0.0).then_inc(S["bd_zeroed"], 1)

            pool.sem_inc(S["q_free"], 1)
            with pool.Fori(0, NX) as x:
                pool.wait_ge(S["q_staged"], x + 1)
                pool.sem_inc(S["q_opened"], 1)
                pool.dma_start(q_scr[bass.ds(x, 1)].rearrange("o p n -> (o p) n"), qst)\
                    .then_inc(S["q_stored"], 16)
                pool.wait_ge(S["q_stored"], 16 * x + 16)
                pool.sem_inc(S["q_free"], 1)

            pool.sem_inc(S["v_used"], len(V_PE))
            pool.sem_inc(S["vv_used"], len(V_VEC))

            def v_free(c, j):
                if j in V_VEC:
                    pool.wait_ge(S["vv_used"], c * len(V_VEC) + RANK[j] + 1)
                else:
                    pool.wait_ge(S["v_used"], c * len(V_PE) + RANK[j] + 1)
            pool.wait_ge(S["lru_stored"], 16 * LF)
            pool.wait_ge(S["q_stored"], 16 * NX)

            def gather(table, idx, j, r):
                pool.indirect_dma_start(ring[:, r, :], None, t[table],
                                        bass.IndirectOffsetOnAxis(idx[:, j:j + 1], 0)).then_inc(got[r], 16)

            with pool.Fori(0, NX) as c:
                pool.wait_ge(S["idx_ready"], c + 1)
                pool.sem_inc(S["u_opened"], 1)
                ch.enter(c, 2)
                ch.link(nc.gpsimd.tensor_copy(idx_u[:, :], idx_new[:, :]))
                pool.sem_inc(S["idx_taken"], 1)
                for j in range(SLOTS):
                    if j < RING:
                        v_free(c, SLOTS - RING + j)
                    else:
                        pool.wait_ge(S["u_used"], c * SLOTS + j - RING + 1)
                    pool.sem_inc(S["u_opened"], 1)
                    gather("u", idx_u, j, j % RING)
                v_free(c, V_PE[-1])
                pool.sem_inc(S["v_opened"], 1)
                v_free(c, V_VEC[-1])
                pool.sem_inc(S["v_opened"], 1)
                ch.link(nc.gpsimd.tensor_copy(idx_v[:, :], idx_u[:, :]))
                for j in range(SLOTS):
                    if j < RING:
                        pool.wait_ge(S["u_used"], c * SLOTS + SLOTS - RING + j + 1)
                    else:
                        v_free(c + 1, j - RING)
                    pool.sem_inc(S["v_opened"], 1)
                    gather("v", idx_v, j, j % RING)
            ch.leave(NX)

        def wait(eng, name, val):
            if isinstance(val, int) and val <= 0:
                return
            eng.wait_ge(S[name], val)

        @block.scalar
        def _(act):
            ch = Chain(act, S["act_chain"])
            A = nc.scalar.activation
            act.wait_ge(S["c_loaded"], 32)
            A(csil, ccol, ACT.Tanh, scale=0.5).then_inc(S["tanh_c"], 1)

            def pair(m, latent, m_is_static):
                act.wait_ge(S["x_loaded"], 16 * m + 16)
                ch.link(A(junk, xp[:, 0, :], ACT.Square, accum_out=small[:, 0:1]))
                A(junk, xp[:, 1, :], ACT.Square, accum_out=small[:, 1:2]).then_inc(S["x_sq"], 1)
                act.wait_ge(S["x_var"], m + 1)
                A(small[:, 2:4], small[:, 2:4], ACT.Sqrt).then_inc(S["x_sd"], 1)
                sc_, sh_ = (0, 1) if latent else (2, 3)
                act.wait_ge(S["xT_ready"], m + 1)
                for kt in range(KT):
                    ins = A(hT[:, kt, P:2 * P], psum[:, D + kt * P:D + (kt + 1) * P], ACT.Identity,
                            scale=modc[:, sc_, kt:kt + 1], bias=modc[:, sh_, kt:kt + 1])
                ins.then_inc(S["hT_act"], 1)
                lo = 0 if latent else D_ATTN
                for tt in range(2):
                    n = 2 * m + tt
                    act.wait_ge(S["qkv_ready"], n + 1)
                    wait(act, "rot_ready", n)
                    A(swp[:, lo:640], psum[:, 2048 + lo:2048 + 640], ACT.Square).then_inc(S["qk_sq"], 1)
                    act.wait_ge(S["qk_var"], n + 1)
                    A(small[:, 16 + lo // HD:26], small[:, 16 + lo // HD:26], ACT.Sqrt).then_inc(S["qk_sd"], 1)
                    if tt == 0 or latent:
                        for f in range(LF):
                            if tt == 0:
                                act.wait_ge(S["lru_ready"], LF * m + f + 1)
                                dst = XL[:, f, bass.ds(m * 256 + (PADL + GAP), 256)] if latent \
                                    else XL[:, f, PADL:PADL + CTX]
                            else:
                                act.wait_ge(S["z_ready"], LF * m - LF + f + 1)
                                dst = Z[:, f, bass.ds(m * 256 - 256, 256)]
                            A(dst, bank(6 + f % 2)[:, 0:256], ACT.Copy).then_inc(S["lz_out"], 1)
                    if latent:
                        act.wait_ge(S["qkT_ready"], n + 1)
                        act.wait_ge(S["q_free"], n - 1)
                        A(qst, bank(4), ACT.Copy).then_inc(S["q_staged"], 1)

            act.wait_ge(S["modc_ready"], 1)
            act.wait_ge(S["wm_used"], 12)
            act.wait_ge(S["bd_zeroed"], 2)
            pair(0, False, True)
            with act.Fori(1, NTOK // 2) as m:
                ch.enter(m - 1, 1)
                pair(m, True, False)
            ch.leave(NTOK // 2 - 1)

            act.wait_ge(S["lam_abs"], 1)
            A(lt[:, 1, :], lt[:, 0, :], ACT.Exp, scale=-1.0).then_inc(S["lam_exp"], 1)
            act.wait_ge(S["lruk_ready"], 1)
            for f in range(LF):
                for d in range(2):
                    k = 2 * f + d
                    act.wait_ge(S["gates_ready"], k + 1)
                    wait(act, "lru_used", k)
                    kcol = lruk[:, LF * d + f:LF * d + f + 1]
                    A(tr, psum[:, 0:LW], ACT.Tanh, scale=0.5, bias=lrub[:, d, 0, f:f + 1]).then_inc(S["gates_out"], 1)
                    A(ti, psum[:, 1536:1536 + LW], ACT.Tanh, scale=0.5, bias=lrub[:, d, 1, f:f + 1])\
                        .then_inc(S["gates_out"], 1)
                    act.wait_ge(S["gates_out"], 2 * k + 2)
                    ch.link(A(av, tr, ACT.Exp, scale=kcol, bias=kcol))
                    A(tr, tr, ACT.Tanh, scale=kcol, bias=kcol).then_inc(S["lru_a"], 1)
                    act.wait_ge(S["lru_m"], k + 1)
                    A(bv, bv, ACT.Sqrt, scale=0.25).then_inc(S["lru_s"], 1)
                act.wait_ge(S["z_in"], f + 1)
                A(tr[:, 0:SEQ], tr[:, 0:SEQ], ACT.Tanh, scale=GELU_K).then_inc(S["z_tanh"], 1)

            def probs(n, h):
                a, b = 44 + h % 2, 46 + h % 2
                act.wait_ge(S["negmax_ready"], n * NQ + h + 1)
                wait(act, "pt_ready", n * ATT_T + 3 * h)
                A(pr, psum[:, 0:KEYS], ACT.Exp, scale=HD ** -0.5, bias=small[:, a:a + 1],
                  accum_out=small[:, b:b + 1]).then_inc(S["probs_ready"], 1)

            def att_step(n, h):
                for g in range(3):
                    k = 4 if g < 2 else 2
                    act.wait_ge(S["pt_ready"], n * ATT_T + 3 * h + g + 1)
                    A(pT[:, 4 * g:4 * g + k, :], bank(3 + (3 * h + g) % 2)[:, 0:k * P], ACT.Copy)\
                        .then_inc(S["pt_out"], 1)
                if h + 1 < NQ:
                    probs(n, h + 1)
                act.wait_ge(S["pv_ready"], n * NQ + h + 1)
                o = 64 * (h % 2)
                A(att[o:o + 64, h // 2, :], bank(5)[0:64, 128 * (h % 2):128 * (h % 2) + 128], ACT.Copy)\
                    .then_inc(S["att_ready"], 1)

            def post(n, step, i):
                if (step, i) == ("out", 1):
                    act.wait_ge(S["out_half"], 2 * n + 2)
                    wait(act, "idx_ready", n)
                    A(mix, psum[:, 0:D], ACT.Square, accum_out=small[:, 48:49]).then_inc(S["mix_sq"], 1)
                    act.wait_ge(S["mix_var"], n + 1)
                    A(small[:, 49:50], small[:, 49:50], ACT.Sqrt).then_inc(S["mix_sd"], 1)
                    act.wait_ge(S["xm_ready"], n + 1)
                    A(mix, xm_new, ACT.Square, accum_out=small[:, 48:49]).then_inc(S["xm_sq"], 1)
                    act.wait_ge(S["xm_var"], n + 1)
                    A(small[:, 49:50], small[:, 49:50], ACT.Sqrt).then_inc(S["xm_sd"], 1)
                elif step == "hxT":
                    act.wait_ge(S["hxT_ready"], n + 1)
                    wait(act, "ff_free", n)
                    A(hxT[:, 4:8, :], bank(4), ACT.Copy).then_inc(S["hxT_odd"], 1)
                elif step == "q":
                    act.wait_ge(S["q_ready"], 4 * n + i + 1)
                    A(q_tok[:, 512 * (i % 2):512 * (i % 2) + 512], bank(i % 2), ACT.Copy).then_inc(S["q_out"], 1)
                elif step == "qT":
                    act.wait_ge(S["qT_ready"], 2 * n + i + 1)
                    A(q_T[:, 4:8, :], bank(4), ACT.Copy).then_inc(S["qT_odd"], 1)
                elif step == "s":
                    act.wait_ge(S["s_ready"], 2 * n + i + 1)
                    wait(act, "sc_used", 2 * n + i)
                    A(sc[:, 4:8, :], bank(5), ACT.Copy).then_inc(S["s_odd"], 1)

            def diags(c, lo, hi):
                if lo == 0:
                    act.wait_ge(S["w_ready"], c + 1)
                for j in range(lo, min(hi, SLOTS)):
                    if j in V_PE:
                        k = RANK[j]
                        act.wait_ge(S["v_used"], (c + 1) * len(V_PE) + k + 1 - DIAGS)
                        A(diag[:, k % DIAGS, :], ident[:, :], ACT.Copy, scale=wt[:, j:j + 1])\
                            .then_inc(S["diag_ready"], 1)

            def gates(n):
                act.wait_ge(S["gate_in"], n + 1)
                A(gate, gate, ACT.Exp).then_inc(S["gate_exp"], 1)

            def finish(c):
                act.wait_ge(S["ffn_ready"], c + 1)
                act.wait_ge(S["ff_free"], c + 1)
                A(ff, vacc, ACT.Square, accum_out=small[:, 52:53]).then_inc(S["ffn_sq"], 1)
                act.wait_ge(S["ffn_var"], c + 1)
                A(small[:, 53:54], small[:, 53:54], ACT.Sqrt).then_inc(S["ffn_sd"], 1)

            def gelu(c):
                act.wait_ge(S["gelu_in"], c + 1)
                A(gx, gx, ACT.Tanh, scale=GELU_K).then_inc(S["gelu_tanh"], 1)

            probs(0, 0)
            for h in range(NQ):
                att_step(0, h)
            for step in AFTER:
                post(0, *step)
            gates(0)
            with act.Fori(0, NX - 1) as c:
                probs(c + 1, 0)
                for h in range(NQ):
                    att_step(c + 1, h)
                for step in AFTER[:-1]:
                    post(c + 1, *step)
                gelu(c)
                ahead = V_PE[RANK[next(j for j in V_PE if j >= LAST_SIM)] + DIAGS]
                diags(c, 0, ahead)
                post(c + 1, *AFTER[-1])
                diags(c, ahead, SLOTS)
                gates(c + 1)
                finish(c)
            gelu(NX - 1)
            diags(NX - 1, 0, SLOTS)
            finish(NX - 1)

        @block.vector
        def _(dve):
            ch = Chain(dve, S["vec_chain"])
            V = nc.vector

            dve.sem_inc(S["ffn_read"], 1)
            dve.wait_ge(S["tanh_c"], 1)
            dve.wait_ge(S["consts_made"], 2)
            ch.link(V.scalar_tensor_tensor(csil, csil, 1.0, ccol, ALU.add, ALU.mult))
            ch.link(V.tensor_scalar(csil, csil, 0.5, None, ALU.mult))
            ch.step(V.tensor_copy(sil2, csil.rearrange("p i t -> p t i")))
            ch.link(V.tensor_copy(silb, csil[:, 0, :].unsqueeze(2).broadcast_to([P, KT, P])))
            dve.sem_inc(S["silu_ready"], 1)

            def mod_row(n):
                dve.wait_ge(S["wm_used"], n + 1)
                src, at_ = bank(n % 2), slice(512 * (n % 2), 512 * (n % 2) + 512)
                if n < 4:
                    ins = V.tensor_copy(rowm[0:2, 512 * n:512 * n + 512], src[0:2, :])
                elif n < 6:
                    ins = V.tensor_tensor(G1[:, at_], src, G1[:, at_], ALU.mult)
                elif n < 8:
                    ins = V.tensor_copy(B2[:, at_], src)
                elif n < 10:
                    ins = V.scalar_tensor_tensor(A2[:, at_], src, 1.0, A2[:, at_], ALU.add, ALU.mult)
                else:
                    ins = V.tensor_tensor(G2[:, at_], src, G2[:, at_], ALU.mult)
                ins.then_inc(S["mod_out"], 1)

            for n in range(4):
                mod_row(n)
            dve.wait_ge(S["modT_ready"], 1)
            dve.wait_ge(S["gains_loaded"], 64)
            cols = bank(2)[:, 0:4 * KT].rearrange("p (j i) -> p i j", i=2)
            for i in range(2):
                ch.step(V.scalar_tensor_tensor(modc[:, 2 * i, :], cols[:, i, KT:2 * KT], 1.0, gcol[:, :],
                                               ALU.add, ALU.mult))
                ch.link(V.tensor_copy(modc[:, 2 * i + 1, :], cols[:, i, 0:KT]))
            dve.sem_inc(S["modc_ready"], 1)
            for n in range(4, 12):
                mod_row(n)

            dve.wait_ge(S["tab_loaded"], 64)
            half = "p n (x h f) -> p n x h f"
            for i in range(2):
                g = gq[:, i, :]
                ch.step(V.tensor_tensor(tabs[:, 2 * i], cosr, g.unsqueeze(1).broadcast_to([P, NTOK, HD]), ALU.mult))
                g4 = g.rearrange("p (x h f) -> p x h f", x=2, h=2)
                for hf_ in range(2):
                    for x_ in range(2):
                        o = 32 * x_ + 16 * hf_
                        ch.step(V.tensor_tensor(tabs[:, 2 * i + 1, :, o:o + 16], sinr[:, :, o:o + 16],
                                                g4[:, x_, 1 - hf_, :].unsqueeze(1).broadcast_to([P, NTOK, 16]),
                                                ALU.mult))
            ch.sync()

            def pair(m, latent):
                dve.wait_ge(S["x_sq"], m + 1)
                ch.step(V.tensor_scalar(small[:, 2:4], small[:, 0:2], 1.0 / D, EPS, ALU.mult, ALU.add))
                ch.sync()
                dve.sem_inc(S["x_var"], 1)
                dve.wait_ge(S["x_sd"], m + 1)
                ch.link(V.reciprocal(small[:, 4:6], small[:, 2:4]))
                ch.step(V.tensor_scalar(xp[:, 0, :], xp[:, 0, :], small[:, 4:5], None, ALU.mult))
                V.tensor_scalar(xp[:, 1, :], xp[:, 1, :], small[:, 5:6], None, ALU.mult)\
                    .then_inc(S["xn_ready"], 1)
                sc_, sh_ = (0, 1) if latent else (2, 3)
                dve.wait_ge(S["xT_ready"], m + 1)
                for kt in range(KT):
                    ins = V.tensor_scalar(hT[:, kt, 0:P], psum[:, kt * P:(kt + 1) * P],
                                          modc[:, sc_, kt:kt + 1], modc[:, sh_, kt:kt + 1], ALU.mult, ALU.add)
                ins.then_inc(S["hT_vec"], 1)
                h0 = 0 if latent else NQ
                lo = h0 * HD
                for tt in range(2):
                    n = 2 * m + tt
                    dve.wait_ge(S["qk_sq"], n + 1)
                    ch.step(V.tensor_copy(v[:, bass.ds(n, 1), :].rearrange("p o d -> p (o d)"),
                                          psum[:, 2048 + 640:2048 + 768]))
                    ch.link(V.tensor_reduce(small[:, 16 + h0:26],
                                            swp[:, lo:640].rearrange("p (h d) -> p h d", d=HD), AX, ALU.add))
                    ch.link(V.tensor_scalar(small[:, 16 + h0:26], small[:, 16 + h0:26], 1.0 / HD, EPS,
                                            ALU.mult, ALU.add))
                    dve.sem_inc(S["qk_var"], 1)
                    dve.wait_ge(S["qk_sd"], n + 1)
                    ch.link(V.reciprocal(small[:, 32 + h0:42], small[:, 16 + h0:26]))
                    nh = 10 - h0
                    ch.link(V.tensor_tensor(
                        qk[:, lo:640].rearrange("p (h d) -> p h d", d=HD),
                        psum[:, 2048 + lo:2048 + 640].rearrange("p (h d) -> p h d", d=HD),
                        small[:, 32 + h0:42].unsqueeze(2).broadcast_to([P, nh, HD]), ALU.mult))
                    wait(dve, "qkT_ready", n)
                    parts = [(1, NQ, 10)] + ([(0, 0, NQ)] if latent else [])
                    for i, a, b in parts:
                        k_ = b - a
                        tab = tabs[:, 2 * i + 1, bass.ds(n, 1), :].rearrange("p o d -> p (o d)")
                        for hf_ in range(2):
                            def half_of(ap, which, heads=k_):
                                ap = ap.rearrange("p (h x s f) -> p h x s f", x=2, s=2, f=16)
                                return ap[:, :, :, which, :]
                            tb = tab.rearrange("p (x s f) -> p x s f", x=2, s=2)[:, :, hf_, :]
                            ch.step(V.tensor_tensor(half_of(swp[:, a * HD:b * HD], hf_),
                                                    half_of(qk[:, a * HD:b * HD], 1 - hf_),
                                                    tb.unsqueeze(1).broadcast_to([P, k_, 2, 16]), ALU.mult))
                    ch.sync()
                    for i, a, b in parts:
                        k_ = b - a
                        q3 = qk[:, a * HD:b * HD].rearrange("p (h d) -> p h d", d=HD)
                        cs = tabs[:, 2 * i, bass.ds(n, 1), :].rearrange("p o d -> p (o d)")
                        ch.step(V.tensor_tensor(q3, q3, cs.unsqueeze(1).broadcast_to([P, k_, HD]), ALU.mult))
                    ch.sync()
                    if latent:
                        ch.step(V.tensor_tensor(rot[:, 0:D_ATTN], qk[:, 0:D_ATTN], swp[:, 0:D_ATTN], ALU.add))
                    for dup in range(2):
                        ch.step(V.tensor_tensor(
                            rot[:, 512:768].rearrange("p (k u d) -> p k u d", k=2, u=2)[:, :, dup, :],
                            qk[:, 512:640].rearrange("p (k d) -> p k d", k=2),
                            swp[:, 512:640].rearrange("p (k d) -> p k d", k=2), ALU.add))
                    ch.sync()
                    dve.sem_inc(S["rot_ready"], 1)
                    dve.wait_ge(S["qkT_ready"], n + 1)
                    V.tensor_copy(kT[:, :, bass.ds(n * P, P)],
                                  bank(5)[:, 0:2 * P].rearrange("p (k n) -> p k n", k=2)).then_inc(S["k_staged"], 1)

            pair(0, False)
            with dve.Fori(1, NTOK // 2) as m:
                ch.enter(m - 1, PAIR_STEPS)
                pair(m, True)
            ch.leave(NTOK // 2 - 1)

            dve.wait_ge(S["lruw_loaded"], 16 * 4)
            lamf = lam[:, :, :].rearrange("p d f -> p (d f)")
            V.scalar_tensor_tensor(lt[:, 0, :], lamf, -1.0, lamf, ALU.mult, ALU.max).then_inc(S["lam_abs"], 1)
            lb = lrub[:, :, :, :].rearrange("p d g f -> p (d g f)")
            ch.step(V.tensor_scalar(lb, lb, 0.5, None, ALU.mult))
            dve.wait_ge(S["lam_exp"], 1)
            ch.link(V.tensor_scalar(lt[:, 2, :], lt[:, 1, :], 2.0, None, ALU.add))
            ch.link(V.reciprocal(lt[:, 2, :], lt[:, 2, :]))
            ch.link(V.tensor_tensor(lt[:, 1, :], lt[:, 1, :], lt[:, 2, :], ALU.mult))
            ch.link(V.tensor_tensor(lt[:, 2, :], lt[:, 1, :], lt[:, 1, :], ALU.mult))
            ch.link(V.tensor_scalar(lt[:, 3, :], lt[:, 2, :], 1.0 / 17, None, ALU.mult))
            for k in range(15, 1, -2):
                ch.link(V.scalar_tensor_tensor(lt[:, 3, :], lt[:, 3, :], 1.0 / k, lt[:, 2, :], ALU.add, ALU.mult))
            ch.link(V.scalar_tensor_tensor(lt[:, 3, :], lt[:, 3, :], 1.0, lt[:, 1, :], ALU.add, ALU.mult))
            ch.link(V.tensor_scalar(lt[:, 4, :], lamf, -1.0, 0.0, ALU.mult, ALU.max))
            ch.link(V.scalar_tensor_tensor(lt[:, 4, :], lt[:, 3, :], 2.0, lt[:, 4, :], ALU.mult, ALU.add))
            ch.link(V.tensor_scalar(lruk[:, :], lt[:, 4, :], -RG_C / 2, None, ALU.mult))
            dve.sem_inc(S["lruk_ready"], 1)

            lx = slice(CTX + GAP, LW)
            dve.wait_ge(S["lz_out"], LF + 2 * LF * (NTOK // 2 - 1))
            for f in range(LF):
                wait(dve, "gates_ready", 2 * f)
                ch.link(V.tensor_scalar(cu, XL[:, f, 0:LW], convw[:, f, 0:1], convb[:, f:f + 1],
                                        ALU.mult, ALU.add))
                for j in range(1, CONV_W):
                    ins = V.scalar_tensor_tensor(cu, XL[:, f, j:j + LW], convw[:, f, j:j + 1], cu,
                                                 ALU.mult, ALU.add)
                    if j < CONV_W - 1:
                        ch.link(ins)
                ch.link(ins)
                dve.sem_inc(S["conv_done"], 1)
                for d in range(2):
                    k = 2 * f + d
                    dve.wait_ge(S["lru_a"], k + 1)
                    ch.link(V.tensor_tensor(bv, av, av, ALU.mult))
                    ch.link(V.scalar_tensor_tensor(bv, bv, 1.0, tr, ALU.add, ALU.mult))
                    V.tensor_scalar(bv, bv, -1.0, 0.0, ALU.mult, ALU.max).then_inc(S["lru_m"], 1)
                    ch.link(V.scalar_tensor_tensor(ti, ti, 1.0, cu, ALU.add, ALU.mult))
                    dve.wait_ge(S["lru_s"], k + 1)
                    ch.link(V.tensor_tensor(bv, bv, ti, ALU.mult))
                    if d == 0:
                        ch.step(V.memset(av[:, CTX:CTX + GAP], 1.0))
                        ch.link(V.memset(bv[:, CTX:CTX + GAP], 0.0))
                        wait(dve, "lru_stored", 16 * f)
                        ins = V.tensor_tensor_scan(hf, av, bv, 0.0, ALU.mult, ALU.add)
                    else:
                        ch.link(V.tensor_tensor_scan(hb[:, 0:CTX][:, ::-1], av[:, 0:CTX][:, ::-1],
                                                     bv[:, 0:CTX][:, ::-1], 0.0, ALU.mult, ALU.add))
                        ins = V.tensor_tensor_scan(hb[:, lx][:, ::-1], av[:, lx][:, ::-1], bv[:, lx][:, ::-1],
                                                   hb[:, 0:1], ALU.mult, ALU.add)
                    ch.link(ins)
                    if d == 0:
                        dve.sem_inc(S["lru_used"], 1)
                zf = Z[:, f, :]
                ch.link(V.tensor_tensor(hf[:, lx], hf[:, lx], hb[:, lx], ALU.add))
                ch.link(V.tensor_tensor(tr[:, 0:SEQ], zf, zf, ALU.mult))
                ch.link(V.tensor_scalar(tr[:, 0:SEQ], tr[:, 0:SEQ], GELU_C, 1.0, ALU.mult, ALU.add))
                V.tensor_tensor(tr[:, 0:SEQ], tr[:, 0:SEQ], zf, ALU.mult).then_inc(S["z_in"], 1)
                ch.link(V.scalar_tensor_tensor(hf[:, lx], hf[:, lx], 0.5, zf, ALU.mult, ALU.mult))
                dve.wait_ge(S["z_tanh"], f + 1)
                ch.link(V.scalar_tensor_tensor(hf[:, lx], tr[:, 0:SEQ], 1.0, hf[:, lx], ALU.add, ALU.mult))
                dve.sem_inc(S["lru_out"], 1)
                dve.sem_inc(S["lru_used"], 1)

            def negmax(n, h):
                a = 44 + h % 2
                dve.wait_ge(S["scores_ready"], n * NQ + h + 1)
                ch.link(V.tensor_reduce(small[:, a:a + 1], psum[:, 0:KEYS], AX, ALU.max))
                V.tensor_scalar(small[:, a:a + 1], small[:, a:a + 1], -HD ** -0.5, None, ALU.mult)\
                    .then_inc(S["negmax_ready"], 1)

            def att_step(n, h):
                b = 46 + h % 2
                dve.wait_ge(S["probs_ready"], n * NQ + h + 1)
                ch.link(V.reciprocal(small[:, b:b + 1], small[:, b:b + 1]))
                V.tensor_scalar(pr, pr, small[:, b:b + 1], None, ALU.mult).then_inc(S["probs_normed"], 1)
                if h + 1 < NQ:
                    negmax(n, h + 1)

            def root(count, at_, sq, var, sd):
                dve.wait_ge(S[sq], count)
                V.tensor_scalar(small[:, at_ + 1:at_ + 2], small[:, at_:at_ + 1], 1.0 / D, EPS,
                                ALU.mult, ALU.add).then_inc(S[var], 1)
                dve.wait_ge(S[sd], count)
                ch.link(V.reciprocal(small[:, at_ + 2:at_ + 3], small[:, at_ + 1:at_ + 2]))

            def top16(vals, idx, src, scratch):
                passed = S["top_passed"]
                ch.link_alone(V.max(vals[:, 0:8], src), passed)
                ch.step(V.max_index(idx[:, 0:8], vals[:, 0:8], src))
                ch.link_alone(V.match_replace(scratch, vals[:, 0:8], src, NEG), passed)
                ch.link_alone(V.max(vals[:, 8:16], scratch), passed)
                ch.link_alone(V.max_index(idx[:, 8:16], vals[:, 8:16], scratch), passed)

            def retrieve(n, u, fill):
                for j in range(4):
                    fill(TOP_AT[u] + TOP_EVERY * j)
                    dve.sem_inc(S["top_passed"], 1)
                    h = 4 * u + j
                    for p_ in range(2):
                        if p_:
                            fill(TOP_AT[u] + TOP_EVERY * j + 3)
                            dve.sem_inc(S["top_passed"], 1)
                        top16(tv[:, p_, :], ixu[:, h, p_, :], sc[:, 2 * j + p_, :], tk)
                    fill(TOP_AT[u] + TOP_EVERY * j + 5)
                    ch.link(V.tensor_tensor(cand.rearrange("p (a b) -> p a b", a=TOPK),
                                            tv[:, 0, :].unsqueeze(2).broadcast_to([P, TOPK, TOPK]),
                                            tv[:, 1, :].unsqueeze(1).broadcast_to([P, TOPK, TOPK]), ALU.add))
                    dve.sem_inc(S["top_passed"], 1)
                    top16(top[:, TOPK * h:TOPK * h + TOPK], posu[:, h, :], cand, cnd2)
                dve.sem_inc(S["sc_used"], 1)
                fill(TOP_AT[u] + TOP_EVERY * 4)
                hs = slice(4 * u, 4 * u + 4)
                ch.step(V.tensor_scalar(pabu[:, 0], posu[:, hs, :], 4, None, ALU.logical_shift_right))
                ch.link(V.tensor_scalar(pabu[:, 1], posu[:, hs, :], 15, None, ALU.bitwise_and))
                for p_ in range(2):
                    fill(TOP_AT[u] + TOP_EVERY * 4 + 3 * p_)
                    ch.link(V.tensor_tensor(
                        oneh.rearrange("p h k a -> p (h k) a"),
                        pabu[:, p_].rearrange("p h k -> p (h k)").unsqueeze(2).broadcast_to([P, 4 * TOPK, TOPK]),
                        iota16[:, :].unsqueeze(1).broadcast_to([P, 4 * TOPK, TOPK]), ALU.is_equal))
                    ch.link(V.tensor_tensor(oneh, oneh, ixu[:, hs, p_, :].unsqueeze(2)
                                            .broadcast_to([P, 4, TOPK, TOPK]), ALU.mult))
                    ch.link(V.tensor_reduce(selv[:, p_], oneh, AX, ALU.add))
                fill(TOP_AT[u] + TOP_EVERY * 4 + 6)
                if u == 0:
                    wait(dve, "idx_taken", n)
                ch.link(V.scalar_tensor_tensor(idxf[:, 64 * u:64 * u + 64],
                                               selv[:, 0].rearrange("p h k -> p (h k)"), float(NK),
                                               selv[:, 1].rearrange("p h k -> p (h k)"), ALU.mult, ALU.add))
                ch.link(V.tensor_copy(idx_new[:, 64 * u:64 * u + 64], idxf[:, 64 * u:64 * u + 64]))

            def post(n, fill):
                fill(MIX_AT)
                root(n + 1, 48, "mix_sq", "mix_var", "mix_sd")
                ch.link(V.scalar_tensor_tensor(mix, psum[:, 0:D], small[:, 50:51], G1, ALU.mult, ALU.mult))
                dve.wait_ge(S["xc_loaded"], 16 * n + 16)
                ch.link(V.tensor_tensor(xm_new, xm_new, mix, ALU.add))
                dve.sem_inc(S["xm_ready"], 1)
                fill(XM_AT)
                root(n + 1, 48, "xm_sq", "xm_var", "xm_sd")
                ch.link(V.scalar_tensor_tensor(hx_new, xm_new, small[:, 50:51], A2, ALU.mult, ALU.mult))
                ch.link(V.tensor_tensor(hx_new, hx_new, B2, ALU.add))
                dve.sem_inc(S["hx_ready"], 1)
                fill(HXT_AT)
                dve.wait_ge(S["hxT_ready"], n + 1)
                wait(dve, "ff_free", n)
                V.tensor_copy(hxT[:, 0:4, :], bank(3)).then_inc(S["hxT_even"], 1)

                def open_half(u):
                    fill(QT_AT[u])
                    dve.wait_ge(S["qT_ready"], 2 * n + u + 1)
                    V.tensor_copy(q_T[:, 0:4, :], bank(3)).then_inc(S["qT_even"], 1)

                open_half(0)
                for u in range(2):
                    fill(SIM_AT[u])
                    dve.wait_ge(S["s_ready"], 2 * n + u + 1)
                    ch.link(V.tensor_copy(sc[:, 0:4, :], bank(2)))
                    dve.sem_inc(S["s_even"], 1)
                    if u == 0:
                        open_half(1)
                    dve.wait_ge(S["s_odd"], 2 * n + u + 1)
                    dve.sem_inc(S["top_passed"], 1)
                    retrieve(n, u, fill)
                t3 = top.rearrange("p (h k) -> p h k", k=TOPK)
                g3 = gate.rearrange("p (h k) -> p h k", k=TOPK)
                V.tensor_tensor(g3, t3, t3[:, :, 0:1].broadcast_to([P, PH, TOPK]), ALU.subtract)\
                    .then_inc(S["gate_in"], 1)
                dve.sem_inc(S["idx_ready"], 1)

            def gates(n):
                g3 = gate.rearrange("p (h k) -> p h k", k=TOPK)
                dve.wait_ge(S["gate_exp"], n + 1)
                ch.link(V.tensor_reduce(small[:, 56:64], g3, AX, ALU.add))
                ch.link(V.reciprocal(small[:, 56:64], small[:, 56:64]))
                ch.link(V.tensor_tensor(g3, g3, small[:, 56:64].unsqueeze(2).broadcast_to([P, PH, TOPK]), ALU.mult))

            def move():
                ch.step(V.tensor_copy(xm_cur, xm_new))
                ch.link(V.tensor_copy(hx_cur, hx_new))
                dve.sem_inc(S["xm_moved"], 1)

            def u_slots(c, lo, hi, tokens):
                for j in range(lo, hi):
                    r = j % RING
                    dve.wait_ge(got[r], c * (16 * 2 * SLOTS // RING) + 16 * (j // RING + 1))
                    V.tensor_tensor_reduce(ring[:, r, :], ring[:, r, :], tokens, 1.0, 0.0, ALU.mult, ALU.add,
                                           act_[:, j:j + 1]).then_inc(S["u_used"], 1)

            def weights(c):
                dve.wait_ge(S["u_used"], c * SLOTS + SLOTS)
                ch.link(V.tensor_tensor(gx, act_, act_, ALU.mult))
                ch.link(V.tensor_scalar(gx, gx, GELU_C, 1.0, ALU.mult, ALU.add))
                V.tensor_tensor(gx, gx, act_, ALU.mult).then_inc(S["gelu_in"], 1)
                dve.wait_ge(S["v_used"], c * len(V_PE) + len(V_PE))
                ch.link(V.scalar_tensor_tensor(wt, act_, 0.5, gate, ALU.mult, ALU.mult))
                dve.wait_ge(S["gelu_tanh"], c + 1)
                ch.link(V.scalar_tensor_tensor(wt, gx, 1.0, wt, ALU.add, ALU.mult))
                dve.sem_inc(S["w_ready"], 1)

            def v_slots(c, lo, hi):
                for j in range(lo, hi):
                    if j not in V_VEC:
                        continue
                    r, k = j % RING, RANK[j]
                    if k:
                        dve.wait_ge(S["vv_used"], c * len(V_VEC) + len(V_VEC) + k)
                    dve.wait_ge(got[r], c * (16 * 2 * SLOTS // RING) + 16 * (SLOTS // RING + j // RING + 1))
                    if k == 0:
                        ins = V.tensor_scalar(vacc, ring[:, r, :], wt[:, j:j + 1], None, ALU.mult)
                    else:
                        ins = V.scalar_tensor_tensor(vacc, ring[:, r, :], wt[:, j:j + 1], vacc, ALU.mult, ALU.add)
                    ins.then_inc(S["vv_used"], 1)

            def finish(c, between):
                dve.wait_ge(S["vv_used"], (c + 2) * len(V_VEC))
                dve.wait_ge(S["v_used"], (c + 2) * len(V_PE))
                ch.link(V.tensor_tensor(vacc, bank(6, 2), vacc, ALU.add))
                dve.sem_inc(S["ffn_read"], 1)
                dve.sem_inc(S["ffn_ready"], 1)
                between()
                root(c + 1, 52, "ffn_sq", "ffn_var", "ffn_sd")
                ch.link(V.scalar_tensor_tensor(ff, vacc, small[:, 54:55], G2, ALU.mult, ALU.mult))
                ch.link(V.tensor_tensor(ff, ff, xm_cur, ALU.add))
                dve.sem_inc(S["out_ready"], 1)

            negmax(0, 0)
            for h in range(NQ):
                att_step(0, h)
            post(0, lambda upto: None)
            u_slots(0, 0, HEAD_START[1], hx_new)
            gates(0)
            move()
            with dve.Fori(0, NX - 1) as c:
                ch.enter(c, CHUNK_STEPS)
                done = [HEAD_START[1]]

                def fill(upto):
                    lo, hi = done[0], min(upto, 2 * SLOTS)
                    if hi <= lo:
                        return
                    u_slots(c, lo, min(hi, SLOTS), hx_cur)
                    if lo < SLOTS <= hi:
                        weights(c)
                    v_slots(c, max(lo - SLOTS, 0), hi - SLOTS)
                    done[0] = hi

                negmax(c + 1, 0)
                for h in range(NQ):
                    fill(HEADS_AT + PER_HEAD * h)
                    att_step(c + 1, h)
                post(c + 1, fill)
                fill(2 * SLOTS)
                u_slots(c + 1, 0, HEAD_START[0], hx_new)
                gates(c + 1)
                finish(c, lambda: u_slots(c + 1, *HEAD_START, hx_new))
                move()
            ch.leave(NX - 1)
            u_slots(NX - 1, HEAD_START[1], SLOTS, hx_cur)
            weights(NX - 1)
            v_slots(NX - 1, 0, SLOTS)
            finish(NX - 1, lambda: None)

        @block.tensor
        def _(pe):
            M = nc.tensor.matmul
            T = nc.tensor.transpose
            pe.wait_ge(S["consts_made"], 2)

            def mod_block(n):
                w = 2 if n < 4 else P
                wait(pe, "mod_out", n - 1)
                pe.wait_ge(S["wm_loaded%d" % (n % 2)], 16 * (n // 2 + 1))
                out = bank(n % 2)[0:w, :]
                M(out, lhsT=ones[0:1, 0:w], rhs=bmod[0:1, 512 * n:512 * n + 512], start=True, stop=False)
                for kt in range(KT):
                    lhs = sil2[:, kt, :] if n < 4 else silb[:, kt, :]
                    ins = M(out, lhsT=lhs, rhs=wm[:, n % 2, kt, :], start=False, stop=(kt == KT - 1))
                ins.then_inc(S["wm_used"], 1)

            pe.wait_ge(S["silu_ready"], 1)
            pe.wait_ge(S["bmod_loaded"], 16)
            for n in range(4):
                mod_block(n)
            pe.wait_ge(S["mod_out"], 4)
            for j in range(2 * KT):
                ins = T(bank(2)[:, 2 * j:2 * j + 2], rowm[0:2, j * P:(j + 1) * P], ident[0:2, 0:2])
            ins.then_inc(S["modT_ready"], 1)
            for n in range(4, 12):
                mod_block(n)
            pe.wait_ge(S["mod_out"], 12)
            pe.wait_ge(S["w_in_loaded"], 16)

            def pair(m, latent):
                pe.wait_ge(S["xn_ready"], m + 1)
                for tt in range(2):
                    for kt in range(KT):
                        ins = T(psum[:, tt * D + kt * P:tt * D + (kt + 1) * P], xp[:, tt, kt * P:(kt + 1) * P],
                                ident[:, :])
                ins.then_inc(S["xT_ready"], 1)
                pe.wait_ge(S["hT_vec"], m + 1)
                pe.wait_ge(S["hT_act"], m + 1)
                out_before = LF + 2 * LF * (m - 1)
                for tt in range(2):
                    n = 2 * m + tt
                    toks = slice(tt * P, tt * P + P)
                    wait(pe, "k_staged", n)
                    if latent:
                        if tt:
                            pe.wait_ge(S["q_staged"], n - 2)
                        for kt in range(KT):
                            M(bank(4), lhsT=hT[:, kt, toks], rhs=w_in[:, kt, 0:512], start=(kt == 0), stop=(kt == KT - 1))
                    for kt in range(KT):
                        ins = M(bank(5)[:, 0:256], lhsT=hT[:, kt, toks], rhs=w_in[:, kt, 512:768],
                                start=(kt == 0), stop=(kt == KT - 1))
                    ins.then_inc(S["qkv_ready"], 1)
                    if tt == 0 or latent:
                        for f in range(LF):
                            l = LF * tt + f
                            if latent:
                                pe.wait_ge(S["lz_out"], out_before + l - 1)
                            else:
                                wait(pe, "lz_out", l - 1)
                            o = QKV + D_LRU * tt + f * P
                            for kt in range(KT):
                                ins = M(bank(6 + f % 2)[:, 0:256], lhsT=w_in[:, kt, o:o + P], rhs=hT[:, kt, :],
                                        start=(kt == 0), stop=(kt == KT - 1))
                            ins.then_inc(S["z_ready" if tt else "lru_ready"], 1)
                    pe.wait_ge(S["rot_ready"], n + 1)
                    if latent:
                        for j in range(4):
                            T(bank(4)[:, j * P:(j + 1) * P], rot[:, j * P:(j + 1) * P], ident[:, :])
                    for j in range(2):
                        ins = T(bank(5)[:, j * P:(j + 1) * P], rot[:, 512 + j * P:512 + (j + 1) * P], ident[:, :])
                    ins.then_inc(S["qkT_ready"], 1)

            pair(0, False)
            with pe.Fori(1, NTOK // 2) as m:
                pair(m, True)

            pe.wait_ge(S["bd_loaded"], 16 * 8)
            pe.wait_ge(S["lz_out"], LF + 2 * LF * (NTOK // 2 - 1))
            for f in range(LF):
                pe.wait_ge(S["conv_done"], f + 1)
                for d in range(2):
                    k = 2 * f + d
                    wait(pe, "gates_out", 2 * k)
                    for g in range(2):
                        for o in range(0, LW, 512):
                            w = min(512, LW - o)
                            ins = M(psum[:, 1536 * g + o:1536 * g + o + w], lhsT=bd[:, (2 * d + g) * LF + f, :],
                                    rhs=cu[:, o:o + w], start=True, stop=True)
                    ins.then_inc(S["gates_ready"], 1)

            def scores(n, h):
                if h == 0:
                    pe.wait_ge(S["q_loaded"], 16 * n + 16)
                    wait(pe, "s_even", 2 * n)
                    wait(pe, "s_odd", 2 * n)
                wait(pe, "probs_ready", n * NQ + h)
                o = 64 * (h % 2)
                for b in range(0, KEYS, 512):
                    w = min(512, KEYS - b)
                    ins = M(psum[:, b:b + w], lhsT=qc[o:o + 64, h // 2, :], rhs=kT[o:o + 64, h // 4, b:b + w],
                            start=True, stop=True)
                ins.then_inc(S["scores_ready"], 1)

            def att_step(n, h):
                if h + 1 < NQ:
                    scores(n, h + 1)
                pe.wait_ge(S["probs_normed"], n * NQ + h + 1)
                for g in range(3):
                    l = 3 * h + g
                    wait(pe, "pt_out", n * ATT_T + l - 1)
                    for j in range(4 if g < 2 else 2):
                        kt = 4 * g + j
                        ins = T(bank(3 + l % 2)[:, j * P:(j + 1) * P], pr[:, kt * P:(kt + 1) * P], ident[:, :])
                    ins.then_inc(S["pt_ready"], 1)
                wait(pe, "att_ready", n * NQ + h - 1)
                for g in range(3):
                    l = 3 * h + g
                    pe.wait_ge(S["pt_out"], n * ATT_T + l + 1)
                    for kt in range(4 * g, 4 * g + (4 if g < 2 else 2)):
                        ins = M(bank(5)[0:64, 128 * (h % 2):128 * (h % 2) + 128],
                                lhsT=v[:, kt, 64 * (h // 4):64 * (h // 4) + 64], rhs=pT[:, kt, :],
                                start=(kt == 0), stop=(kt == NTOK - 1))
                ins.then_inc(S["pv_ready"], 1)

            def post(n, step, i):
                if step == "out":
                    if i == 0:
                        pe.wait_ge(S["att_ready"], n * NQ + NQ)
                        pe.wait_ge(S["l_loaded"], 16 * n + 16)
                    pe.wait_ge(S["wo_loaded"], 32 * n + 16 + 16 * i)
                    for kt in range(KT):
                        ins = M(bank(i), lhsT=att[:, kt, :] if kt < 4 else lc[:, kt - 4, :], rhs=wo[:, kt, :],
                                start=(kt == 0), stop=(kt == KT - 1))
                    ins.then_inc(S["out_half"], 1)
                elif step == "hxT":
                    pe.wait_ge(S["hx_ready"], n + 1)
                    for kt in range(KT):
                        ins = T(psum[:, 1536 + kt * P:1536 + (kt + 1) * P], hx_new[:, kt * P:(kt + 1) * P], ident[:, :])
                    ins.then_inc(S["hxT_ready"], 1)
                elif step == "q":
                    pe.wait_ge(S["hxT_even"], n + 1)
                    pe.wait_ge(S["hxT_odd"], n + 1)
                    pe.wait_ge(S["wq_loaded"], 16)
                    pe.wait_ge(S["sub_loaded"], 16)
                    for kt in range(KT):
                        ins = M(bank(i % 2), lhsT=hxT[:, kt, :], rhs=wq[:, kt, 512 * i:512 * i + 512],
                                start=(kt == 0), stop=(kt == KT - 1))
                    ins.then_inc(S["q_ready"], 1)
                elif step == "qT":
                    pe.wait_ge(S["q_out"], 4 * n + 2 * i + 2)
                    for j in range(8):
                        ins = T(psum[:, 1536 + j * P:1536 + (j + 1) * P], q_tok[:, j * P:(j + 1) * P], ident[:, :])
                    ins.then_inc(S["qT_ready"], 1)
                elif step == "s":
                    pe.wait_ge(S["qT_even"], 2 * n + i + 1)
                    pe.wait_ge(S["qT_odd"], 2 * n + i + 1)
                    if i:
                        pe.wait_ge(S["s_even"], 2 * n + i)
                        pe.wait_ge(S["s_odd"], 2 * n + i)
                    for j in range(8):
                        ins = M(bank(2 if j < 4 else 5)[:, (j % 4) * P:(j % 4 + 1) * P], lhsT=q_T[:, j, :],
                                rhs=skT[:, 8 * i + j, :], start=True, stop=True)
                    ins.then_inc(S["s_ready"], 1)

            def v_slots(c, lo, hi):
                if lo == 0:
                    pe.wait_ge(S["ffn_read"], c + 1)
                for j in range(lo, hi):
                    if j not in V_PE:
                        continue
                    r, k = j % RING, RANK[j]
                    pe.wait_ge(S["diag_ready"], c * len(V_PE) + k + 1)
                    pe.wait_ge(got[r], c * (16 * 2 * SLOTS // RING) + 16 * (SLOTS // RING + j // RING + 1))
                    for b in range(2):
                        ins = M(bank(6 + b), lhsT=diag[:, k % DIAGS, :], rhs=ring[:, r, 512 * b:512 * b + 512],
                                start=(k == 0), stop=(k == len(V_PE) - 1))
                    ins.then_inc(S["v_used"], 1)

            scores(0, 0)
            for h in range(NQ):
                att_step(0, h)
            for step in AFTER:
                post(0, *step)
            with pe.Fori(0, NX - 1) as c:
                scores(c + 1, 0)
                for h in range(NQ):
                    att_step(c + 1, h)
                for step in AFTER:
                    post(c + 1, *step)
                v_slots(c, 0, SLOTS)
            v_slots(NX - 1, 0, SLOTS)


def _rope_tables():
    f = np.float32
    nf = HD // 4
    inv = f(10000.0) ** (-np.arange(nf, dtype=f) / f(nf))
    pos = np.arange(SEQ)
    ang = np.stack([(pos // GRID_W).astype(f)[:, None] * inv, (pos % GRID_W).astype(f)[:, None] * inv], 1)
    cos, sin = np.cos(ang), np.sin(ang)
    cos = np.stack([cos, cos], 2).reshape(SEQ, HD)
    sin = np.stack([-sin, sin], 2).reshape(SEQ, HD)
    cos = np.concatenate([np.ones((CTX, HD), f), cos])
    sin = np.concatenate([np.zeros((CTX, HD), f), sin])
    return [np.ascontiguousarray(a.reshape(NTOK, P, HD).transpose(1, 0, 2).astype(f)) for a in (cos, sin)]


def kernel(**inputs):
    import concourse.bacc as bacc
    from concourse.bass_utils import run_bass_kernel_spmd as run

    one = {n: np.ascontiguousarray(np.asarray(a)) for n, a in inputs.items()}
    cos, sin = _rope_tables()

    def cols(a):
        return np.moveaxis(a.reshape(a.shape[:-1] + (-1, P)), -1, 0)

    arrays = {
        "xin": np.concatenate([one["ctx"][0], one["x"][0]]).reshape(NTOK, P, D),
        "c": one["c"].reshape(D), "c_ctx": one["c_ctx"], "w_mod": one["w_mod"][0], "b_mod": one["b_mod"],
        "g_pre_mix": cols(one["g_pre_mix"][0]), "g_post_mix": one["g_post_mix"], "g_pre_ffn": one["g_pre_ffn"],
        "g_post_ffn": one["g_post_ffn"], "w_in": one["w_in"][0], "q_norm_g": one["q_norm_g"],
        "k_norm_g": one["k_norm_g"], 
        "conv_w": cols(one["conv_w"][0]).transpose(0, 2, 1), "conv_b": cols(one["conv_b"][0]),
        "lru_bias": np.stack([cols(one["rg_ba"][0]), cols(one["rg_bi"][0])], 2),
        "rg_lambda": cols(one["rg_lambda"][0]), "rg_wa": one["rg_wa"][0], "rg_wi": one["rg_wi"][0], "w_out": one["w_out"][0], "wq": one["peer_wq"][0],
        "subkeys": one["peer_subkeys"].reshape(2 * PH, NK, DK).transpose(2, 0, 1), "u": one["peer_u"][0], "v": one["peer_v"][0],
        "cos": cos, "sin": sin,
    }
    arrays = {n: np.ascontiguousarray(a) for n, a in arrays.items()}
    nc = bacc.Bacc("TRN2", target_bir_lowering=False, num_devices=1)
    t = {n: nc.dram_tensor("in_" + n, a.shape, F32, kind="ExternalInput").ap() for n, a in arrays.items()}
    t["out"] = nc.dram_tensor("out", (NX, P, D), F32, kind="ExternalOutput").ap()
    nc.disable_value_cache = True
    layer(nc, t)
    r = run(nc, [{"in_" + n: a for n, a in arrays.items()}], core_ids=[0])
    return r.results[0]["out"].reshape(1, SEQ, D)
```

```python
from contextlib import ExitStack

import numpy as np

import concourse.bass as bass
from concourse import mybir

ALU = mybir.AluOpType
ACT = mybir.ActivationFunctionType
AX = mybir.AxisListType.X
F32 = mybir.dt.float32
U32 = mybir.dt.uint32

P = 128
D = 1024
KT = D // P
SEQ, CTX = 1024, 256
GRID_W = 64
NX, NC_ = SEQ // P, CTX // P
NTOK = NX + NC_
HD = 64
NQ, NKV = 8, 2
D_ATTN = NQ * HD
D_KV = NKV * HD
D_LRU = 512
LF = D_LRU // P
D_IN = D_ATTN + 2 * D_KV + 2 * D_LRU
QKV = D_ATTN + 2 * D_KV
CONV_W, PADL = 4, 2
GAP = 3
XLW = PADL + CTX + GAP + SEQ + 1
LW = CTX + GAP + SEQ
RG_C = 8.0
KEYS = CTX + SEQ
PH, NK, DK = 8, 128, 128
TOPK = 16
SLOTS = PH * TOPK
HALF_SLOTS = SLOTS // 2
RING = 8
DIAGS = 4
EPS = 1e-6
NEG = -3.0e38
GELU_C, GELU_K = 0.044715, 0.7978845608028654
ATT_T = 3 * NQ
AFTER = (("out", 0), ("out", 1), ("rows", 0), ("rows", 1), ("hxT", 0), ("q", 0), ("q", 1), ("qT", 0), ("s", 0),
         ("q", 2), ("q", 3), ("qT", 1), ("s", 1))
HEADS_AT, PER_HEAD = 11, 7
MIX_AT, XM_AT, HXT_AT, QT_AT, SIM_AT = 85, 88, 94, (109, 127), (112, SLOTS + 46)
TOP_AT = (SLOTS + 4, SLOTS + 49)
TOP_EVERY = 8
LAST_SIM = 44
HEAD_START = (5, 7)
V_VEC = [j for j in range(SLOTS) if j % 2 == 1]
V_PE = [j for j in range(SLOTS) if j not in V_VEC]
RANK = {j: i for part in (V_VEC, V_PE) for i, j in enumerate(part)}
assert len(V_PE) % DIAGS == 0
PAIR_STEPS = 31
CHUNK_STEPS = 185


class Chain:

    def __init__(self, eng, sem):
        self.eng, self.sem, self.base, self.k = eng, sem, 0, 0

    def step(self, ins):
        self.k += 1
        return ins.then_inc(self.sem, 1)

    def sync(self):
        self.eng.wait_ge(self.sem, self.base + self.k)

    def link(self, ins):
        self.step(ins)
        self.sync()

    def link_alone(self, ins, passed):
        self.link(ins)
        self.eng.sem_inc(passed, 1)

    def enter(self, i, per):
        self.start = self.base + self.k
        self.per = per
        self.base, self.k = self.start + i * per, 0

    def leave(self, count):
        assert self.k == self.per, (self.k, self.per)
        self.base, self.k = self.start + count * self.per, 0


def layer(nc, t):
    with ExitStack() as ctx:
        def sb(name, shape, dt=F32):
            return ctx.enter_context(nc.sbuf_tensor(name, shape, dt))

        def sem(name):
            return ctx.enter_context(nc.semaphore(name))

        ident = sb("ident", [P, P])
        wbig = sb("wbig", [P, KT * 2048])
        w_in = wbig[:, 0:KT * D_IN].rearrange("p (t n) -> p t n", t=KT)
        wq = wbig[:, :].rearrange("p (t n) -> p t n", t=KT)
        skT = sb("skT", [P, 2 * PH, NK])
        kT = sb("kT", [P, NKV, KEYS])
        v = sb("v", [P, NTOK, D_KV])
        rows = sb("rows", [P, D])
        G1, A2, B2, G2 = (32 * i for i in range(4))
        modc = sb("modc", [P, 4, KT])
        gcol = sb("gcol", [P, KT])
        iota16 = sb("iota16", [P, TOPK])
        small = sb("small", [P, 64])
        convw = sb("convw", [P, LF, CONV_W])
        convb = sb("convb", [P, LF])
        lrub = sb("lrub", [P, 2, 2, LF])
        lam = sb("lam", [P, 2, LF])
        lt = sb("lt", [P, 5, 2 * LF])
        lruk = sb("lruk", [P, 2 * LF])
        ARENA = 28752
        arena = sb("arena", [P, ARENA])

        at = [0]

        def view(n, *dims):
            assert at[0] + n <= ARENA, at[0] + n
            a = arena[:, at[0]:at[0] + n]
            at[0] += n
            if dims:
                names = "abcd"[:len(dims)]
                a = a.rearrange("p (%s) -> p %s" % (" ".join(names), " ".join(names)),
                                **dict(zip(names, dims)))
            return a

        XL = view(LF * XLW, LF, XLW)
        Z = view(LF * SEQ, LF, SEQ)
        lru_at = at[0]
        xp = view(2 * D, 2, D)
        hT = view(KT * 2 * P, KT, 2 * P)
        cosr = view(NTOK * HD, NTOK, HD)
        sinr = view(NTOK * HD, NTOK, HD)
        tabs = view(4 * NTOK * HD, 4, NTOK, HD)
        gq = view(2 * HD, 2, HD)
        early_at = at[0]
        qk = view(640)
        rot = view(768)
        swp = view(640)
        qst = view(4 * P)
        junk = view(D)
        rowm = view(2 * D)
        at[0] = lru_at
        cu = view(LW)
        tr, ti, av, bv = (view(2 * LW, 2, LW) for _ in range(4))
        hf = view(LW)
        hb = view(LW)
        bd = view(16 * P, 16, P)
        ones = view(P)
        csil = view(2 * KT, 2, KT)
        at[0] = 0
        wm = view(2 * 4096, 2, KT, 512)
        at[0] = early_at
        bmod = view(2 * D)
        ccol = view(2 * KT, 2, KT)
        sil2 = view(2 * KT, KT, 2)
        wml = wbig[:, 0:3 * 4096].rearrange("p (i t n) -> p i t n", i=3, t=KT)
        bmodl = wbig[:, 3 * 4096:3 * 4096 + 3 * 512].rearrange("p (i n) -> p i n", i=3)
        silb = wbig[:, 4 * 4096 - KT * P:4 * 4096].rearrange("p (t n) -> p t n", t=KT)
        at[0] = 0
        ring = view(RING * D, RING, D)
        wo = view(KT * D, KT, D)
        pr = view(KEYS)
        pT = view(KEYS, NTOK, P)
        qc = view(4 * P, 4, P)
        lc = view(4 * P, 4, P)
        att = view(4 * P, 4, P)
        xm_new, xm_cur, hx_new, hx_cur = (view(D) for _ in range(4))
        mix = pr[:, 0:D]
        sq = pT.rearrange("p t n -> p (t n)")[:, 0:D]
        hxT = view(KT * P, KT, P)
        sc = view(8 * NK, 8, NK)
        diag = view(DIAGS * P, DIAGS, P)
        ff = hxT.rearrange("p t n -> p (t n)")
        act_, gx, wt, gate, top = (view(SLOTS) for _ in range(5))
        idxf = gx
        vacc = hx_cur
        cand = view(TOPK * TOPK)
        cnd2 = view(TOPK * TOPK)
        tv = view(2 * TOPK, 2, TOPK)
        pabu = cand[:, 0:P].bitcast(U32).rearrange("p (a h k) -> p a h k", a=2, h=4)
        selv = cand[:, P:2 * P].rearrange("p (a h k) -> p a h k", a=2, h=4)
        q_tok = pr[:, 0:D]
        q_T = pT[:, 0:8, :]
        oneh = mix.rearrange("p (h k a) -> p h k a", h=4, k=TOPK)
        ixu = sb("ixu", [P, PH, 2, TOPK], U32)
        posu = sb("posu", [P, PH, TOPK], U32)
        idx_new = sb("idx_new", [P, SLOTS], U32)
        idx_u = sb("idx_u", [P, SLOTS], U32)
        idx_v = sb("idx_v", [P, SLOTS], U32)

        psum = ctx.enter_context(nc.psum_tensor("psum", [P, 8 * 512], F32))

        def bank(b, n=1):
            return psum[:, 512 * b:512 * (b + n)]

        q_scr = nc.dram_tensor("q_scr", (NX, P, 4 * P), F32, kind="Internal").ap()
        l_scr = nc.dram_tensor("l_scr", (LF, P, SEQ), F32, kind="Internal").ap()

        S = {n: sem(n) for n in (
            "consts_made", "vec_chain", "act_chain", "pool_chain", "c_loaded", "bmod_loaded", "gains_loaded",
            "wm_loaded0", "wm_loaded1", "wml_loaded0", "wml_loaded1", "wml_loaded2", "wm_used", "sub_loaded",
            "silu_ready", "silb_ready", "tanh_c", "g1_ready", "a2_ready", "b2_ready", "g2_ready", "mod_out",
            "modT_ready", "row_out", "modc_ready", "w_in_loaded", "w_in_rest", "x_loaded", "x_sq", "x_var",
            "x_sd", "xn_ready", "xT_first", "xT_ready", "hT_vec", "hT_act", "qkv_ready", "lru_ready", "z_ready",
            "lz_out", "qk_sq", "qk_var", "qk_sd", "rot_ready", "qkT_ready", "q_staged", "q_free", "q_opened",
            "ff_free", "sc_used", "k_staged", "q_stored", "tab_loaded", "lruw_loaded", "bd_zeroed", "bd_loaded",
            "conv_done", "gates_ready", "gates_out", "lru_a", "lru_m", "lru_s", "lru_used", "lru_out",
            "lru_stored", "z_tanh", "z_in", "lam_abs", "lam_exp", "lruk_ready", "wq_loaded", "wo_loaded",
            "q_loaded", "l_loaded", "xc_loaded", "scores_ready", "negmax_ready", "probs_ready", "probs_normed",
            "pt_ready", "pt_out", "pv_ready", "att_ready", "out_half", "mix_sq", "mix_var", "mix_sd",
            "xm_ready", "xm_sq", "xm_var", "xm_sd", "hx_ready", "hxT_ready", "hxT_even", "hxT_odd", "q_ready",
            "q_out", "qT_ready", "qT_even", "qT_odd", "s_ready", "s_even", "s_odd", "gate_in", "gate_exp",
            "top_passed", "idx_ready", "xm_moved", "idx_taken", "u_opened", "v_opened", "u_used", "v_used",
            "vv_used", "gelu_in", "gelu_tanh", "w_ready", "diag_ready", "ffn_ready", "ffn_sq", "ffn_var",
            "ffn_sd", "ffn_read", "out_ready", "out_stored")}
        got = [sem(f"got{r}") for r in range(RING)]

        block = ctx.enter_context(nc.Block())

        @block.sync
        def _(sp):
            for i, name in enumerate(("c", "c_ctx")):
                sp.dma_start(ccol[:, i, :], t[name].rearrange("(p t) -> p t", p=P)).then_inc(S["c_loaded"], 16)
            sp.dma_start(bmod[0:1, :], t["b_mod"][:, 0:2 * D]).then_inc(S["bmod_loaded"], 16)
            wmv = t["w_mod"].rearrange("(p t) n -> p t n", p=P)
            for n in range(4):
                if n >= 2:
                    sp.wait_ge(S["wm_used"], n - 1)
                sp.dma_start(wm[:, n % 2, :, :], wmv[:, :, 512 * n:512 * n + 512])\
                    .then_inc(S["wm_loaded%d" % (n % 2)], 16)
                if n == 0:
                    sp.dma_start(xp, t["xin"][0:2].rearrange("t p d -> p t d")).then_inc(S["x_loaded"], 16)
                if n == 1:
                    sp.dma_start(gcol[:, :], t["g_pre_mix"]).then_inc(S["gains_loaded"], 16)
                    sp.dma_start(cosr, t["cos"]).then_inc(S["tab_loaded"], 16)
                    sp.dma_start(sinr, t["sin"]).then_inc(S["tab_loaded"], 16)
                    for i, name in enumerate(("q_norm_g", "k_norm_g")):
                        sp.dma_start(gq[:, i, :], t[name].broadcast_to([P, HD])).then_inc(S["tab_loaded"], 16)
            w_inv = t["w_in"].rearrange("(t p) n -> p t n", p=P)
            for lo, hi in ((D_ATTN, QKV + D_LRU), (0, D_ATTN), (QKV + D_LRU, D_IN)):
                sp.dma_start(w_in[:, :, lo:hi], w_inv[:, :, lo:hi])\
                    .then_inc(S["w_in_loaded" if lo == D_ATTN else "w_in_rest"], 16)
            for dst, name in ((lrub, "lru_bias"), (lam, "rg_lambda"), (convw, "conv_w"), (convb, "conv_b")):
                sp.dma_start(dst[:], t[name]).then_inc(S["lruw_loaded"], 16)
            for g, name in ((G1, "g_post_mix"), (A2, "g_pre_ffn"), (G2, "g_post_ffn")):
                sp.dma_start(rows[g:g + 1, :], t[name]).then_inc(S["gains_loaded"], 16)
            sp.dma_start(skT[:], t["subkeys"]).then_inc(S["sub_loaded"], 16)
            sp.wait_ge(S["bd_zeroed"], 2)
            for d in range(2):
                for g, w in enumerate(("rg_wa", "rg_wi")):
                    for b in range(2):
                        j = (2 * d + g) * LF
                        sp.dma_start(bd[64 * b:64 * b + 64, j:j + LF, 64 * b:64 * b + 64],
                                     t[w][d, b::2].rearrange("f i j -> i f j")).then_inc(S["bd_loaded"], 16)
            with sp.Fori(1, NTOK // 2) as m:
                sp.wait_ge(S["xT_ready"], m)
                sp.dma_start(xp, t["xin"][bass.ds(m * 2, 2)].rearrange("t p d -> p t d"))\
                    .then_inc(S["x_loaded"], 16)
            sp.wait_ge(S["qkv_ready"], NTOK)
            sp.wait_ge(S["lru_ready"], LF * NTOK // 2)
            sp.wait_ge(S["z_ready"], LF * NX // 2)

            def late_block(n):
                if n >= 7:
                    sp.wait_ge(S["wm_used"], n - 2)
                sp.dma_start(wml[:, n % 3, :, :], wmv[:, :, 512 * n:512 * n + 512])\
                    .then_inc(S["wml_loaded%d" % (n % 3)], 16)
                sp.dma_start(bmodl[0:1, n % 3, :], t["b_mod"][:, 512 * n:512 * n + 512])\
                    .then_inc(S["wml_loaded%d" % (n % 3)], 16)

            for n in range(4, 9):
                late_block(n)
            for f in range(LF):
                sp.wait_ge(S["lru_out"], f + 1)
                sp.dma_start(l_scr[f], hf[:, CTX + GAP:LW]).then_inc(S["lru_stored"], 16)
                for n in ((9, 10), (11,), (), ())[f]:
                    late_block(n)

            def load_front(n, first):
                if not first:
                    sp.wait_ge(S["scores_ready"], NQ * n)
                sp.dma_start(qc, q_scr[bass.ds(n, 1)].rearrange("o p (j c) -> (o p) j c", j=4))\
                    .then_inc(S["q_loaded"], 16)
                if not first:
                    sp.wait_ge(S["out_half"], 2 * n)
                sp.dma_start(lc, l_scr[:, :, bass.ds(n * P, P)].rearrange("f p c -> p f c"))\
                    .then_inc(S["l_loaded"], 16)

            def load_x(n, first):
                if not first:
                    sp.wait_ge(S["xm_moved"], n)
                sp.dma_start(xm_new, t["xin"][bass.ds(n + NC_, 1)].rearrange("o p d -> (o p) d"))\
                    .then_inc(S["xc_loaded"], 16)

            def store(c):
                sp.wait_ge(S["out_ready"], c + 1)
                sp.dma_start(t["out"][bass.ds(c, 1)].rearrange("o p d -> (o p) d"), ff)\
                    .then_inc(S["out_stored"], 16)
                sp.wait_ge(S["out_stored"], 16 * c + 16)
                sp.sem_inc(S["ff_free"], 1)

            sp.sem_inc(S["ff_free"], 1)
            sp.wait_ge(S["q_stored"], 16 * NX)
            sp.wait_ge(S["lru_stored"], 16 * LF)
            load_front(0, True)
            sp.dma_start(wo, t["w_out"].rearrange("(t p) n -> p t n", p=P)).then_inc(S["wo_loaded"], 16)
            sp.wait_ge(S["wm_used"], 12)
            sp.dma_start(wq, t["wq"].rearrange("(t p) n -> p t n", p=P)).then_inc(S["wq_loaded"], 16)
            load_x(0, True)
            load_front(1, False)
            with sp.Fori(1, NX - 1) as n:
                load_x(n, False)
                load_front(n + 1, False)
                store(n - 1)
            load_x(NX - 1, False)
            store(NX - 2)
            store(NX - 1)
            sp.wait_ge(S["out_stored"], 16 * NX)
            sp.wait_ge(S["q_stored"], 16 * NX)
            sp.wait_ge(S["lru_stored"], 16 * LF)

        @block.gpsimd
        def _(pool):
            ch = Chain(pool, S["pool_chain"])
            ch.link(nc.gpsimd.memset(ident[:, :], 0.0))
            ch.link(nc.gpsimd.affine_select(out=ident[:, :], in_=ident[:, :], compare_op=ALU.not_equal, fill=1.0,
                                            base=0, pattern=[[-1, P]], channel_multiplier=1))
            nc.gpsimd.memset(ones, 1.0).then_inc(S["consts_made"], 1)
            nc.gpsimd.iota(iota16[:, :], pattern=[[1, TOPK]], base=0, channel_multiplier=0,
                           allow_small_or_imprecise_dtypes=True).then_inc(S["consts_made"], 1)
            pool.wait_ge(S["modc_ready"], 1)
            pool.wait_ge(S["wm_used"], 4)
            nc.gpsimd.memset(XL, 0.0).then_inc(S["bd_zeroed"], 1)
            nc.gpsimd.memset(bd, 0.0).then_inc(S["bd_zeroed"], 1)

            pool.sem_inc(S["q_free"], 1)
            with pool.Fori(0, NX) as x:
                pool.wait_ge(S["q_staged"], x + 1)
                pool.sem_inc(S["q_opened"], 1)
                pool.dma_start(q_scr[bass.ds(x, 1)].rearrange("o p n -> (o p) n"), qst)\
                    .then_inc(S["q_stored"], 16)
                pool.wait_ge(S["q_stored"], 16 * x + 16)
                pool.sem_inc(S["q_free"], 1)

            pool.sem_inc(S["v_used"], len(V_PE))
            pool.sem_inc(S["vv_used"], len(V_VEC))

            def v_free(c, j):
                if j in V_VEC:
                    pool.wait_ge(S["vv_used"], c * len(V_VEC) + RANK[j] + 1)
                else:
                    pool.wait_ge(S["v_used"], c * len(V_PE) + RANK[j] + 1)
            pool.wait_ge(S["lru_stored"], 16 * LF)
            pool.wait_ge(S["q_stored"], 16 * NX)

            def gather(table, idx, j, r):
                pool.indirect_dma_start(ring[:, r, :], None, t[table],
                                        bass.IndirectOffsetOnAxis(idx[:, j:j + 1], 0)).then_inc(got[r], 16)

            with pool.Fori(0, NX) as c:
                ch.enter(c, 3)
                for j in range(SLOTS):
                    if j % HALF_SLOTS == 0:
                        i = j // HALF_SLOTS
                        pool.wait_ge(S["idx_ready"], 2 * c + i + 1)
                        pool.sem_inc(S["u_opened"], 1)
                        half = slice(j, j + HALF_SLOTS)
                        ch.link(nc.gpsimd.tensor_copy(idx_u[:, half], idx_new[:, half]))
                        pool.sem_inc(S["idx_taken"], 1)
                    if j < RING:
                        v_free(c, SLOTS - RING + j)
                    else:
                        pool.wait_ge(S["u_used"], c * SLOTS + j - RING + 1)
                    pool.sem_inc(S["u_opened"], 1)
                    gather("u", idx_u, j, j % RING)
                v_free(c, V_PE[-1])
                pool.sem_inc(S["v_opened"], 1)
                v_free(c, V_VEC[-1])
                pool.sem_inc(S["v_opened"], 1)
                ch.link(nc.gpsimd.tensor_copy(idx_v[:, :], idx_u[:, :]))
                for j in range(SLOTS):
                    if j < RING:
                        pool.wait_ge(S["u_used"], c * SLOTS + SLOTS - RING + j + 1)
                    else:
                        v_free(c + 1, j - RING)
                    pool.sem_inc(S["v_opened"], 1)
                    gather("v", idx_v, j, j % RING)
            ch.leave(NX)

        def wait(eng, name, val):
            if isinstance(val, int) and val <= 0:
                return
            eng.wait_ge(S[name], val)

        @block.scalar
        def _(act):
            ch = Chain(act, S["act_chain"])
            A = nc.scalar.activation
            act.wait_ge(S["c_loaded"], 32)
            A(csil, ccol, ACT.Tanh, scale=0.5).then_inc(S["tanh_c"], 1)

            def x_norm(m):
                act.wait_ge(S["x_loaded"], 16 * m + 16)
                ch.link(A(junk, xp[:, 0, :], ACT.Square, accum_out=small[:, 0:1]))
                A(junk, xp[:, 1, :], ACT.Square, accum_out=small[:, 1:2]).then_inc(S["x_sq"], 1)
                act.wait_ge(S["x_var"], m + 1)
                A(small[:, 2:4], small[:, 2:4], ACT.Sqrt).then_inc(S["x_sd"], 1)

            def x_mod(m, latent):
                sc_, sh_ = (0, 1) if latent else (2, 3)
                act.wait_ge(S["xT_ready"], m + 1)
                for kt in range(KT):
                    ins = A(hT[:, kt, P:2 * P], psum[:, D + kt * P:D + (kt + 1) * P], ACT.Identity,
                            scale=modc[:, sc_, kt:kt + 1], bias=modc[:, sh_, kt:kt + 1])
                ins.then_inc(S["hT_act"], 1)

            def pair(m, latent, more):
                lo = 0 if latent else D_ATTN
                for tt in range(2):
                    n = 2 * m + tt
                    act.wait_ge(S["qkv_ready"], n + 1)
                    wait(act, "rot_ready", n)
                    A(swp[:, lo:640], psum[:, 2048 + lo:2048 + 640], ACT.Square).then_inc(S["qk_sq"], 1)
                    act.wait_ge(S["qk_var"], n + 1)
                    A(small[:, 16 + lo // HD:26], small[:, 16 + lo // HD:26], ACT.Sqrt).then_inc(S["qk_sd"], 1)
                    if tt == 0 or latent:
                        for f in range(LF):
                            if tt == 0:
                                act.wait_ge(S["lru_ready"], LF * m + f + 1)
                                dst = XL[:, f, bass.ds(m * 256 + (PADL + GAP), 256)] if latent \
                                    else XL[:, f, PADL:PADL + CTX]
                            else:
                                act.wait_ge(S["z_ready"], LF * m - LF + f + 1)
                                dst = Z[:, f, bass.ds(m * 256 - 256, 256)]
                            A(dst, bank(6 + f % 2)[:, 0:256], ACT.Copy).then_inc(S["lz_out"], 1)
                    if latent:
                        act.wait_ge(S["qkT_ready"], n + 1)
                        act.wait_ge(S["q_free"], n - 1)
                        A(qst, bank(4), ACT.Copy).then_inc(S["q_staged"], 1)
                    if tt == 0 and more:
                        x_norm(m + 1)
                if more:
                    x_mod(m + 1, True)

            x_norm(0)
            act.wait_ge(S["modc_ready"], 1)
            act.wait_ge(S["wm_used"], 4)
            act.wait_ge(S["bd_zeroed"], 2)
            x_mod(0, False)
            pair(0, False, True)
            with act.Fori(1, NTOK // 2 - 1) as m:
                ch.enter(m - 1, 1)
                pair(m, True, True)
            ch.leave(NTOK // 2 - 2)
            pair(NTOK // 2 - 1, True, False)

            act.wait_ge(S["lam_abs"], 1)
            A(lt[:, 1, :], lt[:, 0, :], ACT.Exp, scale=-1.0).then_inc(S["lam_exp"], 1)
            act.wait_ge(S["lruk_ready"], 1)

            def lru_gates(k):
                f, d = k // 2, k % 2
                act.wait_ge(S["gates_ready"], k + 1)
                wait(act, "lru_used", k - 1)
                kcol = lruk[:, LF * d + f:LF * d + f + 1]
                A(tr[:, d], psum[:, 0:LW], ACT.Tanh, scale=0.5, bias=lrub[:, d, 0, f:f + 1])\
                    .then_inc(S["gates_out"], 1)
                A(ti[:, d], psum[:, 1536:1536 + LW], ACT.Tanh, scale=0.5, bias=lrub[:, d, 1, f:f + 1])\
                    .then_inc(S["gates_out"], 1)
                act.wait_ge(S["gates_out"], 2 * k + 2)
                ch.link(A(av[:, d], tr[:, d], ACT.Exp, scale=kcol, bias=kcol))
                A(tr[:, d], tr[:, d], ACT.Tanh, scale=kcol, bias=kcol).then_inc(S["lru_a"], 1)

            act.wait_ge(S["q_stored"], 16 * NX)
            lru_gates(0)
            lru_gates(1)
            for f in range(LF):
                for d in range(2):
                    act.wait_ge(S["lru_m"], 2 * f + d + 1)
                    A(bv[:, d], bv[:, d], ACT.Sqrt, scale=0.25).then_inc(S["lru_s"], 1)
                if f + 1 < LF:
                    lru_gates(2 * f + 2)
                act.wait_ge(S["z_in"], f + 1)
                A(tr[:, 1, 0:SEQ], tr[:, 1, 0:SEQ], ACT.Tanh, scale=GELU_K).then_inc(S["z_tanh"], 1)
                if f + 1 < LF:
                    lru_gates(2 * f + 3)

            def probs(n, h):
                a, b = 44 + h % 2, 46 + h % 2
                act.wait_ge(S["negmax_ready"], n * NQ + h + 1)
                wait(act, "pt_ready", n * ATT_T + 3 * h)
                A(pr, psum[:, 0:KEYS], ACT.Exp, scale=HD ** -0.5, bias=small[:, a:a + 1],
                  accum_out=small[:, b:b + 1]).then_inc(S["probs_ready"], 1)

            def att_step(n, h):
                for g in range(3):
                    k = 4 if g < 2 else 2
                    act.wait_ge(S["pt_ready"], n * ATT_T + 3 * h + g + 1)
                    A(pT[:, 4 * g:4 * g + k, :], bank(3 + (3 * h + g) % 2)[:, 0:k * P], ACT.Copy)\
                        .then_inc(S["pt_out"], 1)
                if h + 1 < NQ:
                    probs(n, h + 1)
                act.wait_ge(S["pv_ready"], n * NQ + h + 1)
                o = 64 * (h % 2)
                A(att[o:o + 64, h // 2, :], bank(5)[0:64, 128 * (h % 2):128 * (h % 2) + 128], ACT.Copy)\
                    .then_inc(S["att_ready"], 1)

            def post(n, step, i):
                if (step, i) == ("out", 1):
                    act.wait_ge(S["out_half"], 2 * n + 2)
                    wait(act, "idx_ready", 2 * n)
                    A(sq, psum[:, 0:D], ACT.Square, accum_out=small[:, 48:49]).then_inc(S["mix_sq"], 1)
                    A(mix, psum[:, 0:D], ACT.Copy)
                    act.wait_ge(S["mix_var"], n + 1)
                    A(small[:, 49:50], small[:, 49:50], ACT.Sqrt).then_inc(S["mix_sd"], 1)
                    act.wait_ge(S["xm_ready"], n + 1)
                    A(sq, xm_new, ACT.Square, accum_out=small[:, 48:49]).then_inc(S["xm_sq"], 1)
                    act.wait_ge(S["xm_var"], n + 1)
                    A(small[:, 49:50], small[:, 49:50], ACT.Sqrt).then_inc(S["xm_sd"], 1)
                elif step == "hxT":
                    act.wait_ge(S["hxT_ready"], n + 1)
                    wait(act, "ff_free", n)
                    A(hxT[:, 4:8, :], bank(4), ACT.Copy).then_inc(S["hxT_odd"], 1)
                elif step == "q":
                    act.wait_ge(S["q_ready"], 4 * n + i + 1)
                    A(q_tok[:, 512 * (i % 2):512 * (i % 2) + 512], bank(i % 2), ACT.Copy).then_inc(S["q_out"], 1)
                elif step == "qT":
                    act.wait_ge(S["qT_ready"], 2 * n + i + 1)
                    A(q_T[:, 4:8, :], bank(4), ACT.Copy).then_inc(S["qT_odd"], 1)
                elif step == "s":
                    act.wait_ge(S["s_ready"], 2 * n + i + 1)
                    wait(act, "sc_used", 2 * n + i)
                    A(sc[:, 4:8, :], bank(5), ACT.Copy).then_inc(S["s_odd"], 1)

            def diags(c, lo, hi):
                if lo == 0:
                    act.wait_ge(S["w_ready"], c + 1)
                for j in range(lo, min(hi, SLOTS)):
                    if j in V_PE:
                        k = RANK[j]
                        act.wait_ge(S["v_used"], (c + 1) * len(V_PE) + k + 1 - DIAGS)
                        A(diag[:, k % DIAGS, :], ident[:, :], ACT.Copy, scale=wt[:, j:j + 1])\
                            .then_inc(S["diag_ready"], 1)

            def gates(n):
                act.wait_ge(S["gate_in"], n + 1)
                A(gate, gate, ACT.Exp).then_inc(S["gate_exp"], 1)

            def finish(c):
                act.wait_ge(S["ffn_ready"], c + 1)
                act.wait_ge(S["ff_free"], c + 1)
                A(ff, vacc, ACT.Square, accum_out=small[:, 52:53]).then_inc(S["ffn_sq"], 1)
                act.wait_ge(S["ffn_var"], c + 1)
                A(small[:, 53:54], small[:, 53:54], ACT.Sqrt).then_inc(S["ffn_sd"], 1)

            def gelu(c):
                act.wait_ge(S["gelu_in"], c + 1)
                A(gx, gx, ACT.Tanh, scale=GELU_K).then_inc(S["gelu_tanh"], 1)

            probs(0, 0)
            for h in range(NQ):
                att_step(0, h)
            for step in AFTER:
                post(0, *step)
            gates(0)
            with act.Fori(0, NX - 1) as c:
                probs(c + 1, 0)
                for h in range(NQ):
                    att_step(c + 1, h)
                for step in AFTER[:-1]:
                    post(c + 1, *step)
                gelu(c)
                ahead = V_PE[RANK[next(j for j in V_PE if j >= LAST_SIM)] + DIAGS]
                diags(c, 0, ahead)
                post(c + 1, *AFTER[-1])
                diags(c, ahead, SLOTS)
                gates(c + 1)
                finish(c)
            gelu(NX - 1)
            diags(NX - 1, 0, SLOTS)
            finish(NX - 1)

        @block.vector
        def _(dve):
            ch = Chain(dve, S["vec_chain"])
            V = nc.vector

            dve.sem_inc(S["ffn_read"], 1)
            dve.wait_ge(S["tanh_c"], 1)
            dve.wait_ge(S["consts_made"], 2)
            ch.link(V.scalar_tensor_tensor(csil, csil, 1.0, ccol, ALU.add, ALU.mult))
            ch.link(V.tensor_scalar(csil, csil, 0.5, None, ALU.mult))
            ch.link(V.tensor_copy(sil2, csil.rearrange("p i t -> p t i")))
            dve.sem_inc(S["silu_ready"], 1)

            def mod_row(n):
                dve.wait_ge(S["wm_used"], n + 1)
                src, at_ = bank(6 + n % 2), slice(512 * (n % 2), 512 * (n % 2) + 512)
                r = (G1, B2, A2, G2)[n // 2 - 2]
                src, dst = src[r:r + 1, :], rows[r:r + 1, at_]
                if r == B2:
                    ins = V.tensor_copy(dst, src)
                elif r == A2:
                    ins = V.scalar_tensor_tensor(dst, src, 1.0, dst, ALU.add, ALU.mult)
                else:
                    ins = V.tensor_tensor(dst, src, dst, ALU.mult)
                ins.then_inc(S["mod_out"], 1)

            def x_norm(m):
                dve.wait_ge(S["x_sq"], m + 1)
                ch.step(V.tensor_scalar(small[:, 2:4], small[:, 0:2], 1.0 / D, EPS, ALU.mult, ALU.add))
                ch.sync()
                dve.sem_inc(S["x_var"], 1)
                dve.wait_ge(S["x_sd"], m + 1)
                ch.link(V.reciprocal(small[:, 4:6], small[:, 2:4]))
                ch.step(V.tensor_scalar(xp[:, 0, :], xp[:, 0, :], small[:, 4:5], None, ALU.mult))
                V.tensor_scalar(xp[:, 1, :], xp[:, 1, :], small[:, 5:6], None, ALU.mult)\
                    .then_inc(S["xn_ready"], 1)

            def x_mod(m, latent):
                sc_, sh_ = (0, 1) if latent else (2, 3)
                dve.wait_ge(S["xT_first"], m + 1)
                for kt in range(KT):
                    ins = V.tensor_scalar(hT[:, kt, 0:P], psum[:, kt * P:(kt + 1) * P],
                                          modc[:, sc_, kt:kt + 1], modc[:, sh_, kt:kt + 1], ALU.mult, ALU.add)
                ins.then_inc(S["hT_vec"], 1)

            def pair(m, latent, more):
                h0 = 0 if latent else NQ
                lo = h0 * HD
                for tt in range(2):
                    n = 2 * m + tt
                    dve.wait_ge(S["qk_sq"], n + 1)
                    ch.step(V.tensor_copy(v[:, bass.ds(n, 1), :].rearrange("p o d -> p (o d)"),
                                          psum[:, 2048 + 640:2048 + 768]))
                    ch.link(V.tensor_reduce(small[:, 16 + h0:26],
                                            swp[:, lo:640].rearrange("p (h d) -> p h d", d=HD), AX, ALU.add))
                    ch.link(V.tensor_scalar(small[:, 16 + h0:26], small[:, 16 + h0:26], 1.0 / HD, EPS,
                                            ALU.mult, ALU.add))
                    dve.sem_inc(S["qk_var"], 1)
                    dve.wait_ge(S["qk_sd"], n + 1)
                    ch.link(V.reciprocal(small[:, 32 + h0:42], small[:, 16 + h0:26]))
                    nh = 10 - h0
                    ch.link(V.tensor_tensor(
                        qk[:, lo:640].rearrange("p (h d) -> p h d", d=HD),
                        psum[:, 2048 + lo:2048 + 640].rearrange("p (h d) -> p h d", d=HD),
                        small[:, 32 + h0:42].unsqueeze(2).broadcast_to([P, nh, HD]), ALU.mult))
                    wait(dve, "qkT_ready", n)
                    parts = [(1, NQ, 10)] + ([(0, 0, NQ)] if latent else [])
                    for i, a, b in parts:
                        k_ = b - a
                        tab = tabs[:, 2 * i + 1, bass.ds(n, 1), :].rearrange("p o d -> p (o d)")
                        for hf_ in range(2):
                            def half_of(ap, which, heads=k_):
                                ap = ap.rearrange("p (h x s f) -> p h x s f", x=2, s=2, f=16)
                                return ap[:, :, :, which, :]
                            tb = tab.rearrange("p (x s f) -> p x s f", x=2, s=2)[:, :, hf_, :]
                            ch.step(V.tensor_tensor(half_of(swp[:, a * HD:b * HD], hf_),
                                                    half_of(qk[:, a * HD:b * HD], 1 - hf_),
                                                    tb.unsqueeze(1).broadcast_to([P, k_, 2, 16]), ALU.mult))
                    ch.sync()
                    for i, a, b in parts:
                        k_ = b - a
                        q3 = qk[:, a * HD:b * HD].rearrange("p (h d) -> p h d", d=HD)
                        cs = tabs[:, 2 * i, bass.ds(n, 1), :].rearrange("p o d -> p (o d)")
                        ch.step(V.tensor_tensor(q3, q3, cs.unsqueeze(1).broadcast_to([P, k_, HD]), ALU.mult))
                    ch.sync()
                    if latent:
                        ch.step(V.tensor_tensor(rot[:, 0:D_ATTN], qk[:, 0:D_ATTN], swp[:, 0:D_ATTN], ALU.add))
                    for dup in range(2):
                        ch.step(V.tensor_tensor(
                            rot[:, 512:768].rearrange("p (k u d) -> p k u d", k=2, u=2)[:, :, dup, :],
                            qk[:, 512:640].rearrange("p (k d) -> p k d", k=2),
                            swp[:, 512:640].rearrange("p (k d) -> p k d", k=2), ALU.add))
                    ch.sync()
                    dve.sem_inc(S["rot_ready"], 1)
                    dve.wait_ge(S["qkT_ready"], n + 1)
                    V.tensor_copy(kT[:, :, bass.ds(n * P, P)],
                                  bank(5)[:, 0:2 * P].rearrange("p (k n) -> p k n", k=2)).then_inc(S["k_staged"], 1)
                    if tt == 0 and more:
                        x_norm(m + 1)
                if more:
                    x_mod(m + 1, True)

            def mod_pair(n):
                dve.wait_ge(S["wm_used"], n + 1)
                V.tensor_copy(rowm[0:2, 512 * n:512 * n + 512], bank(4 + n % 2)[0:2, :]).then_inc(S["row_out"], 1)

            x_norm(0)
            mod_pair(0)
            mod_pair(1)
            dve.wait_ge(S["tab_loaded"], 64)
            half = "p n (x h f) -> p n x h f"
            for i in range(2):
                g = gq[:, i, :]
                ch.step(V.tensor_tensor(tabs[:, 2 * i], cosr, g.unsqueeze(1).broadcast_to([P, NTOK, HD]), ALU.mult))
                g4 = g.rearrange("p (x h f) -> p x h f", x=2, h=2)
                for hf_ in range(2):
                    for x_ in range(2):
                        o = 32 * x_ + 16 * hf_
                        ch.step(V.tensor_tensor(tabs[:, 2 * i + 1, :, o:o + 16], sinr[:, :, o:o + 16],
                                                g4[:, x_, 1 - hf_, :].unsqueeze(1).broadcast_to([P, NTOK, 16]),
                                                ALU.mult))
            ch.sync()

            for n in range(2, 4):
                mod_pair(n)
            dve.wait_ge(S["modT_ready"], 1)
            dve.wait_ge(S["gains_loaded"], 16)
            cols = bank(6)[:, 0:4 * KT].rearrange("p (j i) -> p i j", i=2)
            for i in range(2):
                ch.step(V.scalar_tensor_tensor(modc[:, 2 * i, :], cols[:, i, KT:2 * KT], 1.0, gcol[:, :],
                                               ALU.add, ALU.mult))
                ch.link(V.tensor_copy(modc[:, 2 * i + 1, :], cols[:, i, 0:KT]))
            dve.sem_inc(S["modc_ready"], 1)

            x_mod(0, False)
            pair(0, False, True)
            with dve.Fori(1, NTOK // 2 - 1) as m:
                ch.enter(m - 1, PAIR_STEPS)
                pair(m, True, True)
            ch.leave(NTOK // 2 - 2)
            pair(NTOK // 2 - 1, True, False)

            dve.wait_ge(S["lruw_loaded"], 16 * 4)
            lamf = lam[:, :, :].rearrange("p d f -> p (d f)")
            V.scalar_tensor_tensor(lt[:, 0, :], lamf, -1.0, lamf, ALU.mult, ALU.max).then_inc(S["lam_abs"], 1)
            lb = lrub[:, :, :, :].rearrange("p d g f -> p (d g f)")
            ch.step(V.tensor_scalar(lb, lb, 0.5, None, ALU.mult))
            dve.wait_ge(S["lam_exp"], 1)
            ch.link(V.tensor_scalar(lt[:, 2, :], lt[:, 1, :], 2.0, None, ALU.add))
            ch.link(V.reciprocal(lt[:, 2, :], lt[:, 2, :]))
            ch.link(V.tensor_tensor(lt[:, 1, :], lt[:, 1, :], lt[:, 2, :], ALU.mult))
            ch.link(V.tensor_tensor(lt[:, 2, :], lt[:, 1, :], lt[:, 1, :], ALU.mult))
            ch.link(V.tensor_scalar(lt[:, 3, :], lt[:, 2, :], 1.0 / 17, None, ALU.mult))
            for k in range(15, 1, -2):
                ch.link(V.scalar_tensor_tensor(lt[:, 3, :], lt[:, 3, :], 1.0 / k, lt[:, 2, :], ALU.add, ALU.mult))
            ch.link(V.scalar_tensor_tensor(lt[:, 3, :], lt[:, 3, :], 1.0, lt[:, 1, :], ALU.add, ALU.mult))
            ch.link(V.tensor_scalar(lt[:, 4, :], lamf, -1.0, 0.0, ALU.mult, ALU.max))
            ch.link(V.scalar_tensor_tensor(lt[:, 4, :], lt[:, 3, :], 2.0, lt[:, 4, :], ALU.mult, ALU.add))
            ch.link(V.tensor_scalar(lruk[:, :], lt[:, 4, :], -RG_C / 2, None, ALU.mult))
            dve.sem_inc(S["lruk_ready"], 1)

            lx = slice(CTX + GAP, LW)
            dve.wait_ge(S["lz_out"], LF + 2 * LF * (NTOK // 2 - 1))

            def conv(f):
                ch.link(V.tensor_scalar(cu, XL[:, f, 0:LW], convw[:, f, 0:1], convb[:, f:f + 1],
                                        ALU.mult, ALU.add))
                for j in range(1, CONV_W):
                    ch.link(V.scalar_tensor_tensor(cu, XL[:, f, j:j + LW], convw[:, f, j:j + 1], cu,
                                                   ALU.mult, ALU.add))
                dve.sem_inc(S["conv_done"], 1)

            conv(0)
            dve.wait_ge(S["qkv_ready"], NTOK)
            dve.wait_ge(S["z_ready"], LF * NX // 2)
            V.tensor_copy(silb, csil[:, 0, :].unsqueeze(2).broadcast_to([P, KT, P])).then_inc(S["silb_ready"], 1)
            dve.wait_ge(S["q_stored"], 16 * NX)
            for f in range(LF):
                for d in range(2):
                    a_, b_, r_, i_ = av[:, d], bv[:, d], tr[:, d], ti[:, d]
                    dve.wait_ge(S["lru_a"], 2 * f + d + 1)
                    ch.link(V.tensor_tensor(b_, a_, a_, ALU.mult))
                    ch.link(V.scalar_tensor_tensor(b_, b_, 1.0, r_, ALU.add, ALU.mult))
                    V.tensor_scalar(b_, b_, -1.0, 0.0, ALU.mult, ALU.max).then_inc(S["lru_m"], 1)
                    ch.link(V.scalar_tensor_tensor(i_, i_, 1.0, cu, ALU.add, ALU.mult))
                if f + 1 < LF:
                    conv(f + 1)
                for d in range(2):
                    a_, b_, i_ = av[:, d], bv[:, d], ti[:, d]
                    dve.wait_ge(S["lru_s"], 2 * f + d + 1)
                    ch.link(V.tensor_tensor(b_, b_, i_, ALU.mult))
                    if d == 0:
                        ch.step(V.memset(a_[:, CTX:CTX + GAP], 1.0))
                        ch.link(V.memset(b_[:, CTX:CTX + GAP], 0.0))
                        wait(dve, "lru_stored", 16 * f)
                        ch.link(V.tensor_tensor_scan(hf, a_, b_, 0.0, ALU.mult, ALU.add))
                        dve.sem_inc(S["lru_used"], 1)
                    else:
                        ch.link(V.tensor_tensor_scan(hb[:, 0:CTX][:, ::-1], a_[:, 0:CTX][:, ::-1],
                                                     b_[:, 0:CTX][:, ::-1], 0.0, ALU.mult, ALU.add))
                        ch.link(V.tensor_tensor_scan(hb[:, lx][:, ::-1], a_[:, lx][:, ::-1], b_[:, lx][:, ::-1],
                                                     hb[:, 0:1], ALU.mult, ALU.add))
                zf, zt = Z[:, f, :], tr[:, 1, 0:SEQ]
                ch.link(V.tensor_tensor(zt, zf, zf, ALU.mult))
                ch.link(V.tensor_scalar(zt, zt, GELU_C, 1.0, ALU.mult, ALU.add))
                V.tensor_tensor(zt, zt, zf, ALU.mult).then_inc(S["z_in"], 1)
                ch.link(V.tensor_tensor(hf[:, lx], hf[:, lx], hb[:, lx], ALU.add))
                ch.link(V.scalar_tensor_tensor(hf[:, lx], hf[:, lx], 0.5, zf, ALU.mult, ALU.mult))
                if f == 0:
                    dve.wait_ge(S["gains_loaded"], 64)
                mod_row(4 + 2 * f)
                dve.wait_ge(S["z_tanh"], f + 1)
                ch.link(V.scalar_tensor_tensor(hf[:, lx], zt, 1.0, hf[:, lx], ALU.add, ALU.mult))
                dve.sem_inc(S["lru_out"], 1)
                dve.sem_inc(S["lru_used"], 1)
                mod_row(5 + 2 * f)
            dve.wait_ge(S["mod_out"], 8)

            def negmax(n, h):
                a = 44 + h % 2
                dve.wait_ge(S["scores_ready"], n * NQ + h + 1)
                ch.link(V.tensor_reduce(small[:, a:a + 1], psum[:, 0:KEYS], AX, ALU.max))
                V.tensor_scalar(small[:, a:a + 1], small[:, a:a + 1], -HD ** -0.5, None, ALU.mult)\
                    .then_inc(S["negmax_ready"], 1)

            def att_step(n, h):
                b = 46 + h % 2
                dve.wait_ge(S["probs_ready"], n * NQ + h + 1)
                ch.link(V.reciprocal(small[:, b:b + 1], small[:, b:b + 1]))
                V.tensor_scalar(pr, pr, small[:, b:b + 1], None, ALU.mult).then_inc(S["probs_normed"], 1)
                if h + 1 < NQ:
                    negmax(n, h + 1)

            def root(count, at_, sq, var, sd):
                dve.wait_ge(S[sq], count)
                V.tensor_scalar(small[:, at_ + 1:at_ + 2], small[:, at_:at_ + 1], 1.0 / D, EPS,
                                ALU.mult, ALU.add).then_inc(S[var], 1)
                dve.wait_ge(S[sd], count)
                ch.link(V.reciprocal(small[:, at_ + 2:at_ + 3], small[:, at_ + 1:at_ + 2]))

            def top16(lists):
                passed = S["top_passed"]

                def each(op, alone=True):
                    for vals, idx, src, scratch in lists:
                        ch.step(op(vals, idx, src, scratch))
                    if alone:
                        ch.sync()
                        dve.sem_inc(passed, 1)

                each(lambda vals, idx, src, scratch: V.max(vals[:, 0:8], src))
                each(lambda vals, idx, src, scratch: V.max_index(idx[:, 0:8], vals[:, 0:8], src), alone=False)
                each(lambda vals, idx, src, scratch: V.match_replace(scratch, vals[:, 0:8], src, NEG))
                each(lambda vals, idx, src, scratch: V.max(vals[:, 8:16], scratch))
                each(lambda vals, idx, src, scratch: V.max_index(idx[:, 8:16], vals[:, 8:16], scratch))

            def retrieve(n, u, fill, meanwhile):
                for j in range(4):
                    fill(TOP_AT[u] + TOP_EVERY * j)
                    dve.sem_inc(S["top_passed"], 1)
                    h = 4 * u + j
                    if j == 3:
                        meanwhile()
                    top16([(tv[:, p_, :], ixu[:, h, p_, :], sc[:, 2 * j + p_, :], cnd2[:, p_ * NK:(p_ + 1) * NK])
                           for p_ in range(2)])
                    fill(TOP_AT[u] + TOP_EVERY * j + 4)
                    ch.link(V.tensor_tensor(cand.rearrange("p (a b) -> p a b", a=TOPK),
                                            tv[:, 0, :].unsqueeze(2).broadcast_to([P, TOPK, TOPK]),
                                            tv[:, 1, :].unsqueeze(1).broadcast_to([P, TOPK, TOPK]), ALU.add))
                    dve.sem_inc(S["top_passed"], 1)
                    top16([(top[:, TOPK * h:TOPK * h + TOPK], posu[:, h, :], cand, cnd2)])
                dve.sem_inc(S["sc_used"], 1)
                fill(TOP_AT[u] + TOP_EVERY * 4)
                hs = slice(4 * u, 4 * u + 4)
                ch.step(V.tensor_scalar(pabu[:, 0], posu[:, hs, :], 4, None, ALU.logical_shift_right))
                ch.link(V.tensor_scalar(pabu[:, 1], posu[:, hs, :], 15, None, ALU.bitwise_and))
                for p_ in range(2):
                    fill(TOP_AT[u] + TOP_EVERY * 4 + 3 * p_)
                    ch.link(V.tensor_tensor(
                        oneh.rearrange("p h k a -> p (h k) a"),
                        pabu[:, p_].rearrange("p h k -> p (h k)").unsqueeze(2).broadcast_to([P, 4 * TOPK, TOPK]),
                        iota16[:, :].unsqueeze(1).broadcast_to([P, 4 * TOPK, TOPK]), ALU.is_equal))
                    ch.link(V.tensor_tensor(oneh, oneh, ixu[:, hs, p_, :].unsqueeze(2)
                                            .broadcast_to([P, 4, TOPK, TOPK]), ALU.mult))
                    ch.link(V.tensor_reduce(selv[:, p_], oneh, AX, ALU.add))
                fill(TOP_AT[u] + TOP_EVERY * 4 + 6)
                wait(dve, "idx_taken", 2 * n - 1 + u)
                ch.link(V.scalar_tensor_tensor(idxf[:, 64 * u:64 * u + 64],
                                               selv[:, 0].rearrange("p h k -> p (h k)"), float(NK),
                                               selv[:, 1].rearrange("p h k -> p (h k)"), ALU.mult, ALU.add))
                ch.link(V.tensor_copy(idx_new[:, 64 * u:64 * u + 64], idxf[:, 64 * u:64 * u + 64]))
                dve.sem_inc(S["idx_ready"], 1)

            def post(n, fill):
                first = isinstance(n, int)
                fill(MIX_AT)
                root(n + 1, 48, "mix_sq", "mix_var", "mix_sd")
                dve.wait_ge(S["g1_ready"], n + 1)
                ch.link(V.scalar_tensor_tensor(mix, mix, small[:, 50:51], bank(2, 2), ALU.mult, ALU.mult))
                dve.wait_ge(S["xc_loaded"], 16 * n + 16)
                ch.link(V.tensor_tensor(xm_new, xm_new, mix, ALU.add))
                dve.sem_inc(S["xm_ready"], 1)
                fill(XM_AT)
                root(n + 1, 48, "xm_sq", "xm_var", "xm_sd")
                dve.wait_ge(S["a2_ready"], n + 1)
                ch.link(V.scalar_tensor_tensor(hx_new, xm_new, small[:, 50:51], bank(4, 2), ALU.mult, ALU.mult))
                dve.wait_ge(S["b2_ready"], n + 1)
                ch.link(V.tensor_tensor(hx_new, hx_new, bank(0, 2), ALU.add))
                dve.sem_inc(S["hx_ready"], 1)
                fill(HXT_AT)
                dve.wait_ge(S["hxT_ready"], n + 1)
                wait(dve, "ff_free", n)
                V.tensor_copy(hxT[:, 0:4, :], bank(3)).then_inc(S["hxT_even"], 1)

                def open_half(u):
                    fill(QT_AT[u])
                    dve.wait_ge(S["qT_ready"], 2 * n + u + 1)
                    V.tensor_copy(q_T[:, 0:4, :], bank(3)).then_inc(S["qT_even"], 1)

                open_half(0)
                for u in range(2):
                    fill(SIM_AT[u])
                    dve.wait_ge(S["s_ready"], 2 * n + u + 1)
                    ch.link(V.tensor_copy(sc[:, 0:4, :], bank(2)))
                    dve.sem_inc(S["s_even"], 1)
                    if u == 0 and not first:
                        open_half(1)
                    dve.wait_ge(S["s_odd"], 2 * n + u + 1)
                    dve.sem_inc(S["top_passed"], 1)
                    retrieve(n, u, fill, lambda: open_half(1) if u == 0 and first else None)
                t3 = top.rearrange("p (h k) -> p h k", k=TOPK)
                g3 = gate.rearrange("p (h k) -> p h k", k=TOPK)
                V.tensor_tensor(g3, t3, t3[:, :, 0:1].broadcast_to([P, PH, TOPK]), ALU.subtract)\
                    .then_inc(S["gate_in"], 1)

            def gates(n):
                g3 = gate.rearrange("p (h k) -> p h k", k=TOPK)
                dve.wait_ge(S["gate_exp"], n + 1)
                ch.link(V.tensor_reduce(small[:, 56:64], g3, AX, ALU.add))
                ch.link(V.reciprocal(small[:, 56:64], small[:, 56:64]))
                ch.link(V.tensor_tensor(g3, g3, small[:, 56:64].unsqueeze(2).broadcast_to([P, PH, TOPK]), ALU.mult))

            def move():
                ch.step(V.tensor_copy(xm_cur, xm_new))
                ch.link(V.tensor_copy(hx_cur, hx_new))
                dve.sem_inc(S["xm_moved"], 1)

            def u_slots(c, lo, hi, tokens):
                for j in range(lo, hi):
                    r = j % RING
                    dve.wait_ge(got[r], c * (16 * 2 * SLOTS // RING) + 16 * (j // RING + 1))
                    V.tensor_tensor_reduce(ring[:, r, :], ring[:, r, :], tokens, 1.0, 0.0, ALU.mult, ALU.add,
                                           act_[:, j:j + 1]).then_inc(S["u_used"], 1)

            def weights(c):
                dve.wait_ge(S["u_used"], c * SLOTS + SLOTS)
                ch.link(V.tensor_tensor(gx, act_, act_, ALU.mult))
                ch.link(V.tensor_scalar(gx, gx, GELU_C, 1.0, ALU.mult, ALU.add))
                V.tensor_tensor(gx, gx, act_, ALU.mult).then_inc(S["gelu_in"], 1)
                dve.wait_ge(S["v_used"], c * len(V_PE) + len(V_PE))
                ch.link(V.scalar_tensor_tensor(wt, act_, 0.5, gate, ALU.mult, ALU.mult))
                dve.wait_ge(S["gelu_tanh"], c + 1)
                ch.link(V.scalar_tensor_tensor(wt, gx, 1.0, wt, ALU.add, ALU.mult))
                dve.sem_inc(S["w_ready"], 1)

            def v_slots(c, lo, hi):
                for j in range(lo, hi):
                    if j not in V_VEC:
                        continue
                    r, k = j % RING, RANK[j]
                    if k:
                        dve.wait_ge(S["vv_used"], c * len(V_VEC) + len(V_VEC) + k)
                    dve.wait_ge(got[r], c * (16 * 2 * SLOTS // RING) + 16 * (SLOTS // RING + j // RING + 1))
                    if k == 0:
                        ins = V.tensor_scalar(vacc, ring[:, r, :], wt[:, j:j + 1], None, ALU.mult)
                    else:
                        ins = V.scalar_tensor_tensor(vacc, ring[:, r, :], wt[:, j:j + 1], vacc, ALU.mult, ALU.add)
                    ins.then_inc(S["vv_used"], 1)

            def finish(c, between):
                dve.wait_ge(S["vv_used"], (c + 2) * len(V_VEC))
                dve.wait_ge(S["v_used"], (c + 2) * len(V_PE))
                ch.link(V.tensor_tensor(vacc, bank(6, 2), vacc, ALU.add))
                dve.sem_inc(S["ffn_read"], 1)
                dve.sem_inc(S["ffn_ready"], 1)
                between()
                root(c + 1, 52, "ffn_sq", "ffn_var", "ffn_sd")
                dve.wait_ge(S["g2_ready"], c + 1)
                ch.link(V.scalar_tensor_tensor(ff, vacc, small[:, 54:55], bank(3, 2), ALU.mult, ALU.mult))
                ch.link(V.tensor_tensor(ff, ff, xm_cur, ALU.add))
                dve.sem_inc(S["out_ready"], 1)

            negmax(0, 0)
            for h in range(NQ):
                att_step(0, h)
            begun = [0]

            def begin(upto):
                hi = min(upto - TOP_AT[1], HEAD_START[1])
                if hi > begun[0]:
                    u_slots(0, begun[0], hi, hx_new)
                    begun[0] = hi

            post(0, begin)
            gates(0)
            move()
            with dve.Fori(0, NX - 1) as c:
                ch.enter(c, CHUNK_STEPS)
                done = [HEAD_START[1]]

                def fill(upto):
                    lo, hi = done[0], min(upto, 2 * SLOTS)
                    if hi <= lo:
                        return
                    u_slots(c, lo, min(hi, SLOTS), hx_cur)
                    if lo < SLOTS <= hi:
                        weights(c)
                    v_slots(c, max(lo - SLOTS, 0), hi - SLOTS)
                    done[0] = hi

                negmax(c + 1, 0)
                for h in range(NQ):
                    fill(HEADS_AT + PER_HEAD * h)
                    att_step(c + 1, h)
                post(c + 1, fill)
                fill(2 * SLOTS)
                u_slots(c + 1, 0, HEAD_START[0], hx_new)
                gates(c + 1)
                finish(c, lambda: u_slots(c + 1, *HEAD_START, hx_new))
                move()
            ch.leave(NX - 1)
            u_slots(NX - 1, HEAD_START[1], SLOTS, hx_cur)
            weights(NX - 1)
            v_slots(NX - 1, 0, SLOTS)
            finish(NX - 1, lambda: None)

        @block.tensor
        def _(pe):
            M = nc.tensor.matmul
            T = nc.tensor.transpose
            pe.wait_ge(S["consts_made"], 2)

            def mod_pair(n):
                wait(pe, "row_out", n - 1)
                pe.wait_ge(S["wm_loaded%d" % (n % 2)], 16 * (n // 2 + 1))
                out = bank(4 + n % 2)[0:2, :]
                M(out, lhsT=ones[0:1, 0:2], rhs=bmod[0:1, 512 * n:512 * n + 512], start=True, stop=False)
                for kt in range(KT):
                    ins = M(out, lhsT=sil2[:, kt, :], rhs=wm[:, n % 2, kt, :], start=False, stop=(kt == KT - 1))
                ins.then_inc(S["wm_used"], 1)

            def mod_block(n):
                wait(pe, "mod_out", n - 5)
                pe.wait_ge(S["wml_loaded%d" % (n % 3)], 32 * (n // 3 if n % 3 else n // 3 - 1))
                out = bank(6 + n % 2)
                M(out, lhsT=ones[0:1, :], rhs=bmodl[0:1, n % 3, :], start=True, stop=False)
                for kt in range(KT):
                    ins = M(out, lhsT=silb[:, kt, :], rhs=wml[:, n % 3, kt, :], start=False, stop=(kt == KT - 1))
                ins.then_inc(S["wm_used"], 1)

            def x_transpose(m):
                pe.wait_ge(S["xn_ready"], m + 1)
                for tt in range(2):
                    for kt in range(KT):
                        ins = T(psum[:, tt * D + kt * P:tt * D + (kt + 1) * P], xp[:, tt, kt * P:(kt + 1) * P],
                                ident[:, :])
                    ins.then_inc(S["xT_ready" if tt else "xT_first"], 1)

            def pair(m, latent, more):
                pe.wait_ge(S["hT_vec"], m + 1)
                out_before = LF + 2 * LF * (m - 1)
                for tt in range(2):
                    n = 2 * m + tt
                    toks = slice(tt * P, tt * P + P)
                    wait(pe, "k_staged", n)
                    if latent:
                        if tt:
                            pe.wait_ge(S["q_staged"], n - 2)
                        for kt in range(KT):
                            M(bank(4), lhsT=hT[:, kt, toks], rhs=w_in[:, kt, 0:512],
                              start=(kt == 0), stop=(kt == KT - 1))
                    for kt in range(KT):
                        ins = M(bank(5)[:, 0:256], lhsT=hT[:, kt, toks], rhs=w_in[:, kt, 512:768],
                                start=(kt == 0), stop=(kt == KT - 1))
                    ins.then_inc(S["qkv_ready"], 1)
                    if tt == 0:
                        pe.wait_ge(S["hT_act"], m + 1)
                    if tt == 0 or latent:
                        for f in range(LF):
                            l = LF * tt + f
                            if latent:
                                pe.wait_ge(S["lz_out"], out_before + l - 1)
                            else:
                                wait(pe, "lz_out", l - 1)
                            o = QKV + D_LRU * tt + f * P
                            for kt in range(KT):
                                ins = M(bank(6 + f % 2)[:, 0:256], lhsT=w_in[:, kt, o:o + P], rhs=hT[:, kt, :],
                                        start=(kt == 0), stop=(kt == KT - 1))
                            ins.then_inc(S["z_ready" if tt else "lru_ready"], 1)
                    pe.wait_ge(S["rot_ready"], n + 1)
                    if latent:
                        for j in range(4):
                            T(bank(4)[:, j * P:(j + 1) * P], rot[:, j * P:(j + 1) * P], ident[:, :])
                    for j in range(2):
                        ins = T(bank(5)[:, j * P:(j + 1) * P], rot[:, 512 + j * P:512 + (j + 1) * P], ident[:, :])
                    ins.then_inc(S["qkT_ready"], 1)
                if more:
                    x_transpose(m + 1)
                    if latent:
                        pe.wait_ge(S["q_staged"], 2 * m)

            pe.wait_ge(S["silu_ready"], 1)
            pe.wait_ge(S["bmod_loaded"], 16)
            mod_pair(0)
            mod_pair(1)
            x_transpose(0)
            mod_pair(2)
            mod_pair(3)
            pe.wait_ge(S["row_out"], 4)
            for j in range(2 * KT):
                ins = T(bank(6)[:, 2 * j:2 * j + 2], rowm[0:2, j * P:(j + 1) * P], ident[0:2, 0:2])
            ins.then_inc(S["modT_ready"], 1)
            pe.wait_ge(S["w_in_loaded"], 16)
            pair(0, False, True)
            pe.wait_ge(S["w_in_rest"], 32)
            with pe.Fori(1, NTOK // 2 - 1) as m:
                pair(m, True, True)
            pair(NTOK // 2 - 1, True, False)

            pe.wait_ge(S["bd_loaded"], 16 * 8)
            pe.wait_ge(S["lz_out"], LF + 2 * LF * (NTOK // 2 - 1))
            for f in range(LF):
                pe.wait_ge(S["conv_done"], f + 1)
                for d in range(2):
                    wait(pe, "gates_out", 4 * f + 2 * d)
                    for g in range(2):
                        for o in range(0, LW, 512):
                            w = min(512, LW - o)
                            ins = M(psum[:, 1536 * g + o:1536 * g + o + w], lhsT=bd[:, (2 * d + g) * LF + f, :],
                                    rhs=cu[:, o:o + w], start=True, stop=True)
                    ins.then_inc(S["gates_ready"], 1)
                pe.wait_ge(S["silb_ready"], 1)
                mod_block(4 + 2 * f)
                mod_block(5 + 2 * f)

            def scores(n, h):
                if h == 0:
                    pe.wait_ge(S["q_loaded"], 16 * n + 16)
                    wait(pe, "s_even", 2 * n)
                    wait(pe, "s_odd", 2 * n)
                wait(pe, "probs_ready", n * NQ + h)
                o = 64 * (h % 2)
                for b in range(0, KEYS, 512):
                    w = min(512, KEYS - b)
                    ins = M(psum[:, b:b + w], lhsT=qc[o:o + 64, h // 2, :], rhs=kT[o:o + 64, h // 4, b:b + w],
                            start=True, stop=True)
                ins.then_inc(S["scores_ready"], 1)

            def att_step(n, h):
                if h + 1 < NQ:
                    scores(n, h + 1)
                pe.wait_ge(S["probs_normed"], n * NQ + h + 1)
                for g in range(3):
                    l = 3 * h + g
                    wait(pe, "pt_out", n * ATT_T + l - 1)
                    for j in range(4 if g < 2 else 2):
                        kt = 4 * g + j
                        ins = T(bank(3 + l % 2)[:, j * P:(j + 1) * P], pr[:, kt * P:(kt + 1) * P], ident[:, :])
                    ins.then_inc(S["pt_ready"], 1)
                wait(pe, "att_ready", n * NQ + h - 1)
                for g in range(3):
                    l = 3 * h + g
                    pe.wait_ge(S["pt_out"], n * ATT_T + l + 1)
                    for kt in range(4 * g, 4 * g + (4 if g < 2 else 2)):
                        ins = M(bank(5)[0:64, 128 * (h % 2):128 * (h % 2) + 128],
                                lhsT=v[:, kt, 64 * (h // 4):64 * (h // 4) + 64], rhs=pT[:, kt, :],
                                start=(kt == 0), stop=(kt == NTOK - 1))
                ins.then_inc(S["pv_ready"], 1)

            def spread(b, r, ready):
                for i in range(2):
                    ins = M(bank(b + i), lhsT=ident[r:r + 1, r:r + 1].broadcast_to([1, P]),
                            rhs=rows[r:r + 1, 512 * i:512 * i + 512], start=True, stop=True)
                ins.then_inc(S[ready], 1)

            def post(n, step, i):
                if step == "out":
                    if i == 0:
                        pe.wait_ge(S["att_ready"], n * NQ + NQ)
                        pe.wait_ge(S["l_loaded"], 16 * n + 16)
                    pe.wait_ge(S["wo_loaded"], 16)
                    for kt in range(KT):
                        ins = M(bank(i), lhsT=att[:, kt, :] if kt < 4 else lc[:, kt - 4, :],
                                rhs=wo[:, kt, 512 * i:512 * i + 512], start=(kt == 0), stop=(kt == KT - 1))
                    ins.then_inc(S["out_half"], 1)
                elif step == "rows":
                    if i == 0:
                        spread(2, G1, "g1_ready")
                        spread(4, A2, "a2_ready")
                    else:
                        pe.wait_ge(S["xm_ready"], n + 1)
                        spread(0, B2, "b2_ready")
                elif step == "hxT":
                    pe.wait_ge(S["hx_ready"], n + 1)
                    for kt in range(KT):
                        ins = T(psum[:, 1536 + kt * P:1536 + (kt + 1) * P], hx_new[:, kt * P:(kt + 1) * P], ident[:, :])
                    ins.then_inc(S["hxT_ready"], 1)
                elif step == "q":
                    pe.wait_ge(S["hxT_even"], n + 1)
                    pe.wait_ge(S["hxT_odd"], n + 1)
                    pe.wait_ge(S["wq_loaded"], 16)
                    pe.wait_ge(S["sub_loaded"], 16)
                    for kt in range(KT):
                        ins = M(bank(i % 2), lhsT=hxT[:, kt, :], rhs=wq[:, kt, 512 * i:512 * i + 512],
                                start=(kt == 0), stop=(kt == KT - 1))
                    ins.then_inc(S["q_ready"], 1)
                elif step == "qT":
                    pe.wait_ge(S["q_out"], 4 * n + 2 * i + 2)
                    for j in range(8):
                        ins = T(psum[:, 1536 + j * P:1536 + (j + 1) * P], q_tok[:, j * P:(j + 1) * P], ident[:, :])
                    ins.then_inc(S["qT_ready"], 1)
                elif step == "s":
                    pe.wait_ge(S["qT_even"], 2 * n + i + 1)
                    pe.wait_ge(S["qT_odd"], 2 * n + i + 1)
                    if i:
                        pe.wait_ge(S["s_even"], 2 * n + i)
                        pe.wait_ge(S["s_odd"], 2 * n + i)
                    for j in range(8):
                        ins = M(bank(2 if j < 4 else 5)[:, (j % 4) * P:(j % 4 + 1) * P], lhsT=q_T[:, j, :],
                                rhs=skT[:, 8 * i + j, :], start=True, stop=True)
                    ins.then_inc(S["s_ready"], 1)

            def v_slots(c, lo, hi):
                if lo == 0:
                    pe.wait_ge(S["ffn_read"], c + 1)
                for j in range(lo, hi):
                    if j not in V_PE:
                        continue
                    r, k = j % RING, RANK[j]
                    pe.wait_ge(S["diag_ready"], c * len(V_PE) + k + 1)
                    pe.wait_ge(got[r], c * (16 * 2 * SLOTS // RING) + 16 * (SLOTS // RING + j // RING + 1))
                    for b in range(2):
                        ins = M(bank(6 + b), lhsT=diag[:, k % DIAGS, :], rhs=ring[:, r, 512 * b:512 * b + 512],
                                start=(k == 0), stop=(k == len(V_PE) - 1))
                    ins.then_inc(S["v_used"], 1)

            scores(0, 0)
            for h in range(NQ):
                att_step(0, h)
            for step in AFTER:
                post(0, *step)
            with pe.Fori(0, NX - 1) as c:
                scores(c + 1, 0)
                for h in range(NQ):
                    att_step(c + 1, h)
                for step in AFTER:
                    post(c + 1, *step)
                v_slots(c, 0, SLOTS - RING)
                spread(3, G2, "g2_ready")
                v_slots(c, SLOTS - RING, SLOTS)
            v_slots(NX - 1, 0, SLOTS - RING)
            spread(3, G2, "g2_ready")
            v_slots(NX - 1, SLOTS - RING, SLOTS)


def _rope_tables():
    f = np.float32
    nf = HD // 4
    inv = f(10000.0) ** (-np.arange(nf, dtype=f) / f(nf))
    pos = np.arange(SEQ)
    ang = np.stack([(pos // GRID_W).astype(f)[:, None] * inv, (pos % GRID_W).astype(f)[:, None] * inv], 1)
    cos, sin = np.cos(ang), np.sin(ang)
    cos = np.stack([cos, cos], 2).reshape(SEQ, HD)
    sin = np.stack([-sin, sin], 2).reshape(SEQ, HD)
    cos = np.concatenate([np.ones((CTX, HD), f), cos])
    sin = np.concatenate([np.zeros((CTX, HD), f), sin])
    return [np.ascontiguousarray(a.reshape(NTOK, P, HD).transpose(1, 0, 2).astype(f)) for a in (cos, sin)]


def kernel(**inputs):
    import concourse.bacc as bacc
    from concourse.bass_utils import run_bass_kernel_spmd as run

    one = {n: np.ascontiguousarray(np.asarray(a)) for n, a in inputs.items()}
    cos, sin = _rope_tables()

    def cols(a):
        return np.moveaxis(a.reshape(a.shape[:-1] + (-1, P)), -1, 0)

    arrays = {
        "xin": np.concatenate([one["ctx"][0], one["x"][0]]).reshape(NTOK, P, D),
        "c": one["c"].reshape(D), "c_ctx": one["c_ctx"], "w_mod": one["w_mod"][0], "b_mod": one["b_mod"],

        "g_pre_mix": cols(one["g_pre_mix"][0]), "g_post_mix": one["g_post_mix"], "g_pre_ffn": one["g_pre_ffn"],
        "g_post_ffn": one["g_post_ffn"], "w_in": one["w_in"][0], "q_norm_g": one["q_norm_g"],
        "k_norm_g": one["k_norm_g"],
        "conv_w": cols(one["conv_w"][0]).transpose(0, 2, 1), "conv_b": cols(one["conv_b"][0]),
        "lru_bias": np.stack([cols(one["rg_ba"][0]), cols(one["rg_bi"][0])], 2),
        "rg_lambda": cols(one["rg_lambda"][0]), "rg_wa": one["rg_wa"][0], "rg_wi": one["rg_wi"][0],
        "w_out": one["w_out"][0], "wq": one["peer_wq"][0],
        "subkeys": one["peer_subkeys"].reshape(2 * PH, NK, DK).transpose(2, 0, 1),
        "u": one["peer_u"][0], "v": one["peer_v"][0],
        "cos": cos, "sin": sin,
    }
    arrays = {n: np.ascontiguousarray(a) for n, a in arrays.items()}
    nc = bacc.Bacc("TRN2", target_bir_lowering=False, num_devices=1)
    t = {n: nc.dram_tensor("in_" + n, a.shape, F32, kind="ExternalInput").ap() for n, a in arrays.items()}
    t["out"] = nc.dram_tensor("out", (NX, P, D), F32, kind="ExternalOutput").ap()
    nc.disable_value_cache = True
    layer(nc, t)
    r = run(nc, [{"in_" + n: a for n, a in arrays.items()}], core_ids=[0])
    return r.results[0]["out"].reshape(1, SEQ, D)
```
